# Optimizing a Trainium2 kernel written in Bass

```python
import jax, jax.numpy as jnp
from jax import lax
import numpy as np
import math

D_MODEL = 1024
BATCH = 1
SEQ = 512
DEPTH = 1

CTX_LEN = 256
GRID_W = 64
CHUNK = 64
N_DIR = 2
GLA_HEADS = 4
GLA_DK = 64
GLA_DV = 128
GLA_RANK = 16
GLA_TAU = 16.0
GLA_QK = GLA_HEADS * GLA_DK
GLA_V = GLA_HEADS * GLA_DV
GDN_HEADS = 4
GDN_DK = 128
GDN_DV = 128
GDN_QK = GDN_HEADS * GDN_DK
GDN_V = GDN_HEADS * GDN_DV
CONV_K = 3
CONV_CH = 2 * GDN_QK + GDN_V
EPS = 1e-6
SPLIT_SIZES = (GLA_QK, GLA_QK, GLA_V, GLA_V, N_DIR * GLA_RANK,
               GDN_QK, GDN_QK, GDN_V, GDN_V, N_DIR * GDN_HEADS, N_DIR * GDN_HEADS,
               2 * D_MODEL)
D_IN = sum(SPLIT_SIZES)


def rmsnorm(x, g):
    xf = x.astype(jnp.float32)
    y = xf * lax.rsqrt(jnp.mean(xf * xf, axis=-1, keepdims=True) + EPS)
    return (y * g.astype(jnp.float32)).astype(x.dtype)

def l2norm(x):
    return x * lax.rsqrt(jnp.sum(x * x, axis=-1, keepdims=True) + EPS)

def rev(a):
    return jnp.flip(a, axis=1)

def split_cols(z):
    outs = []
    start = 0
    for size in SPLIT_SIZES:
        outs.append(z[..., start:start + size])
        start += size
    return outs

def conv_grid(u, w):
    b, t, ch = u.shape
    rows = t // GRID_W
    ug = u.reshape(b, rows, GRID_W, ch)
    out = lax.conv_general_dilated(ug, w[:, :, None, :].astype(u.dtype), window_strides=(1, 1), padding='SAME',
                                   dimension_numbers=('NHWC', 'HWIO', 'NHWC'), feature_group_count=ch)
    return out.reshape(b, t, ch)

def conv_seq(u, w):
    ch = u.shape[-1]
    return lax.conv_general_dilated(u, w[1][:, None, :].astype(u.dtype), window_strides=(1,), padding='SAME',
                                    dimension_numbers=('NWC', 'WIO', 'NWC'), feature_group_count=ch)

def to_chunks(a):
    b, t, h, d = a.shape
    return a.reshape(b, t // CHUNK, CHUNK, h, d).transpose(1, 0, 3, 2, 4)

def from_chunks(a):
    n, b, h, c, d = a.shape
    return a.transpose(1, 0, 3, 2, 4).reshape(b, n * c, h, d)

def gla_chunked(q, k, v, g, s0):
    qc, kc, vc, gc = to_chunks(q), to_chunks(k), to_chunks(v), to_chunks(g)
    bc = jnp.cumsum(gc, axis=3)
    causal = jnp.tril(jnp.ones((CHUNK, CHUNK), dtype=bool))

    def step(s, inp):
        qi, ki, vi, bi = inp
        diff = bi[:, :, :, None, :] - bi[:, :, None, :, :]
        dec = jnp.exp(jnp.where(causal[:, :, None], diff, -jnp.inf))
        att = jnp.einsum('bhtd,bhsd,bhtsd->bhts', qi, ki, dec)
        o = jnp.einsum('bhtd,bhde->bhte', qi * jnp.exp(bi), s) + jnp.einsum('bhts,bhse->bhte', att, vi)
        bl = bi[:, :, -1:, :]
        s_new = s * jnp.exp(bl[:, :, 0, :])[..., None] + jnp.einsum('bhsd,bhse->bhde', ki * jnp.exp(bl - bi), vi)
        return s_new, o

    s_fin, o = lax.scan(step, s0, (qc, kc, vc, bc))
    return from_chunks(o), s_fin

def gdn_chunked(q, k, v, g, beta, s0):
    qc, kc, vc = to_chunks(q), to_chunks(k), to_chunks(v)
    gc = to_chunks(g[..., None])[..., 0]
    bc = to_chunks(beta[..., None])
    gam = jnp.cumsum(gc, axis=-1)
    incl = jnp.tril(jnp.ones((CHUNK, CHUNK), dtype=bool))
    strict = jnp.tril(jnp.ones((CHUNK, CHUNK), dtype=bool), -1)
    dmask = jnp.exp(jnp.where(incl, gam[..., :, None] - gam[..., None, :], -jnp.inf))
    kb = kc * bc
    vb = vc * bc
    low = jnp.where(strict, jnp.einsum('nbhid,nbhjd->nbhij', kb, kc) * dmask, 0.0)
    eye = jnp.eye(CHUNK, dtype=low.dtype)
    tmat = lax.linalg.triangular_solve(eye + low, jnp.broadcast_to(eye, low.shape), left_side=True, lower=True)
    u = jnp.matmul(tmat, vb)
    w = jnp.matmul(tmat, kb * jnp.exp(gam)[..., None])
    aqk = jnp.einsum('nbhid,nbhjd->nbhij', qc, kc) * dmask

    def step(s, inp):
        qi, ki, ui, wi, ai, gi = inp
        v_new = ui - jnp.matmul(wi, s)
        o = jnp.matmul(qi * jnp.exp(gi)[..., None], s) + jnp.matmul(ai, v_new)
        gl = gi[..., -1]
        s_new = s * jnp.exp(gl)[..., None, None] + jnp.einsum('bhcd,bhce->bhde', ki * jnp.exp(gl[..., None] - gi)[..., None], v_new)
        return s_new, o

    s_fin, o = lax.scan(step, s0, (qc, kc, u, w, aqk, gam))
    return from_chunks(o), s_fin

def branch_inputs(h, w_in, gla_up, gla_ub, gdn_conv, gdn_a_log, gdn_dt_bias, on_grid):
    f32 = jnp.float32
    b, t, _ = h.shape
    z = jnp.matmul(h, w_in).astype(f32)
    aq, ak, av, ag, alr, bq, bk, bv, bg, bbeta, bdec, mg = split_cols(z)
    aq = aq.reshape(b, t, GLA_HEADS, GLA_DK) * (GLA_DK ** -0.5)
    ak = ak.reshape(b, t, GLA_HEADS, GLA_DK)
    av = av.reshape(b, t, GLA_HEADS, GLA_DV)
    alr = alr.reshape(b, t, N_DIR, GLA_RANK)
    alog = jax.nn.log_sigmoid(jnp.einsum('btnr,nrk->btnk', alr, gla_up.astype(f32)) + gla_ub.astype(f32)) / GLA_TAU
    alog = alog.reshape(b, t, N_DIR, GLA_HEADS, GLA_DK)
    qkv = jnp.concatenate([bq, bk, bv], axis=-1)
    qkv = jax.nn.silu(conv_grid(qkv, gdn_conv) if on_grid else conv_seq(qkv, gdn_conv))
    bq = l2norm(qkv[..., :GDN_QK].reshape(b, t, GDN_HEADS, GDN_DK)) * (GDN_DK ** -0.5)
    bk = l2norm(qkv[..., GDN_QK:2 * GDN_QK].reshape(b, t, GDN_HEADS, GDN_DK))
    bv = qkv[..., 2 * GDN_QK:].reshape(b, t, GDN_HEADS, GDN_DV)
    beta = jax.nn.sigmoid(bbeta.reshape(b, t, N_DIR, GDN_HEADS))
    glog = -jnp.exp(gdn_a_log.astype(f32)) * jax.nn.softplus(bdec.reshape(b, t, N_DIR, GDN_HEADS) + gdn_dt_bias.astype(f32))
    return aq, ak, av, ag, alog, bq, bk, bv, bg, beta, glog, mg

def run_mixers(aq, ak, av, alog, bq, bk, bv, beta, glog, sa_f, sa_b, sb_f, sb_b):
    oa_f, sa_f = gla_chunked(aq, ak, av, alog[:, :, 0], sa_f)
    oa_b, sa_b = gla_chunked(rev(aq), rev(ak), rev(av), rev(alog[:, :, 1]), sa_b)
    ob_f, sb_f = gdn_chunked(bq, bk, bv, glog[:, :, 0], beta[:, :, 0], sb_f)
    ob_b, sb_b = gdn_chunked(rev(bq), rev(bk), rev(bv), rev(glog[:, :, 1]), rev(beta[:, :, 1]), sb_b)
    return oa_f + rev(oa_b), ob_f + rev(ob_b), sa_f, sa_b, sb_f, sb_b

def branch_merge(oa, ob, ag, bg, mg, gla_onorm, gdn_onorm, w_gla_out, w_gdn_out, b_gate, w_o):
    b, t = oa.shape[0], oa.shape[1]
    ya = rmsnorm(oa, gla_onorm).reshape(b, t, GLA_V) * jax.nn.silu(ag)
    yb = rmsnorm(ob, gdn_onorm).reshape(b, t, GDN_V) * jax.nn.silu(bg)
    gates = jax.nn.sigmoid(mg + b_gate.astype(jnp.float32))
    merged = gates[..., :D_MODEL] * jnp.matmul(ya, w_gla_out) + gates[..., D_MODEL:] * jnp.matmul(yb, w_gdn_out)
    return jnp.matmul(merged, w_o)

def first_inputs(seed: int = 0) -> dict:
    key = jax.random.key(seed)
    ks = jax.random.split(key, 24)

    def nrm(k, shape, scale):
        return jax.random.normal(k, shape, jnp.float32) * scale

    dt = jnp.exp(jax.random.uniform(ks[13], (DEPTH, N_DIR, GDN_HEADS), jnp.float32, np.log(1e-3), np.log(1e-1)))
    return {
        'x': nrm(ks[0], (BATCH, SEQ, D_MODEL), 1.0),
        'c': nrm(ks[1], (BATCH, D_MODEL), 1.0),
        'ctx': nrm(ks[2], (BATCH, CTX_LEN, D_MODEL), 1.0),
        'c_ctx': nrm(ks[3], (D_MODEL,), 1.0),
        'w_mod': nrm(ks[4], (DEPTH, D_MODEL, 3 * D_MODEL), 0.5 * D_MODEL ** -0.5),
        'b_mod': nrm(ks[5], (DEPTH, 3 * D_MODEL), 0.02),
        'norm_g': 1.0 + nrm(ks[6], (DEPTH, D_MODEL), 0.05),
        'w_in': nrm(ks[7], (DEPTH, D_MODEL, D_IN), D_MODEL ** -0.5),
        'gla_up': nrm(ks[8], (DEPTH, N_DIR, GLA_RANK, GLA_QK), GLA_RANK ** -0.5),
        'gla_ub': nrm(ks[9], (DEPTH, N_DIR, GLA_QK), 0.1),
        'gla_onorm': 1.0 + nrm(ks[10], (DEPTH, GLA_DV), 0.05),
        'gdn_conv': nrm(ks[11], (DEPTH, CONV_K, CONV_K, CONV_CH), 1.0 / CONV_K),
        'gdn_a_log': jnp.log(jax.random.uniform(ks[12], (DEPTH, N_DIR, GDN_HEADS), jnp.float32, 1.0, 16.0)),
        'gdn_dt_bias': dt + jnp.log(-jnp.expm1(-dt)),
        'gdn_onorm': 1.0 + nrm(ks[14], (DEPTH, GDN_DV), 0.05),
        'w_gla_out': nrm(ks[15], (DEPTH, GLA_V, D_MODEL), GLA_V ** -0.5),
        'w_gdn_out': nrm(ks[16], (DEPTH, GDN_V, D_MODEL), GDN_V ** -0.5),
        'b_gate': nrm(ks[17], (DEPTH, 2 * D_MODEL), 0.1),
        'w_o': nrm(ks[18], (DEPTH, D_MODEL, D_MODEL), D_MODEL ** -0.5),
        'final_g': 1.0 + nrm(ks[19], (D_MODEL,), 0.05),
    }

def first_block(x, c, ctx, c_ctx, w_mod, b_mod, norm_g, w_in, gla_up, gla_ub, gla_onorm, gdn_conv,
              gdn_a_log, gdn_dt_bias, gdn_onorm, w_gla_out, w_gdn_out, b_gate, w_o, final_g):
    dtype = x.dtype
    b = x.shape[0]
    f32 = jnp.float32
    for l in range(DEPTH):
        mod_x = jnp.matmul(jax.nn.silu(c), w_mod[l]) + b_mod[l]
        mod_c = jnp.matmul(jax.nn.silu(c_ctx), w_mod[l]) + b_mod[l]
        sh_x, sc_x, gt_x = mod_x[:, :D_MODEL], mod_x[:, D_MODEL:2 * D_MODEL], mod_x[:, 2 * D_MODEL:]
        sh_c, sc_c, gt_c = mod_c[:D_MODEL], mod_c[D_MODEL:2 * D_MODEL], mod_c[2 * D_MODEL:]
        hx = rmsnorm(x, norm_g[l]) * (1.0 + sc_x[:, None, :]) + sh_x[:, None, :]
        hc = rmsnorm(ctx, norm_g[l]) * (1.0 + sc_c) + sh_c

        (caq, cak, cav, cag, calog, cbq, cbk, cbv, cbg, cbeta, cglog, cmg) = branch_inputs(
            hc, w_in[l], gla_up[l], gla_ub[l], gdn_conv[l], gdn_a_log[l], gdn_dt_bias[l], False)
        za = jnp.zeros((b, GLA_HEADS, GLA_DK, GLA_DV), f32)
        zb = jnp.zeros((b, GDN_HEADS, GDN_DK, GDN_DV), f32)
        coa, cob, sa_f, sa_b, sb_f, sb_b = run_mixers(caq, cak, cav, calog, cbq, cbk, cbv, cbeta, cglog, za, za, zb, zb)

        (aq, ak, av, ag, alog, bq, bk, bv, bg, beta, glog, mg) = branch_inputs(
            hx, w_in[l], gla_up[l], gla_ub[l], gdn_conv[l], gdn_a_log[l], gdn_dt_bias[l], True)
        oa, ob, _, _, _, _ = run_mixers(aq, ak, av, alog, bq, bk, bv, beta, glog, sa_f, sa_b, sb_f, sb_b)
        out_x = branch_merge(oa, ob, ag, bg, mg, gla_onorm[l], gdn_onorm[l], w_gla_out[l], w_gdn_out[l], b_gate[l], w_o[l])
        if l < DEPTH - 1:
            out_c = branch_merge(coa, cob, cag, cbg, cmg, gla_onorm[l], gdn_onorm[l], w_gla_out[l], w_gdn_out[l], b_gate[l], w_o[l])
            ctx = ctx + (gt_c * out_c).astype(dtype)
        x = x + (gt_x[:, None, :] * out_x).astype(dtype)
    return rmsnorm(x, final_g)


HG_HEADS = 8
HG_DK = 128
HG_DV = 128
HG_WIDTH = HG_HEADS * HG_DK

MA_INNER = 2 * D_MODEL
MA_HEAD_DIM = 64
MA_HEADS = MA_INNER // MA_HEAD_DIM
MA_GROUPS = 8
MA_STATE = 128
MA_CONV = 5
MA_XB = MA_INNER + MA_GROUPS * MA_STATE
MA_XBC = MA_XB + MA_GROUPS * MA_STATE

PEER_HEADS = 8
PEER_NKEYS = 128
PEER_EXPERTS = PEER_NKEYS * PEER_NKEYS
PEER_TOPK = 16
PEER_DKEY = 256
PEER_BLOCK = 128

DN_ALPHA = (2.0 * DEPTH) ** 0.25
DN_BETA = (8.0 * DEPTH) ** -0.25
LN_EPS = 1e-6

STATE_SIZES = (HG_WIDTH, HG_WIDTH, HG_WIDTH, MA_XB, MA_HEADS, MA_HEADS)
READ_SIZES = (HG_WIDTH, HG_WIDTH, MA_GROUPS * MA_STATE, MA_INNER, D_MODEL, D_MODEL)
STATE_DIM = sum(STATE_SIZES)
IN_DIM = STATE_DIM + sum(READ_SIZES)


def _split(a, sizes):
    return jnp.split(a, np.cumsum(sizes)[:-1].tolist(), axis=-1)

def _flip(a):
    return jnp.flip(a, axis=1)

def layer_norm(x):
    xf = x.astype(jnp.float32)
    mu = jnp.mean(xf, -1, keepdims=True)
    var = jnp.mean(jnp.square(xf - mu), -1, keepdims=True)
    return ((xf - mu) * lax.rsqrt(var + LN_EPS)).astype(x.dtype)

def rms_norm(x, w):
    xf = x.astype(jnp.float32)
    return xf * lax.rsqrt(jnp.mean(xf * xf, -1, keepdims=True) + LN_EPS) * w.astype(jnp.float32)

def modulate(x, shift, scale):
    return layer_norm(x) * (1 + scale) + shift

def post_ln(z, g, b):
    return layer_norm(z) * g + b

def to_col_major(a, rows):
    b = a.shape[0]
    return a.reshape(b, rows, GRID_W, *a.shape[2:]).swapaxes(1, 2).reshape(a.shape)

def to_row_major(a, rows):
    b = a.shape[0]
    return a.reshape(b, GRID_W, rows, *a.shape[2:]).swapaxes(1, 2).reshape(a.shape)

def centred_dwconv(a, w, bias, rows):
    b, t, ch = a.shape
    seqs = a if rows is None else a.reshape(b * GRID_W, rows, ch)
    pad = MA_CONV // 2
    y = lax.conv_general_dilated(seqs, w.T[:, None, :].astype(a.dtype), (1,), [(pad, pad)],
                                 dimension_numbers=('NWC', 'WIO', 'NWC'), feature_group_count=ch)
    return (y + bias.astype(a.dtype)).reshape(b, t, ch)

def hgrn2_forget(f_raw, lb):
    f = lb + (1 - lb) * jax.nn.sigmoid(f_raw.astype(jnp.float32))
    return jnp.log(f), 1 - f

def hgrn2_chunk_scan(q, k, v, logf, s0):
    b, t, h, _ = q.shape
    n = t // CHUNK
    causal = jnp.tril(jnp.ones((CHUNK, CHUNK), bool))

    def chunks(a):
        return a.reshape(b, n, CHUNK, h, a.shape[-1]).transpose(1, 0, 3, 2, 4)

    def step(s, inp):
        qc, kc, vc, gc = inp
        gcum = jnp.cumsum(gc, axis=2)
        decay = jnp.exp(jnp.where(causal[:, :, None],
                                  gcum[:, :, :, None, :] - gcum[:, :, None, :, :], -jnp.inf))
        att = jnp.einsum('bhtd,bhtsd,bhsd->bhts', qc, decay, kc)
        glast = gcum[:, :, -1:, :]
        o = (jnp.einsum('bhts,bhsv->bhtv', att, vc)
             + jnp.einsum('bhtd,bhdv->bhtv', qc * jnp.exp(gcum), s))
        s = (jnp.exp(glast[:, :, 0, :, None]) * s
             + jnp.einsum('bhsd,bhsv->bhdv', kc * jnp.exp(glast - gcum), vc))
        return s, o

    s_fin, o = lax.scan(step, s0, (chunks(q), chunks(k), chunks(v), chunks(logf)))
    return o.transpose(1, 0, 3, 2, 4).reshape(b, t, h, v.shape[-1]), s_fin

def hgrn2_final_state(k, v, logf):
    gcum = jnp.cumsum(logf, axis=1)
    return jnp.einsum('bthd,bthv->bhdv', k * jnp.exp(gcum[:, -1:] - gcum), v)

def ssd_chunk_scan(xh, dt, a, bm, cm, h0):
    b, t, h, p = xh.shape
    g, nst = bm.shape[2], bm.shape[3]
    hpg = h // g
    n = t // CHUNK
    causal = jnp.tril(jnp.ones((CHUNK, CHUNK), bool))
    xdt = (xh * dt[..., None]).reshape(b, n, CHUNK, h, p).transpose(1, 0, 2, 3, 4)
    loga = (dt * a).reshape(b, n, CHUNK, h).transpose(1, 0, 3, 2)
    bch = bm.reshape(b, n, CHUNK, g, nst).transpose(1, 0, 2, 3, 4)
    cch = cm.reshape(b, n, CHUNK, g, nst).transpose(1, 0, 2, 3, 4)

    def step(hs, inp):
        xc, lc, bc, cc = inp
        lcum = jnp.cumsum(lc, axis=-1)
        lmat = jnp.exp(jnp.where(causal, lcum[..., :, None] - lcum[..., None, :], -jnp.inf))
        lmat = lmat.reshape(b, g, hpg, CHUNK, CHUNK)
        xg = xc.reshape(b, CHUNK, g, hpg, p)
        cb = jnp.einsum('btgn,bsgn->bgts', cc, bc)
        y_intra = jnp.einsum('bgts,bgjts,bsgjp->btgjp', cb, lmat, xg)
        hg = hs.reshape(b, g, hpg, p, nst)
        y_inter = jnp.einsum('btgn,bgjpn,bgjt->btgjp', cc, hg, jnp.exp(lcum).reshape(b, g, hpg, CHUNK))
        llast = lcum[..., -1]
        dec_out = jnp.exp(llast[..., None] - lcum).reshape(b, g, hpg, CHUNK)
        hs = (jnp.exp(llast)[..., None, None] * hs
              + jnp.einsum('bsgn,bgjs,bsgjp->bgjpn', bc, dec_out, xg).reshape(b, h, p, nst))
        return hs, (y_intra + y_inter).reshape(b, CHUNK, h, p)

    h_fin, y = lax.scan(step, h0, (xdt, loga, bch, cch))
    return y.transpose(1, 0, 2, 3, 4).reshape(b, t, h, p), h_fin

def ssd_final_state(xh, dt, a, bm):
    b, t, h, p = xh.shape
    g, nst = bm.shape[2], bm.shape[3]
    lcum = jnp.cumsum(dt * a, axis=1)
    wgt = dt * jnp.exp(lcum[:, -1:] - lcum)
    xg = (xh * wgt[..., None]).reshape(b, t, g, h // g, p)
    return jnp.einsum('btgn,btgjp->bgjpn', bm, xg).reshape(b, h, p, nst)

def state_side(hs, lw, lb, rows):
    b, t, _ = hs.shape
    f_f, f_b, iv, xb, dt_f, dt_b = _split(hs, STATE_SIZES)
    heads = lambda a: a.reshape(b, t, HG_HEADS, a.shape[-1] // HG_HEADS)
    logf_f, k_f = hgrn2_forget(f_f, lb[0])
    logf_b, k_b = hgrn2_forget(f_b, lb[1])
    if rows is not None:
        xb, dt_f, dt_b = to_col_major(xb, rows), to_col_major(dt_f, rows), to_col_major(dt_b, rows)
    xb = jax.nn.silu(centred_dwconv(xb, lw['ma_conv_w'][:MA_XB], lw['ma_conv_b'][:MA_XB], rows))
    xh, bm = _split(xb, (MA_INNER, MA_GROUPS * MA_STATE))
    dtb = lw['ma_dt_bias'].astype(jnp.float32)
    dt_f = jax.nn.softplus(dt_f.astype(jnp.float32) + dtb[0])
    dt_b = jax.nn.softplus(dt_b.astype(jnp.float32) + dtb[1])
    hg = (heads(k_f), heads(logf_f), heads(k_b), heads(logf_b), heads(iv))
    ma = (xh.reshape(b, t, MA_HEADS, MA_HEAD_DIM), bm.reshape(b, t, MA_GROUPS, MA_STATE), dt_f, dt_b)
    return hg, ma

def context_states(uc, lw, lb):
    hs = jnp.einsum('btd,de->bte', uc, lw['w_in'][:, :STATE_DIM])
    (k_f, lf_f, k_b, lf_b, iv), (xh, bm, dt_f, dt_b) = state_side(hs, lw, lb, None)
    a = -jnp.exp(lw['ma_a_log'].astype(jnp.float32))
    return (hgrn2_final_state(k_f, iv, lf_f),
            hgrn2_final_state(_flip(k_b), _flip(iv), _flip(lf_b)),
            ssd_final_state(xh, dt_f, a[0], bm),
            ssd_final_state(_flip(xh), _flip(dt_b), a[1], _flip(bm)))

def token_mix(u, lw, lb, s_init, rows):
    b, t, _ = u.shape
    proj = jnp.einsum('btd,de->bte', u, lw['w_in'])
    (k_f, lf_f, k_b, lf_b, iv), (xh, bm, dt_f, dt_b) = state_side(proj[..., :STATE_DIM], lw, lb, rows)
    q, og, cm, z, ga, gb = _split(proj[..., STATE_DIM:], READ_SIZES)
    q = jax.nn.silu(q).reshape(b, t, HG_HEADS, HG_DK)
    o_f, s_hf = hgrn2_chunk_scan(q, k_f, iv, lf_f, s_init[0])
    o_b, s_hb = hgrn2_chunk_scan(_flip(q), _flip(k_b), _flip(iv), _flip(lf_b), s_init[1])
    o = rms_norm(o_f + _flip(o_b), lw['hg_norm_w']).astype(u.dtype)
    o = o * jax.nn.silu(og.reshape(b, t, HG_HEADS, HG_DV))
    y_a = jnp.einsum('bte,ed->btd', o.reshape(b, t, HG_WIDTH), lw['w_branch_a'])
    if rows is not None:
        cm = to_col_major(cm, rows)
    cm = jax.nn.silu(centred_dwconv(cm, lw['ma_conv_w'][MA_XB:], lw['ma_conv_b'][MA_XB:], rows))
    cm = cm.reshape(b, t, MA_GROUPS, MA_STATE)
    a = -jnp.exp(lw['ma_a_log'].astype(jnp.float32))
    y_f, h_f = ssd_chunk_scan(xh, dt_f, a[0], bm, cm, s_init[2])
    y_b, h_b = ssd_chunk_scan(_flip(xh), _flip(dt_b), a[1], _flip(bm), _flip(cm), s_init[3])
    y = y_f + _flip(y_b) + xh * lw['ma_d'][:, None]
    y = y.reshape(b, t, MA_INNER).astype(u.dtype)
    if rows is not None:
        y = to_row_major(y, rows)
    yz = (y * jax.nn.silu(z)).reshape(b, t, MA_GROUPS, MA_INNER // MA_GROUPS)
    yz = (rms_norm(yz, jnp.ones((), jnp.float32)).reshape(b, t, MA_INNER) * lw['ma_norm_w']).astype(u.dtype)
    y_b2 = jnp.einsum('bte,ed->btd', yz, lw['w_branch_b'])
    m = jax.nn.sigmoid(ga) * y_a + jax.nn.sigmoid(gb) * y_b2
    out = jnp.einsum('btd,de->bte', m, lw['w_out'])
    return out, (s_hf, s_hb, h_f, h_b)

def peer_ffn(u, wq, subkeys, table_u, table_v):
    b, t, d = u.shape
    half = PEER_DKEY // 2

    def block(tb):
        q = jnp.einsum('pd,de->pe', tb, wq).reshape(-1, PEER_HEADS, 2, half)
        s = jnp.einsum('phik,hink->phin', q, subkeys).astype(jnp.float32)
        s1, i1 = lax.top_k(s[:, :, 0], PEER_TOPK)
        s2, i2 = lax.top_k(s[:, :, 1], PEER_TOPK)
        cand = (s1[..., :, None] + s2[..., None, :]).reshape(s1.shape[0], PEER_HEADS, -1)
        cidx = (i1[..., :, None] * PEER_NKEYS + i2[..., None, :]).reshape(s1.shape[0], PEER_HEADS, -1)
        top_s, pos = lax.top_k(cand, PEER_TOPK)
        idx = jnp.take_along_axis(cidx, pos, axis=-1)
        gate = jax.nn.softmax(top_s, axis=-1)
        ue = jnp.take(table_u, idx, axis=0)
        ve = jnp.take(table_v, idx, axis=0)
        act = jax.nn.gelu(jnp.einsum('pd,phkd->phk', tb, ue).astype(jnp.float32), approximate=False)
        return jnp.einsum('phk,phkd->pd', (gate * act).astype(tb.dtype), ve)

    out = lax.map(block, u.reshape(-1, PEER_BLOCK, d))
    return out.reshape(b, t, d)

def trunk_layer(x, xc, c, c_ctx, lw, lb, last):
    mod = jnp.einsum('bd,de->be', jax.nn.silu(c), lw['w_ada']) + lw['b_ada']
    sh1, sc1, g1, sh2, sc2, g2 = jnp.split(mod[:, None, :], 6, axis=-1)
    modc = jnp.einsum('d,de->e', jax.nn.silu(c_ctx), lw['w_ada']) + lw['b_ada']
    csh1, csc1, cg1, csh2, csc2, cg2 = jnp.split(modc, 6)
    rows = x.shape[1] // GRID_W
    uc = modulate(xc, csh1, csc1)
    if last:
        states = context_states(uc, lw, lb)
    else:
        bsz = xc.shape[0]
        zero = (jnp.zeros((bsz, HG_HEADS, HG_DK, HG_DV), jnp.float32),
                jnp.zeros((bsz, HG_HEADS, HG_DK, HG_DV), jnp.float32),
                jnp.zeros((bsz, MA_HEADS, MA_HEAD_DIM, MA_STATE), jnp.float32),
                jnp.zeros((bsz, MA_HEADS, MA_HEAD_DIM, MA_STATE), jnp.float32))
        mix_c, states = token_mix(uc, lw, lb, zero, None)
    mix, _ = token_mix(modulate(x, sh1, sc1), lw, lb, states, rows)
    x = post_ln(DN_ALPHA * x + g1 * mix, lw['ln1_g'], lw['ln1_b'])
    ffn = peer_ffn(modulate(x, sh2, sc2), lw['peer_wq'], lw['peer_subkeys'], lw['peer_u'], lw['peer_v'])
    x = post_ln(DN_ALPHA * x + g2 * ffn, lw['ln2_g'], lw['ln2_b'])
    if not last:
        xc = post_ln(DN_ALPHA * xc + cg1 * mix_c, lw['ln1_g'], lw['ln1_b'])
        ffn_c = peer_ffn(modulate(xc, csh2, csc2), lw['peer_wq'], lw['peer_subkeys'], lw['peer_u'], lw['peer_v'])
        xc = post_ln(DN_ALPHA * xc + cg2 * ffn_c, lw['ln2_g'], lw['ln2_b'])
    return x, xc

def second_inputs(seed: int = 0) -> dict:
    key = jax.random.key(seed)
    ks = jax.random.split(key, 32)
    f32 = jnp.float32
    nrm = lambda k, shape, s: jax.random.normal(k, shape, f32) * s
    L, D = DEPTH, D_MODEL
    dt0 = jnp.exp(jax.random.uniform(ks[12], (L, 2, MA_HEADS), f32, math.log(1e-3), math.log(1e-1)))
    return {
        'x': nrm(ks[0], (BATCH, SEQ, D), 1.0),
        'c': nrm(ks[1], (BATCH, D), 1.0),
        'ctx': nrm(ks[2], (BATCH, CTX_LEN, D), 1.0),
        'c_ctx': nrm(ks[3], (D,), 1.0),
        'w_ada': nrm(ks[4], (L, D, 6 * D), 0.5 * D ** -0.5),
        'b_ada': nrm(ks[5], (L, 6 * D), 0.02),
        'w_in': nrm(ks[6], (L, D, IN_DIM), D ** -0.5),
        'hg_lb_logits': nrm(ks[7], (2, L + 1, HG_WIDTH), 0.5),
        'hg_norm_w': 1.0 + nrm(ks[8], (L, HG_DV), 0.02),
        'ma_conv_w': nrm(ks[9], (L, MA_XBC, MA_CONV), MA_CONV ** -0.5),
        'ma_conv_b': nrm(ks[10], (L, MA_XBC), 0.02),
        'ma_dt_bias': dt0 + jnp.log(-jnp.expm1(-dt0)),
        'ma_a_log': jnp.log(jax.random.uniform(ks[11], (L, 2, MA_HEADS), f32, 1.0, 16.0)),
        'ma_d': 1.0 + nrm(ks[13], (L, MA_HEADS), 0.02),
        'ma_norm_w': 1.0 + nrm(ks[14], (L, MA_INNER), 0.02),
        'w_branch_a': nrm(ks[15], (L, HG_WIDTH, D), HG_WIDTH ** -0.5),
        'w_branch_b': nrm(ks[16], (L, MA_INNER, D), MA_INNER ** -0.5),
        'w_out': nrm(ks[17], (L, D, D), DN_BETA * D ** -0.5),
        'ln1_g': 1.0 + nrm(ks[18], (L, D), 0.02),
        'ln1_b': nrm(ks[19], (L, D), 0.02),
        'peer_wq': nrm(ks[20], (L, D, PEER_HEADS * PEER_DKEY), D ** -0.5),
        'peer_subkeys': nrm(ks[21], (L, PEER_HEADS, 2, PEER_NKEYS, PEER_DKEY // 2), (PEER_DKEY // 2) ** -0.5),
        'peer_u': nrm(ks[22], (L, PEER_EXPERTS, D), D ** -0.5),
        'peer_v': nrm(ks[23], (L, PEER_EXPERTS, D), DN_BETA),
        'ln2_g': 1.0 + nrm(ks[24], (L, D), 0.02),
        'ln2_b': nrm(ks[25], (L, D), 0.02),
    }

def second_block(x, c, ctx, c_ctx, w_ada, b_ada, w_in, hg_lb_logits, hg_norm_w, ma_conv_w, ma_conv_b,
              ma_dt_bias, ma_a_log, ma_d, ma_norm_w, w_branch_a, w_branch_b, w_out, ln1_g, ln1_b,
              peer_wq, peer_subkeys, peer_u, peer_v, ln2_g, ln2_b):
    lb_all = jnp.cumsum(jax.nn.softmax(hg_lb_logits.astype(jnp.float32), axis=1), axis=1)
    xc = ctx
    for l in range(DEPTH):
        lw = {'w_ada': w_ada[l], 'b_ada': b_ada[l], 'w_in': w_in[l], 'hg_norm_w': hg_norm_w[l],
              'ma_conv_w': ma_conv_w[l], 'ma_conv_b': ma_conv_b[l], 'ma_dt_bias': ma_dt_bias[l],
              'ma_a_log': ma_a_log[l], 'ma_d': ma_d[l], 'ma_norm_w': ma_norm_w[l],
              'w_branch_a': w_branch_a[l], 'w_branch_b': w_branch_b[l], 'w_out': w_out[l],
              'ln1_g': ln1_g[l], 'ln1_b': ln1_b[l], 'peer_wq': peer_wq[l], 'peer_subkeys': peer_subkeys[l],
              'peer_u': peer_u[l], 'peer_v': peer_v[l], 'ln2_g': ln2_g[l], 'ln2_b': ln2_b[l]}
        x, xc = trunk_layer(x, xc, c, c_ctx, lw, lb_all[:, l], l == DEPTH - 1)
    return x


_first_inputs = second_inputs


def second_inputs(seed=0):
    import zlib

    import numpy as np

    out = dict(_first_inputs(seed))
    spreads = {}
    factors = {'ctx': 7.475,
     'c_ctx': 7.665,
     'b_ada': 3.141,
     'hg_lb_logits': 8.0,
     'hg_norm_w': 8.0,
     'ma_conv_b': 8.0,
     'ma_d': 8.0,
     'ma_norm_w': 8.0,
     'ln2_g': 2.856,
     'ln2_b': 2.807}
    for name, (base, spread) in spreads.items():
        noise = np.random.default_rng([zlib.crc32(name.encode()), seed]).standard_normal(out[name].shape)
        drawn = base * np.exp(spread * noise) if base else spread * noise
        out[name] = __import__('jax').numpy.asarray(drawn.astype(out[name].dtype))
    for name, factor in factors.items():
        out[name] = (out[name] * factor).astype(out[name].dtype)
    return out


_narrow_inputs = second_inputs


def second_inputs(seed=0):

    out = dict(_narrow_inputs(seed))
    wider = {'hg_norm_w': 5.92, 'ma_d': 5.63, 'ma_norm_w': 4.27, 'ln2_g': 3.17, 'ln2_b': 3.21}
    for name, times in wider.items():
        mean = out[name].mean()
        out[name] = (mean + times * (out[name] - mean)).astype(out[name].dtype)
    return out


def setup_inputs(seed=0):
    out = dict(first_inputs(seed))
    for name, value in second_inputs(seed + 1).items():
        if name != "x":
            out[name + "_2"] = value
    return out


def reference(
    x, c, ctx, c_ctx, w_mod, b_mod, norm_g, w_in, gla_up, gla_ub, gla_onorm, gdn_conv,
    gdn_a_log, gdn_dt_bias, gdn_onorm, w_gla_out, w_gdn_out, b_gate, w_o, final_g, c_2, ctx_2,
    c_ctx_2, w_ada_2, b_ada_2, w_in_2, hg_lb_logits_2, hg_norm_w_2, ma_conv_w_2, ma_conv_b_2,
    ma_dt_bias_2, ma_a_log_2, ma_d_2, ma_norm_w_2, w_branch_a_2, w_branch_b_2, w_out_2, ln1_g_2,
    ln1_b_2, peer_wq_2, peer_subkeys_2, peer_u_2, peer_v_2, ln2_g_2, ln2_b_2,
):
    x = first_block(
        x, c, ctx, c_ctx, w_mod, b_mod, norm_g, w_in, gla_up, gla_ub, gla_onorm, gdn_conv,
        gdn_a_log, gdn_dt_bias, gdn_onorm, w_gla_out, w_gdn_out, b_gate, w_o, final_g,
    )
    return second_block(
        x, c_2, ctx_2, c_ctx_2, w_ada_2, b_ada_2, w_in_2, hg_lb_logits_2, hg_norm_w_2,
        ma_conv_w_2, ma_conv_b_2, ma_dt_bias_2, ma_a_log_2, ma_d_2, ma_norm_w_2, w_branch_a_2,
        w_branch_b_2, w_out_2, ln1_g_2, ln1_b_2, peer_wq_2, peer_subkeys_2, peer_u_2, peer_v_2,
        ln2_g_2, ln2_b_2,
    )


_drawn_inputs = setup_inputs


def setup_inputs(seed=0):
    import zlib

    import numpy as np

    out = dict(_drawn_inputs(seed))
    spreads = {}
    factors = {'ctx': 3.447,
     'c_ctx': 4.854,
     'b_mod': 2.982,
     'norm_g': 2.933,
     'gla_ub': 6.459,
     'gla_onorm': 5.283,
     'gdn_onorm': 6.109,
     'b_gate': 5.736}
    for name, (base, spread) in spreads.items():
        noise = np.random.default_rng([zlib.crc32(name.encode()), seed]).standard_normal(out[name].shape)
        drawn = base * np.exp(spread * noise) if base else spread * noise
        out[name] = __import__('jax').numpy.asarray(drawn.astype(out[name].dtype))
    for name, factor in factors.items():
        out[name] = (out[name] * factor).astype(out[name].dtype)
    return out
```

```python
from contextlib import ExitStack, contextmanager

import concourse.bass as bass
from concourse import mybir

P = 128
D = 1024
KD = D // P
NCTX, NX = 256, 512
T = NCTX + NX
NC = T // P
C0 = NCTX // P
NXC = NX // P
GRID_W = 64
GRID_H = NX // GRID_W
LEVELS = 7
EPS = 1e-6

F32 = mybir.dt.float32
U32 = mybir.dt.uint32
ALU = mybir.AluOpType
ACT = mybir.ActivationFunctionType
AX = mybir.AxisListType

GLA_HEADS, GLA_RANK, GLA_TAU = 4, 16, 16.0
GDN_HEADS = 4
HG_HEADS = 8
MA_GROUPS, MA_HPG, MA_P = 8, 4, 64
MA_TAPS = 5
PEER_HEADS, PEER_KEYS, TOPK = 8, 128, 16
ALPHA = 2.0 ** 0.25

ORDER = (tuple(range(NC)), tuple(range(C0 - 1, -1, -1)) + tuple(range(NC - 1, C0 - 1, -1)))
LAST = (P - 1, 0)


class Core:

    def __init__(self, nc, ctx, dram):
        self.nc, self.ctx, self.dram, self.made = nc, ctx, dram, 0
        self.pool = [ctx.enter_context(nc.semaphore(f"stage_signal_{i}")) for i in range(40)]

    def sbuf(self, name, shape, dtype=F32):
        self.made += 1
        return self.nc.sbuf_tensor(f"{name}_{self.made}", shape, dtype)

    @contextmanager
    def stage(self, *names):
        free, given = iter(self.pool), []
        for name in names:
            given.append([next(free) for _ in range(int(name.split("*")[1]))] if "*" in name else next(free))
        with self.nc.Block() as block:
            yield (block, *given)
        sems = [s for g in given for s in (g if isinstance(g, list) else [g])]
        with self.nc.Block() as block:
            @block.sync
            def _(sp):
                for s in sems:
                    sp.sem_clear(s)


def chain(engine, sem):
    count = [0]

    def link(ins):
        count[0] += 1
        ins.then_inc(sem, 1)
        engine.wait_ge(sem, count[0])
    return link


def load_all(core, pairs):
    with core.stage("loaded") as (block, loaded):
        @block.sync
        def _(sp):
            for dst, src in pairs:
                sp.dma_start(dst, src).then_inc(loaded, 16)
            sp.wait_ge(loaded, 16 * len(pairs))


def modulation(core, sb, ps, conds, w_cols, n_cols, cols, b_cols, w_rows, n_rows, rows, b_rows):
    nc = core.nc
    RING = 4
    with ExitStack() as ctx:
        w = ctx.enter_context(core.sbuf("mod_w", [P, RING, KD * 512], F32))
        e = ctx.enter_context(core.sbuf("mod_e", [P, KD, 2], F32))
        with core.stage("loaded", "steps", "silu_ready", "w_in*4", "pe_done", "evicted") as (
                block, loaded, steps, silu_ready, w_in, pe_done, evicted):
            quads = n_cols // 4

            @block.sync
            def _(sp):
                for n in range(quads + n_rows):
                    if n >= RING:
                        sp.wait_ge(pe_done, n - RING + 1)
                    src = w_cols[n] if n < quads else w_rows[n - quads]
                    sp.dma_start(w[:, n % RING, :], src).then_inc(w_in[n % RING], 16)

            @block.scalar
            def _(act):
                act.activation(e[:], conds[:], ACT.Sigmoid).then_inc(steps, 1)

            @block.vector
            def _(dve):
                dve.wait_ge(steps, 1)
                dve.tensor_tensor(conds[:], conds[:], e[:], ALU.mult).then_inc(silu_ready, 1)
                for n in range(quads):
                    dve.wait_ge(pe_done, n + 1)
                    dve.tensor_tensor(cols[:, 4 * n:4 * n + 4, :], ps[:, n % 2, 0:8].rearrange("p (a b) -> p a b", a=4),
                                      b_cols[:, 4 * n:4 * n + 4].unsqueeze(2).to_broadcast([P, 4, 2]),
                                      ALU.add).then_inc(evicted, 1)
                for m in range(n_rows):
                    n = quads + m
                    dve.wait_ge(pe_done, n + 1)
                    dve.tensor_tensor(rows[:, m, :], ps[:, n % 2, :], b_rows[:, m, :], ALU.add).then_inc(evicted, 1)

            @block.tensor
            def _(pe):
                pe.wait_ge(silu_ready, 1)
                for n in range(quads + n_rows):
                    pe.wait_ge(w_in[n % RING], 16 * (n // RING + 1))
                    if n >= 2:
                        pe.wait_ge(evicted, n - 1)
                    if n < quads:
                        wt = w[:, n % RING, :].rearrange("p (a k c) -> p a k c", a=4, k=KD)
                        for a in range(4):
                            for k in range(KD):
                                mm = pe.matmul(ps[:, n % 2, 2 * a:2 * a + 2], wt[:, a, k, :], conds[:, k, :],
                                               start=(k == 0), stop=(k == KD - 1))
                    else:
                        wt = w[:, n % RING, :].rearrange("p (k c) -> p k c", k=KD)
                        for k in range(KD):
                            mm = pe.matmul(ps[:, n % 2, :], conds[:, k, 0:1].to_broadcast([P, P]), wt[:, k, :],
                                           start=(k == 0), stop=(k == KD - 1))
                    mm.then_inc(pe_done, 1)


def norm_transpose(core, ps, ident, eps, tiles, centre, scale, shift, hT):
    nc = core.nc
    with ExitStack() as ctx:
        sb = lambda n, s: ctx.enter_context(core.sbuf(n, s, F32))
        xn = sb("nt_xn", [P, 2, D])
        sq = sb("nt_sq", [P, D])
        st = sb("nt_st", [P, len(tiles), 4])
        with core.stage("steps", "sum_ready", "var_ready", "rstd_ready", "xn_ready", "pe_done", "evicted", "asteps") as (
                block, steps, sum_ready, var_ready, rstd_ready, xn_ready, pe_done, evicted, asteps):
            @block.vector
            def _(dve):
                link = chain(dve, steps)
                for i, (src, col, who) in enumerate(tiles):
                    s = st[:, i, :]
                    if centre:
                        link(dve.tensor_reduce(s[:, 0:1], src, AX.X, ALU.add))
                        link(dve.tensor_scalar(s[:, 1:2], s[:, 0:1], -1.0 / D, None, ALU.mult))
                    else:
                        link(dve.memset(s[:, 1:2], 0.0))
                    if i >= 2:
                        dve.wait_ge(pe_done, 2 * (i - 1))
                    dve.tensor_scalar(xn[:, i % 2, :], src, s[:, 1:2], None, ALU.add).then_inc(sum_ready, 1)
                    dve.wait_ge(rstd_ready, i + 1)
                    dve.tensor_scalar(xn[:, i % 2, :], xn[:, i % 2, :], s[:, 3:4], None, ALU.mult).then_inc(xn_ready, 1)
                    for half in range(2):
                        dve.wait_ge(pe_done, 2 * i + half + 1)
                        dve.wait_ge(xn_ready, i + 1)
                        for j in range(4):
                            k = 4 * half + j
                            ins = dve.tensor_scalar(hT[:, k, col:col + P], ps[:, half, P * j:P * j + P],
                                                    scale[:, k, who:who + 1], shift[:, k, who:who + 1], ALU.mult, ALU.add)
                        ins.then_inc(evicted, 1)

            @block.scalar
            def _(act):
                alink = chain(act, asteps)
                for i in range(len(tiles)):
                    s = st[:, i, :]
                    act.wait_ge(sum_ready, i + 1)
                    alink(act.activation(sq[:], xn[:, i % 2, :], ACT.Square, accum_out=s[:, 2:3]))
                    alink(act.activation(s[:, 3:4], s[:, 2:3], ACT.Ln, bias=eps[:, 0:1], scale=1.0 / D))
                    act.activation(s[:, 3:4], s[:, 3:4], ACT.Exp, scale=-0.5).then_inc(rstd_ready, 1)

            @block.tensor
            def _(pe):
                for i in range(len(tiles)):
                    pe.wait_ge(xn_ready, i + 1)
                    for half in range(2):
                        if i > 0:
                            pe.wait_ge(evicted, 2 * (i - 1) + half + 1)
                        for j in range(4):
                            k = 4 * half + j
                            ins = pe.transpose(ps[:, half, P * j:P * j + P], xn[:, i % 2, P * k:P * k + P], ident[:])
                        ins.then_inc(pe_done, 1)


X_ONLY, ALL = "grid tokens", "all tokens"


def project(core, ps, hT, w_dram, tiles):
    nc = core.nc
    RING = 4
    with ExitStack() as ctx:
        w = ctx.enter_context(core.sbuf("proj_w", [P, RING, KD, P], F32))
        with core.stage("w_in*4", "pe_done", "evicted") as (block, w_in, pe_done, evicted):
            @block.sync
            def _(sp):
                for n, (row, _, _) in enumerate(tiles):
                    if n >= RING:
                        sp.wait_ge(pe_done, n - RING + 1)
                    sp.dma_start(w[:, n % RING, :, :], w_dram[row]).then_inc(w_in[n % RING], 16)

            @block.tensor
            def _(pe):
                for n, (_, tokens, dst) in enumerate(tiles):
                    pe.wait_ge(w_in[n % RING], 16 * (n // RING + 1))
                    if n >= 2:
                        pe.wait_ge(evicted, n - 1)
                    M = dst.shape[0]
                    parts = [(0, 384), (384, 384)] if tokens is ALL else [(NCTX, NX)]
                    for b, (t0, nt) in enumerate(parts):
                        for k in range(KD):
                            mm = pe.matmul(ps[0:M, 2 * (n % 2) + b, 0:nt], w[:, n % RING, k, 0:M], hT[:, k, t0:t0 + nt],
                                           start=(k == 0), stop=(k == KD - 1))
                    mm.then_inc(pe_done, 1)

            @block.scalar
            def _(act):
                for n, (_, tokens, dst) in enumerate(tiles):
                    act.wait_ge(pe_done, n + 1)
                    M, b = dst.shape[0], 2 * (n % 2)
                    if tokens is ALL:
                        act.copy(dst.rearrange("p (b t) -> p b t", b=2), ps[0:M, b:b + 2, 0:384]).then_inc(evicted, 1)
                    else:
                        act.copy(dst, ps[0:M, b, :]).then_inc(evicted, 1)


def halves(ap, size):
    return ap.rearrange("p (n h l) -> p n h l", h=2, l=size)


def key_gated_head(core, k, qT, kT, gT, v, gate, norm_w, out):
    nc = core.nc
    ps = k.ps
    with ExitStack() as ctx:
        sb = lambda n, s: ctx.enter_context(core.sbuf(n, s, F32))
        cum = sb("kg_cum", [P, T])
        dec = sb("kg_dec", [P, 2, NX])
        mix = sb("kg_mix", [P, 2, NX])
        att = sb("kg_att", [P, 2, NXC, P])
        qe = sb("kg_qe", [P, 2, NX])
        kd = sb("kg_kd", [P, T])
        ktok = sb("kg_ktok", [P, NC, P])
        ebl = sb("kg_ebl", [P, NC])
        S = sb("kg_S", [P, 2, NXC + 1, P])
        scr = sb("kg_scr", [P, 2, NX])
        n_lv = LEVELS + 1
        with core.stage("dve_steps", "act_steps", "diff_ready", "dec_ready", "mix_ready", "att_done", "att_read",
                        "kd_ready", "kt_done", "kt_read", "u_done", "S_ready", "o_done", "sq_ready", "ss_done",
                        "rstd_ready", "cum_ready", "ce_ready", "wdiff_ready") as (
                block, dve_steps, act_steps, diff_ready, dec_ready, mix_ready, att_done, att_read, kd_ready, kt_done,
                kt_read, u_done, S_ready, o_done, sq_ready, ss_done, rstd_ready, cum_ready, ce_ready, wdiff_ready):
            @block.vector
            def _(dve):
                link = chain(dve, dve_steps)
                for d in range(2):
                    flip = (lambda a: a) if d == 0 else (lambda a: a[:, ::-1])
                    if d == 1:
                        dve.wait_ge(ce_ready, 3)
                    dve.tensor_tensor_scan(flip(cum[:]), flip(k.restart[:, d, :]), flip(gT[d]), 0.0,
                                           ALU.mult, ALU.add).then_inc(cum_ready, 1)
                    dve.wait_ge(cum_ready, d + 1)
                    c3 = cum[:].rearrange("p (c t) -> p c t", c=NC)
                    if d == 1:
                        dve.wait_ge(kt_done, 2)
                    dve.tensor_tensor(kd[:].rearrange("p (c t) -> p c t", c=NC),
                                      c3[:, :, LAST[d]:LAST[d] + 1].to_broadcast([P, NC, P]), c3, ALU.subtract).then_inc(wdiff_ready, 1)
                    dve.wait_ge(ce_ready, 3 * d + 3)
                    link(dve.tensor_tensor(qe[:, d, :], qe[:, d, :], qT, ALU.mult))
                    dve.tensor_tensor(kd[:], kd[:], kT[d], ALU.mult).then_inc(kd_ready, 1)
                    link(dve.memset(att[:, d, :, :], 0.0))
                    link(dve.memset(S[:, d, 0, :], 0.0))
                    x0 = cum[:, NCTX:T]
                    for lv in range(n_lv):
                        n = d * n_lv + lv
                        if lv > 0:
                            size = 1 << (lv - 1)
                            cv = halves(x0, size)
                            ref = cv[:, :, d, size - 1 if d == 0 else 0].unsqueeze(2)
                            shape = [P, NX // (2 * size), size]
                            b = n % 2
                            dv, mv = halves(dec[:, b, :], size), halves(mix[:, b, :], size)
                            qh, kh = 1 - d, d
                            if d == 0 and lv == 1 or d == 1 and lv == 1:
                                pass
                            dve.tensor_tensor(dv[:, :, kh, :], ref.to_broadcast(shape), cv[:, :, kh, :], ALU.subtract)
                            dve.tensor_tensor(dv[:, :, qh, :], cv[:, :, qh, :], ref.to_broadcast(shape),
                                              ALU.subtract).then_inc(diff_ready, 1)
                            dve.wait_ge(dec_ready, d * LEVELS + lv)
                            if n >= 2:
                                dve.wait_ge(att_done, n - 1)
                            dve.tensor_tensor(mv[:, :, kh, :], dv[:, :, kh, :],
                                              halves(kT[d][:, NCTX:T], size)[:, :, kh, :], ALU.mult)
                            dve.tensor_tensor(mv[:, :, qh, :], dv[:, :, qh, :],
                                              halves(qT, size)[:, :, qh, :], ALU.mult).then_inc(mix_ready, 1)
                        if lv > 0:
                            m = n - 1
                            dve.wait_ge(att_done, m + 1)
                            dve.copy_predicated(att[:, d, :, :],
                                                k.level[:, d, lv - 1, :].unsqueeze(1).to_broadcast([P, NXC, P]),
                                                ps[:, m % 2, :].rearrange("p (c t) -> p c t", c=NXC)).then_inc(att_read, 1)
                            dve.wait_ge(att_read, m + 1)
                    m = (d + 1) * n_lv - 1
                    dve.wait_ge(att_done, m + 1)
                    dve.copy_predicated(att[:, d, :, :], k.level[:, d, LEVELS, :].unsqueeze(1).to_broadcast([P, NXC, P]),
                                        ps[:, m % 2, :].rearrange("p (c t) -> p c t", c=NXC)).then_inc(att_read, 1)
                    dve.wait_ge(u_done, d + 1)
                    U = lambda c: ps[:, 4 + c // 4, P * (c % 4):P * (c % 4) + P]
                    slot = 0
                    for i, c in enumerate(ORDER[d][:-1]):
                        nxt = slot if i < C0 else slot + 1
                        ins = dve.scalar_tensor_tensor(out=S[:, d, nxt, :], in0=S[:, d, slot, :], scalar=ebl[:, c:c + 1],
                                                       in1=U(c), op0=ALU.mult, op1=ALU.add)
                        link(ins)
                        slot = nxt
                    dve.sem_inc(S_ready, 1)
                dve.wait_ge(rstd_ready, 1)
                link(dve.tensor_tensor(scr[:, 0, :], ps[:, 6, :], scr[:, 1, :], ALU.mult))
                link(dve.scalar_tensor_tensor(out=out, in0=scr[:, 0, :], scalar=norm_w, in1=gate,
                                              op0=ALU.mult, op1=ALU.mult))

            @block.scalar
            def _(act):
                alink = chain(act, act_steps)
                for d in range(2):
                    act.wait_ge(cum_ready, d + 1)
                    c3 = cum[:].rearrange("p (c t) -> p c t", c=NC)
                    if d == 1:
                        act.wait_ge(S_ready, 1)
                    act.activation(ebl[:], c3[:, :, LAST[d]], ACT.Exp).then_inc(ce_ready, 1)
                    act.activation(qe[:, d, :], cum[:, NCTX:T], ACT.Exp).then_inc(ce_ready, 1)
                    act.wait_ge(wdiff_ready, d + 1)
                    act.activation(kd[:], kd[:], ACT.Exp).then_inc(ce_ready, 1)
                    for lv in range(1, n_lv):
                        act.wait_ge(diff_ready, d * LEVELS + lv)
                        b = (d * n_lv + lv) % 2
                        act.activation(dec[:, b, :], dec[:, b, :], ACT.Exp).then_inc(dec_ready, 1)
                        if lv == 1:
                            act.wait_ge(kt_done, 2 * d + 1)
                            act.copy(ktok[:, 0:4, :], ps[:, 2, :].rearrange("p (c t) -> p c t", c=4)).then_inc(kt_read, 1)
                            act.wait_ge(kt_done, 2 * d + 2)
                            act.copy(ktok[:, 4:6, :], ps[:, 3, 0:2 * P].rearrange("p (c t) -> p c t", c=2)).then_inc(kt_read, 1)
                act.wait_ge(o_done, 1)
                act.activation(scr[:, 0, :], ps[:, 6, :], ACT.Square).then_inc(sq_ready, 1)
                act.wait_ge(ss_done, 1)
                alink(act.activation(scr[:, 1, :], ps[:, 7, :], ACT.Ln, bias=k.eps[:, 0:1], scale=1.0 / P))
                act.activation(scr[:, 1, :], scr[:, 1, :], ACT.Exp, scale=-0.5).then_inc(rstd_ready, 1)

            @block.tensor
            def _(pe):
                for d in range(2):
                    pe.wait_ge(kd_ready, d + 1)
                    for c in range(NC):
                        mm = pe.transpose(ps[:, 2 + c // 4, P * (c % 4):P * (c % 4) + P], kd[:, P * c:P * c + P], k.ident[:])
                        if c in (3, NC - 1):
                            mm.then_inc(kt_done, 1)
                    for lv in range(n_lv):
                        n = d * n_lv + lv
                        if n >= 2:
                            pe.wait_ge(att_read, n - 1)
                        if lv > 0:
                            pe.wait_ge(mix_ready, d * LEVELS + lv)
                        for c in range(NXC):
                            t0 = P * c
                            if lv == 0:
                                mm = pe.matmul(ps[:, n % 2, t0:t0 + P], kT[d][:, NCTX + t0:NCTX + t0 + P],
                                               qT[:, t0:t0 + P], start=True, stop=True)
                            else:
                                mm = pe.matmul(ps[:, n % 2, t0:t0 + P], mix[:, n % 2, t0:t0 + P],
                                               mix[:, n % 2, t0:t0 + P], start=True, stop=True)
                        mm.then_inc(att_done, 1)
                        if lv == 2:
                            pe.wait_ge(kt_read, 2 * d + 2)
                            if d == 1:
                                pe.wait_ge(S_ready, 1)
                            for c in ORDER[d][:-1]:
                                mm = pe.matmul(ps[:, 4 + c // 4, P * (c % 4):P * (c % 4) + P], ktok[:, c, :], v[:, c, :],
                                               start=True, stop=True)
                            mm.then_inc(u_done, 1)
                pe.wait_ge(att_read, 2 * n_lv)
                pe.wait_ge(S_ready, 2)
                for c in range(NXC):
                    o = ps[:, 6, P * c:P * c + P]
                    for d in range(2):
                        slot = ORDER[d][C0:].index(C0 + c)
                        pe.matmul(o, v[:, C0 + c, :], att[:, d, c, :], start=(d == 0), stop=False)
                        mm = pe.matmul(o, S[:, d, slot, :], qe[:, d, P * c:P * c + P], start=False, stop=(d == 1))
                mm.then_inc(o_done, 1)
                pe.wait_ge(sq_ready, 1)
                pe.matmul(ps[:, 7, :], k.ones[:], scr[:, 0, :], start=True, stop=True).then_inc(ss_done, 1)


def log_sigmoids(core, k, jobs):
    with core.stage("dsteps", "abs_ready", "log_ready", "asteps") as (block, dsteps, abs_ready, log_ready, asteps):
        @block.vector
        def _(dve):
            link = chain(dve, dsteps)
            for n, (src, bias, out, scratch, softplus, times) in enumerate(jobs):
                near, far = (ALU.max, ALU.min) if softplus else (ALU.min, ALU.max)
                if bias.shape[-1] == 1 and len(bias.shape) == 2:
                    link(dve.tensor_scalar(out, src, bias, 0.0, ALU.add, near))
                    link(dve.tensor_scalar(scratch, src, bias, 0.0, ALU.add, far))
                else:
                    link(dve.tensor_tensor(scratch, src, bias, ALU.add))
                    link(dve.tensor_scalar(out, scratch, 0.0, None, near))
                    link(dve.tensor_scalar(scratch, scratch, 0.0, None, far))
                lo, hi = (scratch, out) if softplus else (out, scratch)
                dve.tensor_tensor(scratch, lo, hi, ALU.subtract).then_inc(abs_ready, 1)
                dve.wait_ge(log_ready, n + 1)
                link(dve.tensor_tensor(out, out, scratch, ALU.add if softplus else ALU.subtract))
                if isinstance(times, float):
                    link(dve.tensor_scalar(out, out, times, None, ALU.mult))
                elif times is not None:
                    link(dve.tensor_tensor(times[0], out, times[1], ALU.mult))

        @block.scalar
        def _(act):
            alink = chain(act, asteps)
            for n, (src, bias, out, scratch, softplus, times) in enumerate(jobs):
                act.wait_ge(abs_ready, n + 1)
                alink(act.activation(scratch, scratch, ACT.Exp))
                act.activation(scratch, scratch, ACT.Ln, bias=1.0).then_inc(log_ready, 1)


def gated(core, jobs):
    with core.stage("sig_ready", "done") as (block, sig_ready, done):
        @block.scalar
        def _(act):
            for x, bias, out, scratch, silu in jobs:
                kw = {} if bias is None else {"bias": bias}
                act.activation(scratch if silu else out, x, ACT.Sigmoid, **kw).then_inc(sig_ready, 1)

        @block.vector
        def _(dve):
            for n, (x, bias, out, scratch, silu) in enumerate(jobs):
                dve.wait_ge(sig_ready, n + 1)
                if silu:
                    dve.tensor_tensor(out, x, scratch, ALU.mult).then_inc(done, 1)


def transposes(core, k, jobs):
    ps = k.ps
    with core.stage("pe_done", "evicted") as (block, pe_done, evicted):
        @block.tensor
        def _(pe):
            for n, (srcs, dst) in enumerate(jobs):
                if n >= 8:
                    pe.wait_ge(evicted, n - 7)
                R = srcs[0].shape[0]
                C = srcs[0].shape[1]
                for j, s in enumerate(srcs):
                    ins = pe.transpose(ps[0:C, n % 8, R * j:R * j + R], s, k.ident[0:R, 0:R])
                ins.then_inc(pe_done, 1)

        @block.scalar
        def _(act):
            for n, (srcs, dst) in enumerate(jobs):
                act.wait_ge(pe_done, n + 1)
                R, C, g = srcs[0].shape[0], srcs[0].shape[1], len(srcs)
                act.copy(dst, ps[0:C, n % 8, 0:R * g].rearrange("p (a b) -> p a b", a=g)).then_inc(evicted, 1)


def gla_pair(core, k, hT, pair, alrT, d, out):
    nc = core.nc
    with ExitStack() as ctx:
        sb = lambda n, s: ctx.enter_context(core.sbuf(n, s, F32))
        q = sb("gla_q", [P, NX])
        qpad = sb("gla_qpad", [P, 2, NX])
        kT = sb("gla_k", [P, T])
        v = sb("gla_v", [P, 2, T])
        vt = sb("gla_vt", [P, 2, NC, P])
        gate = sb("gla_gate", [P, 2, NX])
        g = sb("gla_g", [P, 2, T])
        scr = sb("gla_scr", [P, 2, T])
        up = sb("gla_up", [32, 2, P])
        ub = sb("gla_ub", [P, 2])
        project(core, k.ps, hT, d["w_in_gla"][pair], [
            (0, X_ONLY, q[:]), (1, ALL, kT[:]), (2, ALL, v[:, 0, :]), (3, ALL, v[:, 1, :]),
            (4, X_ONLY, gate[:, 0, :]), (5, X_ONLY, gate[:, 1, :])])
        with core.stage("loaded", "up_clear", "pad_clear") as (block, loaded, up_clear, pad_clear):
            @block.sync
            def _(sp):
                sp.dma_start(ub[:], d["gla_ub"][pair]).then_inc(loaded, 16)
                sp.wait_ge(up_clear, 1)
                sp.dma_start(up[0:16, 0, :], d["gla_up"][pair, 0]).then_inc(loaded, 16)
                sp.dma_start(up[16:32, 1, :], d["gla_up"][pair, 1]).then_inc(loaded, 16)
                sp.wait_ge(loaded, 48)

            @block.vector
            def _(dve):
                dve.memset(up[:], 0.0).then_inc(up_clear, 1)
                dve.memset(qpad[:], 0.0).then_inc(pad_clear, 1)
                dve.wait_ge(pad_clear, 1)
                for e in range(2):
                    r = slice(64 * e, 64 * e + 64)
                    dve.tensor_scalar(qpad[r, e, :], q[r, :], 64.0 ** -0.5, None, ALU.mult)

            @block.tensor
            def _(pe):
                pe.wait_ge(loaded, 48)
                for n in range(2):
                    for b in range(2):
                        pe.matmul(k.ps[:, 2 * n + b, 0:384], up[:, n, :], alrT[0:32, 384 * b:384 * b + 384],
                                  start=True, stop=True)
        log_sigmoids(core, k, [
            (k.ps[:, 2 * n:2 * n + 2, 0:384], ub[:, n:n + 1], g[:, n, :].rearrange("p (b t) -> p b t", b=2),
             scr[:, n, :].rearrange("p (b t) -> p b t", b=2), False, 1.0 / GLA_TAU) for n in range(2)])
        gated(core, [(gate[:, e, :], None, gate[:, e, :], scr[:, e, 0:NX], True) for e in range(2)])
        transposes(core, k, [([v[:, e, P * c:P * c + P] for c in cs], vt[:, e, cs[0]:cs[-1] + 1, :])
                             for e in range(2) for cs in (range(0, 4), range(4, 6))])
        for e in range(2):
            key_gated_head(core, k, qpad[:, e, :], (kT[:], kT[:]), (g[:, 0, :], g[:, 1, :]), vt[:, e, :, :],
                           gate[:, e, :], k.gla_onorm[:, 0:1], out(e))


def gdn_head(core, k, hT, head, small, out):
    nc = core.nc
    d = core.dram
    ps = k.ps
    with ExitStack() as ctx:
        sb = lambda n, s: ctx.enter_context(core.sbuf(n, s, F32))
        raw = sb("gdn_raw", [P, 3, T])
        act_ = sb("gdn_act", [P, 3, T])
        scr = sb("gdn_scr", [P, 2, T])
        gate = sb("gdn_gate", [P, NX])
        cw = sb("gdn_cw", [P, 3, 9])
        col = sb("gdn_col", [P, 4, NC])
        ktok = sb("gdn_ktok", [P, NC, P])
        vtok = sb("gdn_vtok", [P, NC, P])
        project(core, ps, hT, d["w_in_gdn"][head], [
            (0, ALL, raw[:, 0, :]), (1, ALL, raw[:, 1, :]), (2, ALL, raw[:, 2, :]), (3, X_ONLY, gate[:])])
        with core.stage("loaded", "dsteps") as (block, loaded, dsteps):
            @block.sync
            def _(sp):
                sp.dma_start(cw[:], d["gdn_conv"][head]).then_inc(loaded, 16)
                sp.wait_ge(loaded, 16)

            @block.vector
            def _(dve):
                link = chain(dve, dsteps)
                link(dve.tensor_copy(col[:], small[:, :, :, head].rearrange("p c a -> p a c")))
                dve.wait_ge(loaded, 16)
                for j in range(3):
                    ci, co = raw[:, j, 0:NCTX], act_[:, j, 0:NCTX]
                    link(dve.tensor_scalar(act_[:, j, :], raw[:, j, :], cw[:, j, 4:5], None, ALU.mult))
                    n = NCTX
                    for dw, o, i in ((-1, slice(1, n), slice(0, n - 1)), (1, slice(0, n - 1), slice(1, n))):
                        link(dve.scalar_tensor_tensor(out=co[:, o], in0=ci[:, i], scalar=cw[:, j, 4 + dw:5 + dw],
                                                      in1=co[:, o], op0=ALU.mult, op1=ALU.add))
                    gi = raw[:, j, NCTX:T].rearrange("p (r w) -> p r w", w=GRID_W)
                    go = act_[:, j, NCTX:T].rearrange("p (r w) -> p r w", w=GRID_W)
                    for dr in (-1, 0, 1):
                        for dw in (-1, 0, 1):
                            if dr == 0 and dw == 0:
                                continue
                            r0, r1 = max(0, -dr), GRID_H - max(0, dr)
                            w0, w1 = max(0, -dw), GRID_W - max(0, dw)
                            tap = 3 * (dr + 1) + dw + 1
                            link(dve.scalar_tensor_tensor(
                                out=go[:, r0:r1, w0:w1], in0=gi[:, r0 + dr:r1 + dr, w0 + dw:w1 + dw],
                                scalar=cw[:, j, tap:tap + 1], in1=go[:, r0:r1, w0:w1], op0=ALU.mult, op1=ALU.add))
        gated(core, [(act_[:, j, :], None, act_[:, j, :], raw[:, j, :], True) for j in range(3)]
              + [(gate[:], None, gate[:], scr[:, 0, 0:NX], True)])
        with core.stage("sq_ready", "ss_done", "rstd_ready", "asteps", "dsteps", "v_done") as (
                block, sq_ready, ss_done, rstd_ready, asteps, dsteps, v_done):
            @block.scalar
            def _(act):
                alink = chain(act, asteps)
                act.activation(scr[:], act_[:, 0:2, :], ACT.Square).then_inc(sq_ready, 1)
                act.wait_ge(ss_done, 1)
                sv = scr[:].rearrange("p a (b t) -> p (a b) t", b=2)
                alink(act.activation(sv, ps[:, 0:4, 0:384], ACT.Ln, bias=k.eps[:, 0:1]))
                act.activation(scr[:], scr[:], ACT.Exp, scale=-0.5).then_inc(rstd_ready, 1)

            @block.tensor
            def _(pe):
                pe.wait_ge(sq_ready, 1)
                for n in range(4):
                    mm = pe.matmul(ps[:, n, 0:384], k.ones[:], scr[:, n // 2, 384 * (n % 2):384 * (n % 2) + 384],
                                   start=True, stop=True)
                mm.then_inc(ss_done, 1)

            @block.vector
            def _(dve):
                dve.wait_ge(rstd_ready, 1)
                dve.scalar_tensor_tensor(out=act_[:, 0, :], in0=act_[:, 0, :], scalar=float(P) ** -0.5,
                                         in1=scr[:, 0, :], op0=ALU.mult, op1=ALU.mult)
                dve.tensor_tensor(act_[:, 1, :], act_[:, 1, :], scr[:, 1, :], ALU.mult)
        transposes(core, k, [([act_[:, a, P * c:P * c + P] for c in cs], dst[:, cs[0]:cs[-1] + 1, :])
                             for a, dst in ((1, ktok), (2, vtok)) for cs in (range(0, 4), range(4, 6))])
        qT, kT = act_[:, 0, NCTX:T], act_[:, 1, :]

        gc = sb("gdn_gc", [P, 2, NC])
        ex = sb("gdn_ex", [P, 3, NC])
        dec = sb("gdn_dec", [P, NC, P])
        low = sb("gdn_low", [P, NC, P])
        bt = sb("gdn_bt", [P, NC, P])
        Tm = sb("gdn_T", [P, NC, P])
        Um = sb("gdn_U", [P, NC, P])
        Pm = sb("gdn_P", [P, NC, P])
        att = sb("gdn_att", [P, 2, NXC, P])
        qe = sb("gdn_qe", [P, 2, NX])
        kg = sb("gdn_kg", [P, NC, P])
        vb = sb("gdn_vb", [P, NC, P])
        S = sb("gdn_S", [P, NC + 1, P])
        R = sb("gdn_R", [P, P])
        vn = sb("gdn_vn", [P, 2, P])
        c3 = lambda a: a.rearrange("p (b c) t -> p b c t", b=2)
        bank2 = lambda b: ps[:, b:b + 2, 0:384].rearrange("p b (c t) -> p b c t", c=3)
        chunk = lambda b, c: ps[:, b + c // 3, P * (c % 3):P * (c % 3) + P]
        for dr in range(2):
            incl = k.incl[:, dr, :]
            with core.stage("sums_done", "gc_ready", "gram_done", "dsteps", "dec_ready", "exp_ready", "low_ready",
                            "turn_done", "asteps", "evict") as (
                    block, sums_done, gc_ready, gram_done, dsteps, dec_ready, exp_ready, low_ready, turn_done, asteps, evict):
                @block.tensor
                def _(pe):
                    beta, g = col[:, dr, :], col[:, 2 + dr, :]
                    pe.matmul(ps[:, 6, 0:NC], incl, g, start=True, stop=True)
                    pe.matmul(ps[:, 6, NC:2 * NC], k.ones[:], g, start=True, stop=True).then_inc(sums_done, 1)
                    for c in range(NC):
                        pe.matmul(chunk(0, c), g[:, c:c + 1].to_broadcast([P, P]), incl, start=True, stop=True)
                        mm = pe.matmul(chunk(2, c), beta[:, c:c + 1].to_broadcast([P, P]), k.ident[:], start=True, stop=True)
                    mm.then_inc(sums_done, 1)
                    for c in range(NC):
                        kc = kT[:, P * c:P * c + P]
                        mm = pe.matmul(chunk(4, c), kc, kc, start=True, stop=True)
                    mm.then_inc(gram_done, 1)
                    pe.wait_ge(low_ready, 1)
                    for c in range(NC):
                        mm = pe.transpose(chunk(0, c), Um[:, c, :], k.ident[:])
                    mm.then_inc(turn_done, 1)
                    pe.wait_ge(gc_ready, 1)
                    for c in range(NXC):
                        mm = pe.matmul(ps[:, 7, P * c:P * c + P], kT[:, NCTX + P * c:NCTX + P * c + P],
                                       qT[:, P * c:P * c + P], start=True, stop=True)
                    mm.then_inc(turn_done, 1)

                @block.vector
                def _(dve):
                    link = chain(dve, dsteps)
                    dve.wait_ge(sums_done, 1)
                    link(dve.tensor_copy(gc[:], ps[:, 6, 0:2 * NC].rearrange("p (a c) -> p a c", a=2)))
                    dve.tensor_tensor(ex[:, 1, :], gc[:, 1, :], gc[:, 0, :], ALU.subtract).then_inc(gc_ready, 1)
                    dve.wait_ge(sums_done, 2)
                    for c in range(NC):
                        ins = dve.tensor_scalar(dec[:, c, :], chunk(0, c), gc[:, 0, c:c + 1], 0.0, ALU.subtract, ALU.min)
                    ins.then_inc(dec_ready, 1)
                    dve.wait_ge(exp_ready, 3)
                    link(dve.tensor_tensor(ex[:, 0, :], ex[:, 0, :], col[:, dr, :], ALU.mult))
                    link(dve.tensor_tensor(kg[:], ktok[:], ex[:, 1, :].unsqueeze(2).to_broadcast([P, NC, P]), ALU.mult))
                    link(dve.tensor_tensor(vb[:], vtok[:], col[:, dr, :].unsqueeze(2).to_broadcast([P, NC, P]), ALU.mult))
                    dve.wait_ge(exp_ready, 4)
                    link(dve.tensor_tensor(qe[:, dr, :], qe[:, dr, :], qT, ALU.mult))
                    dve.wait_ge(exp_ready, 5)
                    link(dve.tensor_tensor(c3(low[:]), c3(dec[:]), bank2(2), ALU.mult))
                    dve.wait_ge(gram_done, 1)
                    link(dve.tensor_tensor(c3(low[:]), c3(low[:]), bank2(4), ALU.mult))
                    link(dve.tensor_tensor(bt[:], low[:], k.levelf[:, dr, 1, :].unsqueeze(1).to_broadcast([P, NC, P]), ALU.mult))
                    dve.tensor_tensor(Um[:], k.ident[:].unsqueeze(1).to_broadcast([P, NC, P]), bt[:],
                                      ALU.subtract).then_inc(low_ready, 1)
                    dve.wait_ge(turn_done, 1)
                    link(dve.tensor_copy(c3(Tm[:]), bank2(0)))
                    dve.wait_ge(turn_done, 2)
                    link(dve.tensor_tensor(att[:, dr, :, :], dec[:, C0:NC, :],
                                           ps[:, 7, :].rearrange("p (c t) -> p c t", c=NXC), ALU.mult))
                    link(dve.tensor_tensor(att[:, dr, :, :], att[:, dr, :, :],
                                           incl.unsqueeze(1).to_broadcast([P, NXC, P]), ALU.mult))

                @block.scalar
                def _(act):
                    act.wait_ge(gc_ready, 1)
                    act.activation(ex[:, 0, :], gc[:, 0, :], ACT.Exp).then_inc(exp_ready, 1)
                    act.activation(ex[:, 1, :], ex[:, 1, :], ACT.Exp).then_inc(exp_ready, 1)
                    act.activation(ex[:, 2, :], gc[:, 1, :], ACT.Exp).then_inc(exp_ready, 1)
                    act.wait_ge(dec_ready, 1)
                    for c in range(NXC):
                        ins = act.activation(qe[:, dr, P * c:P * c + P], chunk(0, C0 + c), ACT.Exp)
                    ins.then_inc(exp_ready, 1)
                    act.activation(dec[:], dec[:], ACT.Exp).then_inc(exp_ready, 1)
            with core.stage("dsteps", "b_ready", "p_done", "p_read", "q_done", "t_ready") as (
                    block, dsteps, b_ready, p_done, p_read, q_done, t_ready):
                @block.vector
                def _(dve):
                    for i in range(1, LEVELS):
                        dve.tensor_tensor(bt[:], low[:], k.levelf[:, dr, i + 1, :].unsqueeze(1).to_broadcast([P, NC, P]),
                                          ALU.mult).then_inc(b_ready, 1)
                        dve.wait_ge(q_done, i)
                        dve.tensor_tensor(c3(Tm[:]), c3(Tm[:]), bank2(2), ALU.subtract).then_inc(t_ready, 1)
                        dve.tensor_tensor(c3(Um[:]), c3(Um[:]), bank2(4), ALU.subtract).then_inc(t_ready, 1)

                @block.scalar
                def _(act):
                    for i in range(1, LEVELS):
                        act.wait_ge(p_done, i)
                        act.copy(c3(Pm[:]), bank2(0)).then_inc(p_read, 1)

                @block.tensor
                def _(pe):
                    for i in range(1, LEVELS):
                        pe.wait_ge(b_ready, i)
                        if i > 1:
                            pe.wait_ge(t_ready, 2 * (i - 1))
                        for c in range(NC):
                            mm = pe.matmul(chunk(0, c), bt[:, c, :], Tm[:, c, :], start=True, stop=True)
                        mm.then_inc(p_done, 1)
                        pe.wait_ge(p_read, i)
                        for c in range(NC):
                            pe.matmul(chunk(2, c), Um[:, c, :], Pm[:, c, :], start=True, stop=True)
                            mm = pe.matmul(chunk(4, c), Pm[:, c, :], Um[:, c, :], start=True, stop=True)
                        mm.then_inc(q_done, 1)
            with core.stage("dsteps", "S_ready", "x_done", "r_ready", "w_done", "v_ready", "u_done") as (
                    block, dsteps, S_ready, x_done, r_ready, w_done, v_ready, u_done):
                @block.vector
                def _(dve):
                    link = chain(dve, dsteps)
                    dve.memset(S[:, 0, :], 0.0).then_inc(S_ready, 1)
                    for i, c in enumerate(ORDER[dr]):
                        dve.wait_ge(x_done, i + 1)
                        dve.scalar_tensor_tensor(out=R[:], in0=ps[:, 0, 0:P], scalar=ex[:, 0, c:c + 1], in1=vb[:, c, :],
                                                 op0=ALU.mult, op1=ALU.subtract).then_inc(r_ready, 1)
                        dve.wait_ge(w_done, i + 1)
                        dve.tensor_scalar(vn[:, i % 2, :], ps[:, 1, 0:P], -1.0, None, ALU.mult).then_inc(v_ready, 1)
                        dve.wait_ge(u_done, i + 1)
                        dve.scalar_tensor_tensor(out=S[:, i + 1, :], in0=S[:, i, :], scalar=ex[:, 2, c:c + 1],
                                                 in1=ps[:, 2, 0:P], op0=ALU.mult, op1=ALU.add).then_inc(S_ready, 1)

                @block.tensor
                def _(pe):
                    for i, c in enumerate(ORDER[dr]):
                        pe.wait_ge(S_ready, i + 1)
                        pe.matmul(ps[:, 0, 0:P], kT[:, P * c:P * c + P], S[:, i, :], start=True, stop=True).then_inc(x_done, 1)
                        pe.wait_ge(r_ready, i + 1)
                        pe.matmul(ps[:, 1, 0:P], Um[:, c, :], R[:], start=True, stop=True).then_inc(w_done, 1)
                        pe.wait_ge(v_ready, i + 1)
                        pe.matmul(ps[:, 2, 0:P], kg[:, c, :], vn[:, i % 2, :], start=True, stop=True).then_inc(u_done, 1)
                        if c >= C0:
                            o = ps[:, 6 + dr, P * (c - C0):P * (c - C0) + P]
                            pe.matmul(o, S[:, i, :], qe[:, dr, P * (c - C0):P * (c - C0) + P], start=True, stop=False)
                            pe.matmul(o, vn[:, i % 2, :], att[:, dr, c - C0, :], start=False, stop=True)
            if dr == 0:
                with core.stage("kept") as (block, kept):
                    @block.vector
                    def _(dve):
                        dve.tensor_copy(raw[:, 2, 0:NX], ps[:, 6, :]).then_inc(kept, 1)
        with core.stage("dsteps", "o_ready", "sq_ready", "ss_done", "rstd_ready", "asteps") as (
                block, dsteps, o_ready, sq_ready, ss_done, rstd_ready, asteps):
            @block.vector
            def _(dve):
                link = chain(dve, dsteps)
                dve.tensor_tensor(raw[:, 0, 0:NX], raw[:, 2, 0:NX], ps[:, 7, :], ALU.add).then_inc(o_ready, 1)
                dve.wait_ge(rstd_ready, 1)
                link(dve.tensor_tensor(raw[:, 0, 0:NX], raw[:, 0, 0:NX], raw[:, 1, 0:NX], ALU.mult))
                link(dve.scalar_tensor_tensor(out=out, in0=raw[:, 0, 0:NX], scalar=k.gdn_onorm[:, 0:1], in1=gate[:],
                                              op0=ALU.mult, op1=ALU.mult))

            @block.scalar
            def _(act):
                alink = chain(act, asteps)
                act.wait_ge(o_ready, 1)
                act.activation(raw[:, 1, 0:NX], raw[:, 0, 0:NX], ACT.Square).then_inc(sq_ready, 1)
                act.wait_ge(ss_done, 1)
                alink(act.activation(raw[:, 1, 0:NX], ps[:, 0, :], ACT.Ln, bias=k.eps[:, 0:1], scale=1.0 / P))
                act.activation(raw[:, 1, 0:NX], raw[:, 1, 0:NX], ACT.Exp, scale=-0.5).then_inc(rstd_ready, 1)

            @block.tensor
            def _(pe):
                pe.wait_ge(sq_ready, 1)
                pe.matmul(ps[:, 0, :], k.ones[:], raw[:, 1, 0:NX], start=True, stop=True).then_inc(ss_done, 1)


def merge(core, k, hT, w_dram, nA, nB, aT, bT, gate_bias, mT):
    nc = core.nc
    ps = k.ps
    width = nA + nB + 2 * KD
    with ExitStack() as ctx:
        w = ctx.enter_context(core.sbuf("mg_w", [P, 2, width, P], F32))
        sg = ctx.enter_context(core.sbuf("mg_sg", [P, 2, 2, NX], F32))
        with core.stage("w_in*2", "pe_done", "sg_ready", "dsteps", "out_done") as (
                block, w_in, pe_done, sg_ready, dsteps, out_done):
            @block.sync
            def _(sp):
                for n in range(KD):
                    if n >= 2:
                        sp.wait_ge(pe_done, n - 1)
                    sp.dma_start(w[:, n % 2, :, :], w_dram[n]).then_inc(w_in[n % 2], 16)

            @block.tensor
            def _(pe):
                for n in range(KD):
                    pe.wait_ge(w_in[n % 2], 16 * (n // 2 + 1))
                    if n >= 2:
                        pe.wait_ge(out_done, n - 1)
                    b, o = 4 * (n % 2), 0
                    for bank, (kn, src) in enumerate(((KD, None), (KD, None), (nA, aT), (nB, bT))):
                        off = (nA + nB, nA + nB + KD, 0, nA)[bank]
                        for j in range(kn):
                            rhs = hT[:, j, NCTX:T] if src is None else src[:, j, :]
                            mm = pe.matmul(ps[:, b + bank, :], w[:, n % 2, off + j, :], rhs, start=(j == 0), stop=(j == kn - 1))
                    mm.then_inc(pe_done, 1)

            @block.scalar
            def _(act):
                for n in range(KD):
                    act.wait_ge(pe_done, n + 1)
                    if n >= 2:
                        act.wait_ge(out_done, n - 1)
                    b = 4 * (n % 2)
                    for a in range(2):
                        kw = {} if gate_bias is None else {"bias": gate_bias[:, KD * a + n:KD * a + n + 1]}
                        act.activation(sg[:, n % 2, a, :], ps[:, b + a, :], ACT.Sigmoid, **kw).then_inc(sg_ready, 1)

            @block.vector
            def _(dve):
                link = chain(dve, dsteps)
                for n in range(KD):
                    dve.wait_ge(sg_ready, 2 * n + 2)
                    b = 4 * (n % 2)
                    for a in range(2):
                        link(dve.tensor_tensor(sg[:, n % 2, a, :], sg[:, n % 2, a, :], ps[:, b + 2 + a, :], ALU.mult))
                    dve.tensor_tensor(mT[:, n, :], sg[:, n % 2, 0, :], sg[:, n % 2, 1, :], ALU.add).then_inc(out_done, 1)


def output_product(core, k, mT, w_dram, gate_row, alpha, xs):
    nc = core.nc
    ps = k.ps
    with ExitStack() as ctx:
        w = ctx.enter_context(core.sbuf("op_w", [P, KD, D], F32))
        y = ctx.enter_context(core.sbuf("op_y", [P, 2, 512], F32))
        with core.stage("w_in", "pe_done", "out_done", "dsteps") as (block, w_in, pe_done, out_done, dsteps):
            @block.sync
            def _(sp):
                for j in range(KD):
                    sp.dma_start(w[:, j, :], w_dram[P * j:P * j + P, :]).then_inc(w_in, 16)
                sp.wait_ge(w_in, 16 * KD)

            @block.tensor
            def _(pe):
                pe.wait_ge(w_in, 16 * KD)
                for n in range(8):
                    t, h = n // 2, n % 2
                    for j in range(KD):
                        mm = pe.matmul(ps[:, n, :], mT[:, j, P * t:P * t + P], w[:, j, 512 * h:512 * h + 512],
                                       start=(j == 0), stop=(j == KD - 1))
                    mm.then_inc(pe_done, 1)

            @block.vector
            def _(dve):
                link = chain(dve, dsteps)
                for n in range(8):
                    t, h = n // 2, n % 2
                    dve.wait_ge(pe_done, n + 1)
                    link(dve.tensor_tensor(y[:, n % 2, :], ps[:, n, :], gate_row[:, h, :], ALU.mult))
                    x = xs[t][:, 512 * h:512 * h + 512]
                    link(dve.scalar_tensor_tensor(out=x, in0=x, scalar=alpha, in1=y[:, n % 2, :], op0=ALU.mult, op1=ALU.add))


def norm_rows(core, k, tiles, centre, g, b):
    nc = core.nc
    with ExitStack() as ctx:
        sq = ctx.enter_context(core.sbuf("nr_sq", [P, D], F32))
        st = ctx.enter_context(core.sbuf("nr_st", [P, len(tiles), 4], F32))
        with core.stage("dsteps", "asteps", "mean_ready", "rstd_ready") as (block, dsteps, asteps, mean_ready, rstd_ready):
            @block.vector
            def _(dve):
                link = chain(dve, dsteps)
                for i, x in enumerate(tiles):
                    s = st[:, i, :]
                    if centre:
                        link(dve.tensor_reduce(s[:, 0:1], x, AX.X, ALU.add))
                        link(dve.tensor_scalar(s[:, 1:2], s[:, 0:1], -1.0 / D, None, ALU.mult))
                        link(dve.tensor_scalar(x, x, s[:, 1:2], None, ALU.add))
                    dve.sem_inc(mean_ready, 1)
                for i, x in enumerate(tiles):
                    s = st[:, i, :]
                    dve.wait_ge(rstd_ready, i + 1)
                    link(dve.scalar_tensor_tensor(out=x, in0=x, scalar=s[:, 3:4], in1=g, op0=ALU.mult, op1=ALU.mult))
                    if b is not None:
                        link(dve.tensor_tensor(x, x, b, ALU.add))

            @block.scalar
            def _(act):
                alink = chain(act, asteps)
                for i, x in enumerate(tiles):
                    s = st[:, i, :]
                    act.wait_ge(mean_ready, i + 1)
                    alink(act.activation(sq[:], x, ACT.Square, accum_out=s[:, 2:3]))
                    alink(act.activation(s[:, 3:4], s[:, 2:3], ACT.Ln, bias=k.eps[:, 0:1], scale=1.0 / D))
                    act.activation(s[:, 3:4], s[:, 3:4], ACT.Exp, scale=-0.5).then_inc(rstd_ready, 1)


class Buffers:
    pass


def program(nc, dram, out, taps=None, upto=99):
    d = dram
    with ExitStack() as ctx:
        core = Core(nc, ctx, dram)
        sbt = lambda n, s, dt=F32: ctx.enter_context(core.sbuf(n, s, dt))
        k = Buffers()
        k.ps = ctx.enter_context(nc.psum_tensor("ps", [P, 8, 512], F32))
        k.ident, k.ones = sbt("ident", [P, P]), sbt("ones", [P, P])
        k.incl, k.levelf = sbt("incl", [P, 2, P]), sbt("levelf", [P, 2, LEVELS + 1, P])
        k.level = sbt("level", [P, 2, LEVELS + 1, P], U32)
        k.restart = sbt("restart", [P, 2, T])
        k.eps = sbt("eps", [P, 1])
        hT = sbt("hT", [P, KD, T])
        xs = sbt("xs", [P, NXC, D])

        def tap(name, ap):
            if taps is not None and name in taps:
                with core.stage("kept") as (block, kept):
                    @block.sync
                    def _(sp):
                        sp.dma_start(taps[name], ap).then_inc(kept, 16)
                        sp.wait_ge(kept, 16)

        load_all(core, [(k.ident[:], d["ident"]), (k.ones[:], d["ones"]), (k.incl[:], d["incl"]),
                        (k.levelf[:], d["levelf"]), (k.level[:], d["level"]), (k.restart[:], d["restart"])]
                 + [(xs[:, t, :], d["x"][P * t:P * t + P, :]) for t in range(NXC)])
        with core.stage("eps_ready") as (block, eps_ready):
            @block.vector
            def _(dve):
                dve.memset(k.eps[:], EPS).then_inc(eps_ready, 1)

        first_block(core, k, hT, xs, tap)
        tap("x1", xs[:])
        if upto > 1:
            second_block(core, k, hT, xs, tap, upto)
        with core.stage("stored") as (block, stored):
            @block.sync
            def _(sp):
                for t in range(NXC):
                    sp.dma_start(out[P * t:P * t + P, :], xs[:, t, :]).then_inc(stored, 16)
                sp.wait_ge(stored, 16 * NXC)


def first_block(core, k, hT, xs, tap):
    nc, d = core.nc, core.dram
    with ExitStack() as ctx:
        sbt = lambda n, s, dt=F32: ctx.enter_context(core.sbuf(n, s, dt))
        cond = sbt("cond", [P, KD, 2])
        cols = sbt("cols", [P, 2 * KD, 2])
        rows = sbt("rows", [P, 2, 512])
        b_cols, b_rows = sbt("b_cols", [P, 2 * KD]), sbt("b_rows", [P, 2, 512])
        norm_g = sbt("norm_g", [P, KD])
        scale = sbt("scale", [P, KD, 2])
        k.gla_onorm, k.gdn_onorm = sbt("gla_onorm", [P, 1]), sbt("gdn_onorm", [P, 1])
        b_gate = sbt("b_gate", [P, 2 * KD])
        glog_rows = sbt("glog_rows", [P, 2, 8])
        load_all(core, [(cond[:], d["cond"]), (b_cols[:], d["b_mod_cols"]),
                        (b_rows[:], d["b_mod_rows"].partition_broadcast(P)),
                        (norm_g[:], d["norm_g"]), (k.gla_onorm[:], d["gla_onorm"]), (k.gdn_onorm[:], d["gdn_onorm"]),
                        (b_gate[:], d["b_gate"]), (glog_rows[:, 0, :], d["gdn_a_log"].partition_broadcast(P)),
                        (glog_rows[:, 1, :], d["gdn_dt_bias"].partition_broadcast(P))])
        modulation(core, sbt, k.ps, cond, d["w_mod_cols"], 2 * KD, cols, b_cols, d["w_mod_rows"], 2, rows, b_rows)
        with core.stage("steps") as (block, steps):
            @block.vector
            def _(dve):
                link = chain(dve, steps)
                link(dve.tensor_scalar(scale[:], cols[:, KD:2 * KD, :], 1.0, None, ALU.add))
                link(dve.tensor_tensor(scale[:], scale[:], norm_g[:].unsqueeze(2).to_broadcast([P, KD, 2]), ALU.mult))
        tap("cols1", cols[:])
        with core.sbuf("ctx_rows", [P, C0, D], F32) as ctx_rows:
            load_all(core, [(ctx_rows[:, t, :], d["ctx"][P * t:P * t + P, :]) for t in range(C0)])
            norm_transpose(core, k.ps, k.ident, k.eps,
                           [(ctx_rows[:, t, :], P * t, 1) for t in range(C0)]
                           + [(xs[:, t, :], NCTX + P * t, 0) for t in range(NXC)], False, scale, cols[:, 0:KD, :], hT)
        tap("hT1", hT[:])
        smallT = sbt("smallT", [48, T])
        small = sbt("small", [P, NC, 48])
        gates = sbt("gates", [P, NC, 4, 4])
        tmp = sbt("gates_tmp", [P, NC, 8])
        project(core, k.ps, hT, d["w_in_small"], [(0, ALL, smallT[:])])
        transposes(core, k, [([smallT[:, P * c:P * c + P] for c in cs], small[:, cs[0]:cs[-1] + 1, :])
                             for cs in (range(0, 4), range(4, 6))])
        with core.stage("exp_ready") as (block, exp_ready):
            @block.scalar
            def _(act):
                act.activation(gates[:, :, 0:2, :], small[:, :, 32:40].rearrange("p c (a h) -> p c a h", a=2), ACT.Sigmoid)
                act.activation(glog_rows[:, 0, :], glog_rows[:, 0, :], ACT.Exp).then_inc(exp_ready, 1)

            @block.vector
            def _(dve):
                dve.wait_ge(exp_ready, 1)
                dve.tensor_scalar(glog_rows[:, 0, :], glog_rows[:, 0, :], -1.0, None, ALU.mult)
        wide = lambda a: a.unsqueeze(1).to_broadcast([P, NC, 8])
        lg = gates[:, :, 2:4, :].rearrange("p c a h -> p c (a h)")
        log_sigmoids(core, k, [(small[:, :, 40:48], wide(glog_rows[:, 1, :]), lg, tmp[:], True, (lg, wide(glog_rows[:, 0, :])))])
        yaT, ybT = sbt("yaT", [P, 4, NX]), sbt("ybT", [P, 4, NX])
        with nc.Fori(0, GLA_HEADS // 2) as pair:
            gla_pair(core, k, hT, pair, smallT, d, lambda e: yaT[:, pair * 2 + e, :])
        tap("yaT", yaT[:])
        with nc.Fori(0, GDN_HEADS) as head:
            gdn_head(core, k, hT, head, gates, ybT[:, head, :])
        tap("ybT", ybT[:])
        mT = sbt("mT", [P, KD, NX])
        merge(core, k, hT, d["w_merge"], 4, 4, yaT, ybT, b_gate[:], mT)
        tap("mT1", mT[:])
        output_product(core, k, mT, d["w_o"], rows, 1.0, [xs[:, t, :] for t in range(NXC)])
        with core.sbuf("final_g", [P, D], F32) as final_g:
            load_all(core, [(final_g[:], d["final_g"].partition_broadcast(P))])
            norm_rows(core, k, [xs[:, t, :] for t in range(NXC)], False, final_g[:], None)


TG = 64
JG = 8
N_TG, N_JG = NX // TG, PEER_KEYS // JG


def top16(dve, link, values, copy, best, index):
    link(dve.max(best[:, 0:8], values))
    link(dve.max_index(index[:, 0:8], best[:, 0:8], values))
    link(dve.match_replace(copy, best[:, 0:8], values, -3.0e38))
    link(dve.max(best[:, 8:16], copy))
    link(dve.max_index(index[:, 8:16], best[:, 8:16], copy))


def route_head(core, k, hT, head, iota16, chosen):
    nc, d, ps = core.nc, core.dram, k.ps
    with ExitStack() as ctx:
        sb = lambda n, s, dt=F32: ctx.enter_context(core.sbuf(n, s, dt))
        q = sb("pr_q", [P, 2, NX])
        keys = sb("pr_keys", [P, 2, P])
        sc = sb("pr_sc", [P, 2, NXC, P])
        copy = sb("pr_copy", [P, 2 * P])
        best = sb("pr_best", [P, 2, NXC, TOPK])
        idx = sb("pr_idx", [P, 2, NXC, TOPK], U32)
        idf = sb("pr_idf", [P, 2, NXC, TOPK])
        cand = sb("pr_cand", [P, NXC, TOPK, TOPK])
        top = sb("pr_top", [P, NXC, TOPK])
        pos = sb("pr_pos", [P, NXC, TOPK], U32)
        part = sb("pr_part", [P, 2, NXC, TOPK], U32)
        partf = sb("pr_partf", [P, 2, NXC, TOPK])
        hot = sb("pr_hot", [P, NXC, TOPK, TOPK])
        val = sb("pr_val", [P, 3, NXC, TOPK])
        s1 = sb("pr_s1", [P, NXC])
        project(core, ps, hT, d["w_q"][head], [(0, X_ONLY, q[:, 0, :]), (1, X_ONLY, q[:, 1, :])])
        with core.stage("loaded", "score_done", "dsteps", "shift_ready", "exp_ready") as (
                block, loaded, score_done, dsteps, shift_ready, exp_ready):
            @block.sync
            def _(sp):
                sp.dma_start(keys[:], d["subkeys"][head]).then_inc(loaded, 16)
                sp.wait_ge(loaded, 16)

            @block.tensor
            def _(pe):
                pe.wait_ge(loaded, 16)
                for i in range(2):
                    for t in range(NXC):
                        mm = pe.matmul(ps[:, i, P * t:P * t + P], q[:, i, P * t:P * t + P], keys[:, i, :], start=True, stop=True)
                    mm.then_inc(score_done, 1)

            @block.vector
            def _(dve):
                link = chain(dve, dsteps)
                big = [P, NXC, TOPK, TOPK]
                for i in range(2):
                    dve.wait_ge(score_done, i + 1)
                    link(dve.tensor_copy(sc[:, i], ps[:, i, :].rearrange("p (t n) -> p t n", t=NXC)))
                    for t in range(NXC):
                        top16(dve, link, sc[:, i, t, :], copy[:, 0:P], best[:, i, t, :], idx[:, i, t, :])
                link(dve.tensor_copy(idf[:], idx[:]))
                link(dve.tensor_tensor(cand[:], best[:, 0].unsqueeze(3).to_broadcast(big),
                                       best[:, 1].unsqueeze(2).to_broadcast(big), ALU.add))
                for t in range(NXC):
                    top16(dve, link, cand[:, t].rearrange("p a b -> p (a b)"), copy[:], top[:, t, :], pos[:, t, :])
                dve.tensor_tensor(val[:, 2], top[:], top[:, :, 0:1].to_broadcast([P, NXC, TOPK]), ALU.subtract).then_inc(shift_ready, 1)
                link(dve.tensor_scalar(part[:, 0], pos[:], 4, None, ALU.logical_shift_right))
                link(dve.tensor_scalar(part[:, 1], pos[:], 15, None, ALU.bitwise_and))
                link(dve.tensor_copy(partf[:], part[:]))
                for i in range(2):
                    link(dve.tensor_tensor(hot[:], partf[:, i].unsqueeze(3).to_broadcast(big),
                                           iota16.unsqueeze(1).unsqueeze(1).to_broadcast(big), ALU.is_equal))
                    link(dve.tensor_tensor(hot[:], hot[:], idf[:, i].unsqueeze(2).to_broadcast(big), ALU.mult))
                    link(dve.tensor_reduce(val[:, i], hot[:], AX.X, ALU.add))
                dve.wait_ge(exp_ready, 1)
                link(dve.tensor_reduce(s1[:], val[:, 2], AX.X, ALU.add))
                link(dve.reciprocal(s1[:], s1[:]))
                link(dve.tensor_tensor(val[:, 2], val[:, 2], s1[:].unsqueeze(2).to_broadcast([P, NXC, TOPK]), ALU.mult))
                link(dve.tensor_copy(chosen[:, :, :, bass.ds(head * TOPK, TOPK)], val[:].rearrange("p a t m -> p t a m")))

            @block.scalar
            def _(act):
                act.wait_ge(shift_ready, 1)
                act.activation(val[:, 2], val[:, 2], ACT.Exp).then_inc(exp_ready, 1)


def spread_gates(core, k, chosenT, iota, g_dram):
    nc, ps = core.nc, k.ps
    OH = 8
    with ExitStack() as ctx:
        sb = lambda n, s: ctx.enter_context(core.sbuf(n, s))
        cur = sb("sg_cur", [P, 3, TG])
        one = sb("sg_one", [P, OH, P])
        two = sb("sg_two", [P, OH, P])
        gbuf = sb("sg_gbuf", [P, PEER_KEYS, TG])
        with nc.Fori(0, N_TG) as tg:
            with core.stage("cur_ready", "hot_ready", "g_done", "g_read", "stored") as (
                    block, cur_ready, hot_ready, g_done, g_read, stored):
                @block.vector
                def _(dve):
                    dve.tensor_copy(cur[:], chosenT[:, :, bass.ds(tg * TG, TG)]).then_inc(cur_ready, 1)
                    dve.wait_ge(cur_ready, 1)
                    for t in range(TG):
                        if t % 4 == 0 and t >= OH:
                            dve.wait_ge(g_done, (t - OH) // 4 + 1)
                        dve.tensor_scalar(one[:, t % OH, :], iota, cur[:, 0, t:t + 1], None, ALU.is_equal)
                        ins = dve.tensor_scalar(two[:, t % OH, :], iota, cur[:, 1, t:t + 1], cur[:, 2, t:t + 1],
                                                ALU.is_equal, ALU.mult)
                        if t % 4 == 3:
                            ins.then_inc(hot_ready, 1)

                @block.tensor
                def _(pe):
                    for n in range(TG // 4):
                        pe.wait_ge(hot_ready, n + 1)
                        if n >= 8:
                            pe.wait_ge(g_read, n - 7)
                        for a in range(4):
                            t = (4 * n + a) % OH
                            mm = pe.matmul(ps[:, n % 8, P * a:P * a + P], one[:, t, :], two[:, t, :], start=True, stop=True)
                        mm.then_inc(g_done, 1)

                @block.scalar
                def _(act):
                    for n in range(TG // 4):
                        act.wait_ge(g_done, n + 1)
                        act.copy(gbuf[:, :, 4 * n:4 * n + 4].rearrange("p j t -> p t j"),
                                 ps[:, n % 8, :].rearrange("p (t j) -> p t j", t=4)).then_inc(g_read, 1)

                @block.sync
                def _(sp):
                    sp.wait_ge(g_read, TG // 4)
                    sp.dma_start(g_dram[:, :, tg].rearrange("g p e -> p g e"),
                                 gbuf[:].rearrange("p (g j) t -> p g (j t)", j=JG)).then_inc(stored, 16)
                    sp.wait_ge(stored, 16)


def expert_layer(core, k, hT, g_dram, acc):
    nc, d, ps = core.nc, core.dram, k.ps
    VB = 6
    n_out = 2 * NXC
    with ExitStack() as ctx:
        sb = lambda n, s: ctx.enter_context(core.sbuf(n, s))
        u = sb("ex_u", [P, JG, KD, P])
        v = sb("ex_v", [P, JG, D])
        g = sb("ex_g", [P, N_TG, JG, TG])
        ab = sb("ex_ab", [P, 2, NX])
        A = sb("ex_A", [P, JG, NX])
        with core.stage("u_in*8", "v_in", "g_in", "h_done", "h_read", "ab_used", "a_ready", "v_done", "v_read", "clear") as (
                block, u_in, v_in, g_in, h_done, h_read, ab_used, a_ready, v_done, v_read, clear):
            @block.sync
            def _(sp):
                def load_u(jg, j):
                    sp.dma_start(u[:, j], d["peer_u"][jg, j]).then_inc(u_in[j], 16)

                def load_g(jg):
                    sp.dma_start(g[:].rearrange("p t j e -> p (t j e)"), g_dram[jg].rearrange("p t e -> p (t e)")).then_inc(g_in, 16)

                def load_v(jg):
                    sp.dma_start(v[:], d["peer_v"][jg]).then_inc(v_in, 16)
                load_u(0, 0)
                load_g(0)
                for j in range(1, JG):
                    load_u(0, j)
                load_v(0)
                with sp.Fori(1, N_JG) as jg:
                    for j in range(JG):
                        sp.wait_ge(h_done, jg * JG + (j + 1 - JG))
                        load_u(jg, j)
                    sp.wait_ge(ab_used, jg * JG)
                    load_g(jg)
                    sp.wait_ge(v_done, jg * n_out)
                    load_v(jg)

            @block.tensor
            def _(pe):
                def group(jg, first):
                    for j in range(JG):
                        pe.wait_ge(u_in[j], jg * 16 + 16)
                        if not (first and j < 2):
                            pe.wait_ge(h_read, jg * JG + (j - 1))
                        for kk in range(KD):
                            mm = pe.matmul(ps[:, j % 2, :], u[:, j, kk, :], hT[:, kk, NCTX:T], start=(kk == 0), stop=(kk == KD - 1))
                        mm.then_inc(h_done, 1)
                    pe.wait_ge(v_in, jg * 16 + 16)
                    for n in range(n_out):
                        if not (first and n < VB):
                            pe.wait_ge(v_read, jg * n_out + (n - VB + 1))
                        for j in range(JG):
                            if n == 0:
                                pe.wait_ge(a_ready, jg * JG + (j + 1))
                            mm = pe.matmul(ps[:, 2 + n % VB, :], A[:, j, P * (n // 2):P * (n // 2) + P],
                                           v[:, j, 512 * (n % 2):512 * (n % 2) + 512], start=(j == 0), stop=(j == JG - 1))
                        mm.then_inc(v_done, 1)
                group(0, True)
                with pe.Fori(1, N_JG) as jg:
                    group(jg, False)

            @block.scalar
            def _(act):
                def group(jg, first):
                    for j in range(JG):
                        act.wait_ge(h_done, jg * JG + (j + 1))
                        if not (first and j < 2):
                            act.wait_ge(ab_used, jg * JG + (j - 1))
                        act.activation(ab[:, j % 2, :], ps[:, j % 2, :], ACT.Gelu).then_inc(h_read, 1)
                group(0, True)
                with act.Fori(1, N_JG) as jg:
                    group(jg, False)

            @block.vector
            def _(dve):
                dve.memset(acc[:], 0.0).then_inc(clear, 1)
                dve.wait_ge(clear, 1)

                def group(jg, first):
                    dve.wait_ge(g_in, jg * 16 + 16)
                    for j in range(JG):
                        dve.wait_ge(h_read, jg * JG + (j + 1))
                        if not first and j == 0:
                            dve.wait_ge(v_done, jg * n_out)
                        dve.tensor_tensor(A[:, j, :].rearrange("p (t e) -> p t e", e=TG),
                                          ab[:, j % 2, :].rearrange("p (t e) -> p t e", e=TG), g[:, :, j, :],
                                          ALU.mult).then_inc(ab_used, 1)
                        dve.wait_ge(ab_used, jg * JG + (j + 1))
                        dve.sem_inc(a_ready, 1)
                    for n in range(n_out):
                        dve.wait_ge(v_done, jg * n_out + (n + 1))
                        if not first:
                            dve.wait_ge(v_read, jg * n_out + (n + 1 - n_out))
                        dve.tensor_tensor(acc[:, n // 2, n % 2, :], acc[:, n // 2, n % 2, :], ps[:, 2 + n % VB, :],
                                          ALU.add).then_inc(v_read, 1)
                group(0, True)
                with dve.Fori(1, N_JG) as jg:
                    group(jg, False)


def experts(core, k, hT, xs, cols, rows, tap):
    nc, d = core.nc, core.dram
    norm_transpose(core, k.ps, k.ident, k.eps, [(xs[:, t, :], NCTX + P * t, 0) for t in range(NXC)], True,
                   cols[:, 3 * KD:4 * KD, :], cols[:, 2 * KD:3 * KD, :], hT)
    tap("hT3", hT[:, :, NCTX:T])
    g_dram = nc.dram_tensor("gates_by_expert", (N_JG, P, N_TG, JG * TG), F32, kind="Internal").ap()
    with ExitStack() as ctx:
        sb = lambda n, s: ctx.enter_context(core.sbuf(n, s))
        iota = sb("iota", [P, P])
        chosen, chosenT = sb("chosen", [P, NXC, 3, P]), sb("chosenT", [P, 3, NX])
        load_all(core, [(iota[:], d["iota"].partition_broadcast(P))])
        with nc.Fori(0, PEER_HEADS) as head:
            route_head(core, k, hT, head, iota[:, 0:TOPK], chosen)
        tap("chosen", chosen[:])
        transposes(core, k, [([chosen[:, t, a, :] for t in range(NXC)], chosenT[:, a, :].rearrange("p (t e) -> p t e", t=NXC))
                             for a in range(3)])
        spread_gates(core, k, chosenT, iota[:], g_dram)
    with ExitStack() as ctx:
        acc = ctx.enter_context(core.sbuf("ex_acc", [P, NXC, 2, 512]))
        expert_layer(core, k, hT, g_dram, acc)
        tap("ffn", acc[:])
        with core.stage("steps") as (block, steps):
            @block.vector
            def _(dve):
                link = chain(dve, steps)
                for t in range(NXC):
                    link(dve.tensor_tensor(acc[:, t], acc[:, t], rows[:, 2:4, :], ALU.mult))
                    x = xs[:, t, :].rearrange("p (h c) -> p h c", h=2)
                    link(dve.scalar_tensor_tensor(out=x, in0=x, scalar=ALPHA, in1=acc[:, t], op0=ALU.mult, op1=ALU.add))


def head_block(core, k, hT, head, lower, norm_w, out):
    nc, d = core.nc, core.dram
    with ExitStack() as ctx:
        sb = lambda n, s: ctx.enter_context(core.sbuf(n, s))
        f = sb("hg_f", [P, 2, T])
        kT = sb("hg_k", [P, 2, T])
        v = sb("hg_v", [P, T])
        vt = sb("hg_vt", [P, NC, P])
        q, gate = sb("hg_q", [P, NX]), sb("hg_gate", [P, NX])
        scr = sb("hg_scr", [P, 2, NX])
        lb = sb("hg_lb", [P, 2, 2])
        project(core, k.ps, hT, d["w_in_hg"][head], [
            (0, ALL, f[:, 0, :]), (1, ALL, f[:, 1, :]), (2, ALL, v[:]), (3, X_ONLY, q[:]), (4, X_ONLY, gate[:])])
        gated(core, [(f[:, n, :], None, f[:, n, :], None, False) for n in range(2)]
              + [(q[:], None, q[:], scr[:, 0, :], True), (gate[:], None, gate[:], scr[:, 1, :], True)])
        with core.stage("dsteps", "f_ready", "done") as (block, dsteps, f_ready, done):
            @block.vector
            def _(dve):
                link = chain(dve, dsteps)
                link(dve.tensor_copy(lb[:, 0, :], lower[:, :, head]))
                link(dve.tensor_scalar(lb[:, 1, :], lb[:, 0, :], -1.0, 1.0, ALU.mult, ALU.add))
                for n in range(2):
                    link(dve.tensor_scalar(f[:, n, :], f[:, n, :], lb[:, 1, n:n + 1], lb[:, 0, n:n + 1], ALU.mult, ALU.add))
                    link(dve.tensor_scalar(kT[:, n, :], f[:, n, :], -1.0, 1.0, ALU.mult, ALU.add))
                    dve.tensor_scalar(f[:, n, :], f[:, n, :], 1e-19, None, ALU.max).then_inc(f_ready, 1)

            @block.scalar
            def _(act):
                for n in range(2):
                    act.wait_ge(f_ready, n + 1)
                    act.activation(f[:, n, :], f[:, n, :], ACT.Ln).then_inc(done, 1)
        transposes(core, k, [([v[:, P * c:P * c + P] for c in cs], vt[:, cs[0]:cs[-1] + 1, :])
                             for cs in (range(0, 4), range(4, 6))])
        key_gated_head(core, k, q[:], (kT[:, 0, :], kT[:, 1, :]), (f[:, 0, :], f[:, 1, :]), vt, gate[:], norm_w, out)


def ssd_group(core, k, hT, g, dt, loga, out):
    nc, d, ps = core.nc, core.dram, k.ps
    with ExitStack() as ctx:
        sb = lambda n, s: ctx.enter_context(core.sbuf(n, s))
        raw = sb("ma_raw", [P, 4, T])
        cv = sb("ma_cv", [P, 4, T])
        z = sb("ma_z", [P, 2, NX])
        cw, cb = sb("ma_cw", [P, 4, MA_TAPS]), sb("ma_cb", [P, 4])
        par = sb("ma_par", [P, 2, 2])
        col = sb("ma_col", [P, 2, NC, 2, MA_HPG])
        xtok = sb("ma_xtok", [P, NC, 2 * P])
        btok = sb("ma_btok", [P, NC, P])
        project(core, ps, hT, d["w_in_ma"][g], [
            (0, ALL, raw[:, 0, :]), (1, ALL, raw[:, 1, :]), (2, ALL, raw[:, 2, :]), (3, X_ONLY, raw[:, 3, NCTX:T]),
            (4, X_ONLY, z[:, 0, :]), (5, X_ONLY, z[:, 1, :])])
        with core.stage("loaded", "dsteps") as (block, loaded, dsteps):
            @block.sync
            def _(sp):
                sp.dma_start(cw[:], d["ma_conv_w"][g]).then_inc(loaded, 16)
                sp.dma_start(cb[:], d["ma_conv_b"][g]).then_inc(loaded, 16)
                sp.dma_start(par[:], d["ma_par"][g]).then_inc(loaded, 16)
                sp.wait_ge(loaded, 48)

            @block.vector
            def _(dve):
                link = chain(dve, dsteps)
                link(dve.tensor_copy(col[:, 0], dt[:, :, :, bass.ds(g * MA_HPG, MA_HPG)]))
                link(dve.tensor_copy(col[:, 1], loga[:, :, :, bass.ds(g * MA_HPG, MA_HPG)]))
                dve.wait_ge(loaded, 48)
                mid = MA_TAPS // 2
                for j in range(4):
                    for lo, n, step in (((0, NCTX, 1),) if j < 3 else ()) + ((NCTX, NX, GRID_W),):
                        src, dst = raw[:, j, lo:lo + n], cv[:, j, lo:lo + n]
                        link(dve.tensor_scalar(dst, src, cw[:, j, mid:mid + 1], cb[:, j:j + 1], ALU.mult, ALU.add))
                        for s in (-2, -1, 1, 2):
                            o0, o1 = max(0, -s * step), n - max(0, s * step)
                            link(dve.scalar_tensor_tensor(out=dst[:, o0:o1], in0=src[:, o0 + s * step:o1 + s * step],
                                                          scalar=cw[:, j, mid + s:mid + s + 1], in1=dst[:, o0:o1],
                                                          op0=ALU.mult, op1=ALU.add))
        by_col = lambda a: a.rearrange("p (r w) -> p w r", w=GRID_W)
        cols = lambda a: a.rearrange("p (w r) -> p w r", r=GRID_H)
        gated(core, [(cv[:, j, 0:NCTX], None, raw[:, j, 0:NCTX], raw[:, j, 0:NCTX], True) for j in range(3)]
              + [(by_col(cv[:, j, NCTX:T]), None, cols(raw[:, j, NCTX:T]), cols(raw[:, j, NCTX:T]), True) for j in range(4)]
              + [(z[:, e, :], None, z[:, e, :], cv[:, e, 0:NX], True) for e in range(0)])
        with core.stage("sig", "mul") as (block, sig, mul):
            @block.scalar
            def _(act):
                for e in range(2):
                    act.activation(cv[:, e, 0:NX], z[:, e, :], ACT.Sigmoid).then_inc(sig, 1)

            @block.vector
            def _(dve):
                for e in range(2):
                    dve.wait_ge(sig, e + 1)
                    dve.tensor_tensor(z[:, e, :], z[:, e, :], cv[:, e, 0:NX], ALU.mult).then_inc(mul, 1)
        transposes(core, k, [([raw[:, a, P * c:P * c + P] for c in cs], dst[:, cs[0]:cs[-1] + 1, s])
                             for a, dst, s in ((0, xtok, slice(0, P)), (1, xtok, slice(P, 2 * P)), (2, btok, slice(0, P)))
                             for cs in (range(0, 4), range(4, 6))])
        BT, CT = raw[:, 2, :], raw[:, 3, NCTX:T]
        lc = sb("ma_lc", [P, 2, NC, MA_HPG])
        ex = sb("ma_ex", [P, 2, NC, MA_HPG])
        xdt = sb("ma_xdt", [P, NC, 2 * P])
        xw = sb("ma_xw", [P, NC, 2 * P])
        cbm = sb("ma_cbm", [P, 2, NXC, P])
        L = sb("ma_L", [P, 2, MA_HPG, P])
        ce = sb("ma_ce", [P, 2, MA_HPG, P])
        H = sb("ma_H", [P, 2, NXC + 1, 2 * P])
        tmp = sb("ma_tmp", [P, 2 * P])
        y = sb("ma_y", [P, 2, NX])
        rs = sb("ma_rs", [P, NX])
        heads = lambda a: a.rearrange("p c (h e) -> p c h e", e=MA_P)
        over = lambda a: a.unsqueeze(3).to_broadcast([P, NC, MA_HPG, MA_P])
        with core.stage("cb_done", "sums_done", "lc_ready", "ex_ready", "xw_ready", "u_done", "dsteps", "H_ready",
                        "rows_done", "l_ready", "dec_ready", "ce_ready", "m_ready", "y_done", "cb_read", "lexp_ready", "u_read") as (
                block, cb_done, sums_done, lc_ready, ex_ready, xw_ready, u_done, dsteps, H_ready,
                rows_done, l_ready, dec_ready, ce_ready, m_ready, y_done, cb_read, lexp_ready, u_read):
            @block.tensor
            def _(pe):
                for c in range(NXC):
                    mm = pe.matmul(ps[:, 0, P * c:P * c + P], BT[:, NCTX + P * c:NCTX + P * c + P], CT[:, P * c:P * c + P],
                                   start=True, stop=True)
                mm.then_inc(cb_done, 1)
                for dr in range(2):
                    g_ = col[:, 1, :, dr, :]
                    if dr == 1:
                        pe.wait_ge(lc_ready, 1)
                    pe.matmul(ps[:, 1, 0:24].rearrange("p (c h) -> p c h", c=NC), k.incl[:, dr, :], g_, start=True, stop=True)
                    pe.matmul(ps[:, 1, 24:48].rearrange("p (c h) -> p c h", c=NC), k.ones[:], g_,
                              start=True, stop=True).then_inc(sums_done, 1)
                    pe.wait_ge(xw_ready, dr + 1)
                    for i, c in enumerate(ORDER[dr][:-1]):
                        n = 5 * dr + i
                        if n >= 2:
                            pe.wait_ge(u_read, n - 1)
                        pe.matmul(ps[:, 2 + n % 2, 0:2 * P], btok[:, c, :], xw[:, c, :], start=True, stop=True).then_inc(u_done, 1)
                    for c in range(NXC):
                        n = NXC * dr + c
                        if n >= 2:
                            pe.wait_ge(ce_ready, n - 1)
                            pe.wait_ge(l_ready, n - 1)
                        for j in range(MA_HPG):
                            mm = pe.matmul(ps[:, 4 + n % 2, P * j:P * j + P],
                                           col[:, 1, C0 + c, dr, j:j + 1].to_broadcast([P, P]), k.incl[:, dr, :],
                                           start=True, stop=True)
                        mm.then_inc(rows_done, 1)
                        pe.wait_ge(m_ready, n + 1)
                        slot = ORDER[dr][C0:].index(C0 + c)
                        for j in range(MA_HPG):
                            o = ps[MA_P * (j % 2):MA_P * (j % 2) + MA_P, 6 + j // 2, P * c:P * c + P]
                            hs = slice(MA_P * j, MA_P * j + MA_P)
                            pe.matmul(o, xdt[:, C0 + c, hs], L[:, n % 2, j, :], start=True, stop=False)
                            mm = pe.matmul(o, H[:, dr, slot, hs], ce[:, n % 2, j, :], start=False, stop=True)
                        mm.then_inc(y_done, 1)

            @block.vector
            def _(dve):
                link = chain(dve, dsteps)
                dve.wait_ge(cb_done, 1)
                for dr in range(2):
                    link(dve.tensor_tensor(cbm[:, dr], ps[:, 0, :].rearrange("p (c t) -> p c t", c=NXC),
                                           k.incl[:, dr, :].unsqueeze(1).to_broadcast([P, NXC, P]), ALU.mult))
                for dr in range(2):
                    dve.wait_ge(sums_done, dr + 1)
                    if dr == 1:
                        dve.wait_ge(y_done, NXC)
                        link(dve.tensor_copy(y[:], ps[:, 6:8, :]))
                    link(dve.tensor_copy(lc[:], ps[:, 1, 0:48].rearrange("p (a c h) -> p a c h", a=2, c=NC)))
                    dve.tensor_tensor(ex[:, 0], lc[:, 1], lc[:, 0], ALU.subtract).then_inc(lc_ready, 1)
                    link(dve.tensor_tensor(heads(xdt[:]), heads(xtok[:]), over(col[:, 0, :, dr, :]), ALU.mult))
                    dve.wait_ge(ex_ready, dr + 1)
                    dve.tensor_tensor(heads(xw[:]), heads(xdt[:]), over(ex[:, 0]), ALU.mult).then_inc(xw_ready, 1)
                    link(dve.memset(H[:, dr, 0, :], 0.0))
                    slot = 0
                    for i, c in enumerate(ORDER[dr][:-1]):
                        n = 5 * dr + i
                        nxt = slot if i < C0 else slot + 1
                        link(dve.tensor_tensor(tmp[:].rearrange("p (h e) -> p h e", e=MA_P),
                                               H[:, dr, slot, :].rearrange("p (h e) -> p h e", e=MA_P),
                                               ex[:, 1, c, :].unsqueeze(2).to_broadcast([P, MA_HPG, MA_P]), ALU.mult))
                        dve.wait_ge(u_done, n + 1)
                        dve.tensor_tensor(H[:, dr, nxt, :], tmp[:], ps[:, 2 + n % 2, 0:2 * P], ALU.add).then_inc(u_read, 1)
                        dve.wait_ge(u_read, n + 1)
                        slot = nxt
                    for c in range(NXC):
                        n = NXC * dr + c
                        dve.wait_ge(rows_done, n + 1)
                        if n >= 2:
                            dve.wait_ge(y_done, n - 1)
                        for j in range(MA_HPG):
                            ins = dve.tensor_scalar(L[:, n % 2, j, :], ps[:, 4 + n % 2, P * j:P * j + P],
                                                    lc[:, 0, C0 + c, j:j + 1], 0.0, ALU.subtract, ALU.min)
                        ins.then_inc(l_ready, 1)
                        dve.wait_ge(ce_ready, n + 1)
                        link(dve.tensor_tensor(ce[:, n % 2], ce[:, n % 2],
                                               CT[:, P * c:P * c + P].unsqueeze(1).to_broadcast([P, MA_HPG, P]), ALU.mult))
                        dve.wait_ge(lexp_ready, n + 1)
                        dve.tensor_tensor(L[:, n % 2], L[:, n % 2],
                                          cbm[:, dr, c, :].unsqueeze(1).to_broadcast([P, MA_HPG, P]), ALU.mult).then_inc(m_ready, 1)

            @block.scalar
            def _(act):
                for dr in range(2):
                    act.wait_ge(lc_ready, dr + 1)
                    act.activation(ex[:, 1], lc[:, 1], ACT.Exp)
                    act.activation(ex[:, 0], ex[:, 0], ACT.Exp).then_inc(ex_ready, 1)
                    for c in range(NXC):
                        n = NXC * dr + c
                        act.wait_ge(l_ready, n + 1)
                        if n >= 2:
                            act.wait_ge(y_done, n - 1)
                        act.activation(ce[:, n % 2], ps[:, 4 + n % 2, :].rearrange("p (h t) -> p h t", h=MA_HPG),
                                       ACT.Exp).then_inc(ce_ready, 1)
                        act.activation(L[:, n % 2], L[:, n % 2], ACT.Exp).then_inc(lexp_ready, 1)
        with core.stage("dsteps", "y_ready", "sq_ready", "ss_done", "rstd_ready", "asteps") as (
                block, dsteps, y_ready, sq_ready, ss_done, rstd_ready, asteps):
            @block.vector
            def _(dve):
                link = chain(dve, dsteps)
                link(dve.tensor_tensor(y[:], y[:], ps[:, 6:8, :], ALU.add))
                for e in range(2):
                    link(dve.scalar_tensor_tensor(out=y[:, e, :], in0=raw[:, e, NCTX:T], scalar=par[:, e, 0:1], in1=y[:, e, :],
                                                  op0=ALU.mult, op1=ALU.add))
                    rm = lambda a: a.rearrange("p (r w) -> p r w", w=GRID_W)
                    ins = dve.tensor_tensor(rm(z[:, e, :]), y[:, e, :].rearrange("p (w r) -> p r w", r=GRID_H), rm(z[:, e, :]),
                                            ALU.mult)
                ins.then_inc(y_ready, 1)
                dve.wait_ge(rstd_ready, 1)
                for e in range(2):
                    dve.scalar_tensor_tensor(out=out[:, e, :], in0=z[:, e, :], scalar=par[:, e, 1:2], in1=rs[:],
                                             op0=ALU.mult, op1=ALU.mult)

            @block.scalar
            def _(act):
                alink = chain(act, asteps)
                act.wait_ge(y_ready, 1)
                act.activation(cv[:, 0:2, 0:NX], z[:], ACT.Square).then_inc(sq_ready, 1)
                act.wait_ge(ss_done, 1)
                alink(act.activation(rs[:], ps[:, 0, :], ACT.Ln, bias=k.eps[:, 0:1], scale=1.0 / (2 * P)))
                act.activation(rs[:], rs[:], ACT.Exp, scale=-0.5).then_inc(rstd_ready, 1)

            @block.tensor
            def _(pe):
                pe.wait_ge(sq_ready, 1)
                for e in range(2):
                    mm = pe.matmul(ps[:, 0, :], k.ones[:], cv[:, e, 0:NX], start=(e == 0), stop=(e == 1))
                mm.then_inc(ss_done, 1)


def second_block(core, k, hT, xs, tap, upto):
    nc, d = core.nc, core.dram
    with ExitStack() as ctx:
        sbt = lambda n, s, dt=F32: ctx.enter_context(core.sbuf(n, s, dt))
        xt = [xs[:, t, :] for t in range(NXC)]
        cols = sbt("cols2", [P, 4 * KD, 2])
        rows = sbt("rows2", [P, 4, 512])
        with ExitStack() as ctx2:
            sb2 = lambda n, s: ctx2.enter_context(core.sbuf(n, s))
            cond = sb2("cond2", [P, KD, 2])
            b_cols, b_rows = sb2("b_cols2", [P, 4 * KD]), sb2("b_rows2", [P, 4, 512])
            ctx_rows = sb2("ctx_rows2", [P, C0, D])
            load_all(core, [(cond[:], d["cond_2"]), (b_cols[:], d["b_ada_cols"]), (b_rows[:], d["b_ada_rows"].partition_broadcast(P))]
                     + [(ctx_rows[:, t, :], d["ctx_2"][P * t:P * t + P, :]) for t in range(C0)])
            modulation(core, sbt, k.ps, cond, d["w_ada_cols"], 4 * KD, cols, b_cols, d["w_ada_rows"], 4, rows, b_rows)
            with core.stage("steps") as (block, steps):
                @block.vector
                def _(dve):
                    for a in (1, 3):
                        s = cols[:, KD * a:KD * a + KD, :]
                        dve.tensor_scalar(s, s, 1.0, None, ALU.add).then_inc(steps, 1)
            norm_transpose(core, k.ps, k.ident, k.eps,
                           [(ctx_rows[:, t, :], P * t, 1) for t in range(C0)]
                           + [(xs[:, t, :], NCTX + P * t, 0) for t in range(NXC)], True,
                           cols[:, KD:2 * KD, :], cols[:, 0:KD, :], hT)
        tap("hT2", hT[:])
        with ExitStack() as ctx2:
            sb2 = lambda n, s: ctx2.enter_context(core.sbuf(n, s))
            oT = sb2("oT", [P, HG_HEADS, NX])
            yzT = sb2("yzT", [P, 2 * MA_GROUPS, NX])
            with ExitStack() as ctx3:
                sb3 = lambda n, s: ctx3.enter_context(core.sbuf(n, s))
                lower = sb3("lower", [P, 2, HG_HEADS])
                lg = sb3("lower_logits", [P, 2, 2, HG_HEADS])
                top = sb3("lower_top", [P, 2, HG_HEADS])
                norm_w = sb3("hg_norm_w", [P, 1])
                load_all(core, [(lg[:], d["hg_lb"]), (norm_w[:], d["hg_norm_w"])])
                with core.stage("dsteps", "diff_ready", "exp_ready") as (block, dsteps, diff_ready, exp_ready):
                    @block.vector
                    def _(dve):
                        link = chain(dve, dsteps)
                        link(dve.tensor_tensor(top[:], lg[:, :, 0, :], lg[:, :, 1, :], ALU.max))
                        dve.tensor_tensor(lg[:], lg[:], top[:].unsqueeze(2).to_broadcast([P, 2, 2, HG_HEADS]),
                                          ALU.subtract).then_inc(diff_ready, 1)
                        dve.wait_ge(exp_ready, 1)
                        link(dve.tensor_tensor(top[:], lg[:, :, 0, :], lg[:, :, 1, :], ALU.add))
                        link(dve.reciprocal(top[:], top[:]))
                        link(dve.tensor_tensor(lower[:], lg[:, :, 0, :], top[:], ALU.mult))

                    @block.scalar
                    def _(act):
                        act.wait_ge(diff_ready, 1)
                        act.activation(lg[:], lg[:], ACT.Exp).then_inc(exp_ready, 1)
                with nc.Fori(0, HG_HEADS) as head:
                    head_block(core, k, hT, head, lower, norm_w[:, 0:1], oT[:, head, :])
            tap("oT", oT[:])
            with ExitStack() as ctx3:
                sb3 = lambda n, s: ctx3.enter_context(core.sbuf(n, s))
                dt, loga = sb3("ma_dt", [P, NC, 2, 32]), sb3("ma_loga", [P, NC, 2, 32])
                par = sb3("ma_rows", [P, 2, 2 * 32])
                with ExitStack() as ctx4:
                    sb4 = lambda n, s: ctx4.enter_context(core.sbuf(n, s))
                    dT, dT2 = sb4("dT", [64, T]), sb4("dT2", [64, T])
                    tmp = sb4("dt_tmp", [P, NC, 64])
                    load_all(core, [(par[:, 0, :], d["ma_dt_bias"].partition_broadcast(P)),
                                    (par[:, 1, :], d["ma_a_log"].partition_broadcast(P))])
                    project(core, k.ps, hT, d["w_in_dt"], [(0, ALL, dT[:])])
                    with core.stage("turned", "exp_ready") as (block, turned, exp_ready):
                        @block.vector
                        def _(dve):
                            dve.tensor_copy(dT2[:, 0:NCTX], dT[:, 0:NCTX]).then_inc(turned, 1)
                            dve.tensor_copy(dT2[:, NCTX:T].rearrange("p (w r) -> p w r", r=GRID_H),
                                            dT[:, NCTX:T].rearrange("p (r w) -> p w r", w=GRID_W)).then_inc(turned, 1)
                            dve.wait_ge(exp_ready, 1)
                            dve.tensor_scalar(par[:, 1, :], par[:, 1, :], -1.0, None, ALU.mult)

                        @block.scalar
                        def _(act):
                            act.activation(par[:, 1, :], par[:, 1, :], ACT.Exp).then_inc(exp_ready, 1)
                    flat = lambda a: a[:].rearrange("p c a h -> p c (a h)")
                    transposes(core, k, [([dT2[:, P * c:P * c + P] for c in cs], flat(dt)[:, cs[0]:cs[-1] + 1, :])
                                         for cs in (range(0, 4), range(4, 6))])
                    wide = lambda a: a.unsqueeze(1).to_broadcast([P, NC, 64])
                    log_sigmoids(core, k, [(flat(dt), wide(par[:, 0, :]), flat(dt), tmp[:], True,
                                            (flat(loga), wide(par[:, 1, :])))])
                with nc.Fori(0, MA_GROUPS) as g:
                    ssd_group(core, k, hT, g, dt, loga, yzT[:, bass.ds(2 * g, 2), :])
            tap("yzT", yzT[:])
            mT = sb2("mT2", [P, KD, NX])
            merge(core, k, hT, d["w_merge_2"], 8, 16, oT, yzT, None, mT)
            output_product(core, k, mT, d["w_out_2"], rows[:, 0:2, :], ALPHA, xt)
        with ExitStack() as ctx2:
            gb = ctx2.enter_context(core.sbuf("ln_gb", [P, 2, D]))
            load_all(core, [(gb[:, 0, :], d["ln1_g"].partition_broadcast(P)), (gb[:, 1, :], d["ln1_b"].partition_broadcast(P))])
            norm_rows(core, k, xt, True, gb[:, 0, :], gb[:, 1, :])
        tap("xln1", xs[:])
        if upto > 2:
            experts(core, k, hT, xs, cols, rows, tap)
            gb = sbt("ln2_gb", [P, 2, D])
            load_all(core, [(gb[:, 0, :], d["ln2_g"].partition_broadcast(P)), (gb[:, 1, :], d["ln2_b"].partition_broadcast(P))])
            norm_rows(core, k, xt, True, gb[:, 0, :], gb[:, 1, :])


def second_laid_out(a, d, col, rows_of, tiles, quads, wide_rows):
    import numpy as np
    d["cond_2"], d["ctx_2"] = np.stack([col(a["c_2"]), col(a["c_ctx_2"])], -1), a["ctx_2"]
    c_starts = [s + P * j for s in (0, D, 3 * D, 4 * D) for j in range(KD)]
    r_starts = [2 * D, 2 * D + 512, 5 * D, 5 * D + 512]
    d["w_ada_cols"], d["w_ada_rows"] = quads(a["w_ada_2"], c_starts), wide_rows(a["w_ada_2"], r_starts)
    d["b_ada_cols"] = np.stack([a["b_ada_2"][s:s + P] for s in c_starts], 1)
    d["b_ada_rows"] = np.stack([a["b_ada_2"][s:s + 512] for s in r_starts])
    d["hg_lb"] = a["hg_lb_logits_2"].reshape(2, 2, HG_HEADS, P).transpose(3, 0, 1, 2)
    d["hg_norm_w"] = col(a["hg_norm_w_2"])
    at = dict(zip(("f_f", "f_b", "iv", "xh", "b", "dt", "q", "og", "cm", "z", "ga", "gb"),
                  np.cumsum([0, D, D, D, 2 * D, D, 64, D, D, D, 2 * D, D]).tolist()))
    w = a["w_in_2"]
    d["w_in_hg"] = np.stack([tiles(w, [at[n] + P * h for n in ("f_f", "f_b", "iv", "q", "og")]) for h in range(HG_HEADS)])
    d["w_in_ma"] = np.stack([tiles(w, (at["xh"] + 2 * P * g, at["xh"] + 2 * P * g + P, at["b"] + P * g, at["cm"] + P * g,
                                       at["z"] + 2 * P * g, at["z"] + 2 * P * g + P)) for g in range(MA_GROUPS)])
    dtw = rows_of(w)[:, :, at["dt"]:at["dt"] + 64]
    d["w_in_dt"] = np.pad(dtw, ((0, 0), (0, 0), (0, 64))).transpose(1, 0, 2)[None]
    d["ma_dt_bias"], d["ma_a_log"] = a["ma_dt_bias_2"].reshape(-1), a["ma_a_log_2"].reshape(-1)
    chans = lambda g: [2 * P * g, 2 * P * g + P, 2 * D + P * g, 3 * D + P * g]
    d["ma_conv_w"] = np.stack([np.stack([a["ma_conv_w_2"][s:s + P] for s in chans(g)], 1) for g in range(MA_GROUPS)])
    d["ma_conv_b"] = np.stack([np.stack([a["ma_conv_b_2"][s:s + P] for s in chans(g)], 1) for g in range(MA_GROUPS)])
    md = np.repeat(a["ma_d_2"], MA_P)
    d["ma_par"] = np.stack([md.reshape(MA_GROUPS, 2, P), a["ma_norm_w_2"].reshape(MA_GROUPS, 2, P)], -1).transpose(0, 2, 1, 3)
    d["w_merge_2"] = np.concatenate([tiles(a["w_branch_a_2"], range(0, D, P)), tiles(a["w_branch_b_2"], range(0, D, P)),
                                     tiles(w, range(at["ga"], at["ga"] + D, P)), tiles(w, range(at["gb"], at["gb"] + D, P))], 2)
    d["w_out_2"], d["ln1_g"], d["ln1_b"], d["ln2_g"], d["ln2_b"] = (
        a["w_out_2"], a["ln1_g_2"], a["ln1_b_2"], a["ln2_g_2"], a["ln2_b_2"])
    d["w_q"] = np.stack([tiles(a["peer_wq_2"], (2 * P * h, 2 * P * h + P)) for h in range(PEER_HEADS)])
    d["subkeys"] = a["peer_subkeys_2"].transpose(0, 3, 1, 2)
    d["iota"] = np.arange(P, dtype=np.float32)
    d["peer_u"] = a["peer_u_2"].reshape(P, N_JG, JG, KD, P).transpose(1, 2, 4, 3, 0)
    d["peer_v"] = a["peer_v_2"].reshape(P, N_JG, JG, D).transpose(1, 0, 2, 3)


def laid_out(i):
    import numpy as np
    a = {n: np.asarray(v) for n, v in i.items()}
    for n in list(a):
        if n in ("w_mod", "b_mod", "norm_g", "w_in", "gla_up", "gla_ub", "gla_onorm", "gdn_conv", "gdn_a_log", "gdn_dt_bias",
                 "gdn_onorm", "w_gla_out", "w_gdn_out", "b_gate", "w_o", "w_ada_2", "b_ada_2", "w_in_2", "hg_norm_w_2",
                 "ma_conv_w_2", "ma_conv_b_2", "ma_dt_bias_2", "ma_a_log_2", "ma_d_2", "ma_norm_w_2", "w_branch_a_2",
                 "w_branch_b_2", "w_out_2", "ln1_g_2", "ln1_b_2", "peer_wq_2", "peer_subkeys_2", "peer_u_2", "peer_v_2",
                 "ln2_g_2", "ln2_b_2", "x", "ctx", "ctx_2", "c", "c_2"):
            a[n] = a[n][0]
    tri = np.tril(np.ones((P, P), np.float32))
    t = np.arange(P)
    level = np.zeros((2, LEVELS + 1, P, P), np.float32)
    level[:, 0] = np.eye(P)
    for i_ in range(1, LEVELS + 1):
        size = 1 << (i_ - 1)
        same = (t[:, None] // (2 * size)) == (t[None, :] // (2 * size))
        first, second = (t // size) % 2 == 0, (t // size) % 2 == 1
        level[0, i_] = same & first[:, None] & second[None, :]
        level[1, i_] = same & second[:, None] & first[None, :]
    restart = np.ones((2, T), np.float32)
    restart[0, 0::P] = 0
    restart[1, P - 1::P] = 0
    d = {
        "ident": np.eye(P, dtype=np.float32), "ones": np.ones((P, P), np.float32),
        "incl": np.stack([tri.T, tri], 1),
        "levelf": level.transpose(2, 0, 1, 3), "level": level.transpose(2, 0, 1, 3).astype(np.uint32),
        "restart": np.broadcast_to(restart, (P, 2, T)),
    }
    col = lambda v: v.reshape(-1, P).T
    rows_of = lambda w: w.reshape(-1, P, w.shape[-1])

    def tiles(w, starts):
        r = rows_of(w)
        return np.stack([r[:, :, s:s + P].transpose(1, 0, 2) for s in starts])

    def quads(w, starts):
        return tiles(w, starts).reshape(len(starts) // 4, 4, P, KD, P).transpose(0, 2, 1, 3, 4).reshape(len(starts) // 4, P, -1)

    def wide_rows(w, starts):
        r = rows_of(w)
        return np.stack([r[:, :, s:s + 512].transpose(1, 0, 2).reshape(P, -1) for s in starts])

    d["x"], d["ctx"], d["cond"] = a["x"], a["ctx"], np.stack([col(a["c"]), col(a["c_ctx"])], -1)
    d["w_mod_cols"] = quads(a["w_mod"], range(0, 2 * D, P))
    d["w_mod_rows"] = wide_rows(a["w_mod"], (2 * D, 2 * D + 512))
    d["b_mod_cols"], d["b_mod_rows"] = col(a["b_mod"][:2 * D]), a["b_mod"][2 * D:].reshape(2, 512)
    d["norm_g"], d["gla_onorm"], d["gdn_onorm"], d["b_gate"] = (
        col(a["norm_g"]), col(a["gla_onorm"]), col(a["gdn_onorm"]), col(a["b_gate"]))
    d["gdn_a_log"], d["gdn_dt_bias"], d["final_g"] = a["gdn_a_log"].reshape(-1), a["gdn_dt_bias"].reshape(-1), a["final_g"]
    at = dict(zip(("aq", "ak", "av", "ag", "alr", "bq", "bk", "bv", "bg", "bbeta", "bdec", "mg"),
                  np.cumsum([0, 256, 256, 512, 512, 32, 512, 512, 512, 512, 8, 8]).tolist()))
    w = a["w_in"]
    d["w_in_gla"] = np.stack([tiles(w, (at["aq"] + P * p, at["ak"] + P * p, at["av"] + 2 * P * p, at["av"] + 2 * P * p + P,
                                        at["ag"] + 2 * P * p, at["ag"] + 2 * P * p + P)) for p in range(2)])
    d["w_in_gdn"] = np.stack([tiles(w, (at["bq"] + P * h, at["bk"] + P * h, at["bv"] + P * h, at["bg"] + P * h))
                              for h in range(GDN_HEADS)])
    r = rows_of(w)
    small = np.concatenate([r[:, :, at["alr"]:at["alr"] + 32], r[:, :, at["bbeta"]:at["bbeta"] + 16]], -1)
    d["w_in_small"] = np.pad(small, ((0, 0), (0, 0), (0, P - 48))).transpose(1, 0, 2)[None]
    d["gla_up"] = a["gla_up"].reshape(2, GLA_RANK, 2, P).transpose(2, 0, 1, 3)
    d["gla_ub"] = a["gla_ub"].reshape(2, 2, P).transpose(1, 2, 0)
    d["gdn_conv"] = a["gdn_conv"].reshape(9, 3, GDN_HEADS, P).transpose(2, 3, 1, 0)
    ta, tb = tiles(a["w_gla_out"], range(0, D, P)), tiles(a["w_gdn_out"], range(0, D, P))
    d["w_merge"] = np.concatenate([ta, tb, tiles(w, range(at["mg"], at["mg"] + D, P)),
                                   tiles(w, range(at["mg"] + D, at["mg"] + 2 * D, P))], 2)
    d["w_o"] = a["w_o"]
    second_laid_out(a, d, col, rows_of, tiles, quads, wide_rows)
    return {n: np.ascontiguousarray(v) for n, v in d.items()}


def kernel(**inputs):
    import numpy as _np
    import concourse.bacc as _bacc
    from concourse import mybir as _mybir
    from concourse.bass_utils import run_bass_kernel_spmd as _run

    arrays = laid_out(inputs)
    nc = _bacc.Bacc("TRN2", target_bir_lowering=False, num_devices=1)
    dram = {n: nc.dram_tensor(f"in_{n}", v.shape, _mybir.dt.from_np(v.dtype), kind="ExternalInput").ap()
            for n, v in arrays.items()}
    out = nc.dram_tensor("out", (NX, D), F32, kind="ExternalOutput").ap()
    program(nc, dram, out)
    r = _run(nc, [{f"in_{n}": v for n, v in arrays.items()}], core_ids=[0])
    return _np.asarray(r.results[0]["out"]).reshape(1, NX, D)
```

```python
from contextlib import ExitStack, contextmanager

import concourse.bass as bass
from concourse import mybir

P = 128
D = 1024
KD = D // P
NCTX, NX = 256, 512
T = NCTX + NX
NC = T // P
C0 = NCTX // P
NXC = NX // P
GRID_W = 64
GRID_H = NX // GRID_W
LEVELS = 7
EPS = 1e-6

F32 = mybir.dt.float32
F32R = mybir.dt.float32r
U32 = mybir.dt.uint32
ALU = mybir.AluOpType
ACT = mybir.ActivationFunctionType
AX = mybir.AxisListType

GLA_HEADS, GLA_RANK, GLA_TAU = 4, 16, 16.0
GDN_HEADS = 4
HG_HEADS = 8
MA_GROUPS, MA_HPG, MA_P = 8, 4, 64
MA_TAPS = 5
PEER_HEADS, PEER_KEYS, TOPK = 8, 128, 16
ALPHA = 2.0 ** 0.25

ORDER = (tuple(range(NC)), tuple(range(C0 - 1, -1, -1)) + tuple(range(NC - 1, C0 - 1, -1)))
LAST = (P - 1, 0)


class Core:

    def __init__(self, nc, ctx, dram):
        self.nc, self.ctx, self.dram, self.made = nc, ctx, dram, 0
        self.pool = [ctx.enter_context(nc.semaphore(f"stage_signal_{i}")) for i in range(40)]

    def sbuf(self, name, shape, dtype=F32):
        self.made += 1
        return self.nc.sbuf_tensor(f"{name}_{self.made}", shape, dtype)

    @contextmanager
    def stage(self, *names):
        free, given = iter(self.pool), []
        for name in names:
            given.append([next(free) for _ in range(int(name.split("*")[1]))] if "*" in name else next(free))
        with self.nc.Block() as block:
            yield (block, *given)
        sems = [s for g in given for s in (g if isinstance(g, list) else [g])]
        with self.nc.Block() as block:
            @block.sync
            def _(sp):
                for s in sems:
                    sp.sem_clear(s)


def chain(engine, sem):
    count = [0]

    def link(ins):
        count[0] += 1
        ins.then_inc(sem, 1)
        engine.wait_ge(sem, count[0])
    return link


def load_all(core, pairs):
    with core.stage("loaded") as (block, loaded):
        @block.sync
        def _(sp):
            for dst, src in pairs:
                sp.dma_start(dst, src).then_inc(loaded, 16)
            sp.wait_ge(loaded, 16 * len(pairs))


def modulation(core, sb, ps, conds, w_cols, n_cols, cols, b_cols, w_rows, n_rows, rows, b_rows):
    nc = core.nc
    RING = 4
    with ExitStack() as ctx:
        w = ctx.enter_context(core.sbuf("mod_w", [P, RING, KD * 512], F32))
        e = ctx.enter_context(core.sbuf("mod_e", [P, KD, 2], F32))
        with core.stage("loaded", "steps", "silu_ready", "w_in*4", "pe_done", "evicted") as (
                block, loaded, steps, silu_ready, w_in, pe_done, evicted):
            quads = n_cols // 4

            @block.sync
            def _(sp):
                for n in range(quads + n_rows):
                    if n >= RING:
                        sp.wait_ge(pe_done, n - RING + 1)
                    src = w_cols[n] if n < quads else w_rows[n - quads]
                    sp.dma_start(w[:, n % RING, :], src).then_inc(w_in[n % RING], 16)

            @block.scalar
            def _(act):
                act.activation(e[:], conds[:], ACT.Sigmoid).then_inc(steps, 1)

            @block.vector
            def _(dve):
                dve.wait_ge(steps, 1)
                dve.tensor_tensor(conds[:], conds[:], e[:], ALU.mult).then_inc(silu_ready, 1)
                for n in range(quads):
                    dve.wait_ge(pe_done, n + 1)
                    dve.tensor_tensor(cols[:, 4 * n:4 * n + 4, :], ps[:, n % 2, 0:8].rearrange("p (a b) -> p a b", a=4),
                                      b_cols[:, 4 * n:4 * n + 4].unsqueeze(2).to_broadcast([P, 4, 2]),
                                      ALU.add).then_inc(evicted, 1)
                for m in range(n_rows):
                    n = quads + m
                    dve.wait_ge(pe_done, n + 1)
                    dve.tensor_tensor(rows[:, m, :], ps[:, n % 2, :], b_rows[:, m, :], ALU.add).then_inc(evicted, 1)

            @block.tensor
            def _(pe):
                pe.wait_ge(silu_ready, 1)
                for n in range(quads + n_rows):
                    pe.wait_ge(w_in[n % RING], 16 * (n // RING + 1))
                    if n >= 2:
                        pe.wait_ge(evicted, n - 1)
                    if n < quads:
                        wt = w[:, n % RING, :].rearrange("p (a k c) -> p a k c", a=4, k=KD)
                        for a in range(4):
                            for k in range(KD):
                                mm = pe.matmul(ps[:, n % 2, 2 * a:2 * a + 2], wt[:, a, k, :], conds[:, k, :],
                                               start=(k == 0), stop=(k == KD - 1))
                    else:
                        wt = w[:, n % RING, :].rearrange("p (k c) -> p k c", k=KD)
                        for k in range(KD):
                            mm = pe.matmul(ps[:, n % 2, :], conds[:, k, 0:1].to_broadcast([P, P]), wt[:, k, :],
                                           start=(k == 0), stop=(k == KD - 1))
                    mm.then_inc(pe_done, 1)


def norm_transpose(core, ps, ident, eps, tiles, centre, scale, shift, hT):
    nc = core.nc
    with ExitStack() as ctx:
        sb = lambda n, s: ctx.enter_context(core.sbuf(n, s, F32))
        xn = sb("nt_xn", [P, 2, D])
        sq = sb("nt_sq", [P, D])
        st = sb("nt_st", [P, len(tiles), 4])
        with core.stage("steps", "sum_ready", "var_ready", "rstd_ready", "xn_ready", "pe_done", "evicted", "asteps") as (
                block, steps, sum_ready, var_ready, rstd_ready, xn_ready, pe_done, evicted, asteps):
            @block.vector
            def _(dve):
                link = chain(dve, steps)

                def centred(i):
                    src, s = tiles[i][0], st[:, i, :]
                    if centre:
                        link(dve.tensor_reduce(s[:, 0:1], src, AX.X, ALU.add))
                        link(dve.tensor_scalar(s[:, 1:2], s[:, 0:1], -1.0 / D, None, ALU.mult))
                    else:
                        link(dve.memset(s[:, 1:2], 0.0))
                    if i >= 2:
                        dve.wait_ge(pe_done, 2 * (i - 1))
                    dve.tensor_scalar(xn[:, i % 2, :], src, s[:, 1:2], None, ALU.add).then_inc(sum_ready, 1)

                def scaled(i):
                    dve.wait_ge(rstd_ready, i + 1)
                    dve.tensor_scalar(xn[:, i % 2, :], xn[:, i % 2, :], st[:, i, 3:4], None, ALU.mult).then_inc(xn_ready, 1)

                def modulated(i):
                    _, col, who = tiles[i]
                    for half in range(2):
                        dve.wait_ge(pe_done, 2 * i + half + 1)
                        for j in range(4):
                            k = 4 * half + j
                            ins = dve.tensor_scalar(hT[:, k, col:col + P], ps[:, half, P * j:P * j + P],
                                                    scale[:, k, who:who + 1], shift[:, k, who:who + 1], ALU.mult, ALU.add)
                        ins.then_inc(evicted, 1)

                centred(0)
                for i in range(len(tiles)):
                    scaled(i)
                    if i > 0:
                        modulated(i - 1)
                    if i + 1 < len(tiles):
                        centred(i + 1)
                modulated(len(tiles) - 1)

            @block.scalar
            def _(act):
                alink = chain(act, asteps)
                for i in range(len(tiles)):
                    s = st[:, i, :]
                    act.wait_ge(sum_ready, i + 1)
                    alink(act.activation(sq[:], xn[:, i % 2, :], ACT.Square, accum_out=s[:, 2:3]))
                    alink(act.activation(s[:, 3:4], s[:, 2:3], ACT.Ln, bias=eps[:, 0:1], scale=1.0 / D))
                    act.activation(s[:, 3:4], s[:, 3:4], ACT.Exp, scale=-0.5).then_inc(rstd_ready, 1)

            @block.tensor
            def _(pe):
                for i in range(len(tiles)):
                    pe.wait_ge(xn_ready, i + 1)
                    for half in range(2):
                        if i > 0:
                            pe.wait_ge(evicted, 2 * (i - 1) + half + 1)
                        for j in range(4):
                            k = 4 * half + j
                            ins = pe.transpose(ps[:, half, P * j:P * j + P], xn[:, i % 2, P * k:P * k + P], ident[:])
                        ins.then_inc(pe_done, 1)


X_ONLY, ALL, X_AT_0 = "grid tokens", "all tokens", "grid tokens alone"


def product3(pe, out, a, b, start, stop):
    pe.matmul(out, a[1], b[0], start=start, stop=False)
    pe.matmul(out, a[0], b[1], start=False, stop=False)
    return pe.matmul(out, a[0], b[0], start=False, stop=stop)


def split(core, src, high, low):
    with core.stage("high_ready", "done") as (block, high_ready, done):
        n = src.shape[1]

        @block.scalar
        def _(act):
            for j in range(n):
                act.copy(high[:, j], src[:, j]).then_inc(high_ready, 1)

        @block.vector
        def _(dve):
            for j in range(n):
                dve.wait_ge(high_ready, j + 1)
                dve.tensor_tensor(low[:, j], src[:, j], high[:, j].bitcast(F32), ALU.subtract).then_inc(done, 1)


def project(core, ps, hT, w_dram, tiles, small=(), follow=None, gates=None):
    nc = core.nc
    with ExitStack() as ctx:
        w = ctx.enter_context(core.sbuf("proj_w", [P, 2, KD * P], F32))
        wh = ctx.enter_context(core.sbuf("proj_wh", [P, 2, KD * P], F32R))
        wl = ctx.enter_context(core.sbuf("proj_wl", [P, 2, KD * P], F32R))
        with core.stage("w_in*2", "high_ready", "low_ready", "pe_done", "evicted", "loaded", "steps", "sig_ready", "gated_done") as (
                block, w_in, high_ready, low_ready, pe_done, evicted, loaded, steps, sig_ready, gated_done):
            @block.sync
            def _(sp):
                for n, (row, _, _) in enumerate(tiles):
                    if n >= 2:
                        sp.wait_ge(low_ready, n - 1)
                    sp.dma_start(w[:, n % 2, :], w_dram[row].rearrange("p k c -> p (k c)")).then_inc(w_in[n % 2], 16)
                    if n == 0:
                        for dst, src in small:
                            sp.dma_start(dst, src).then_inc(loaded, 16)

            @block.gpsimd
            def _(pool):
                for n in range(len(tiles)):
                    pool.wait_ge(high_ready, n + 1)
                    pool.tensor_tensor(wl[:, n % 2, :], w[:, n % 2, :], wh[:, n % 2, :].bitcast(F32),
                                       ALU.subtract).then_inc(low_ready, 1)

            @block.tensor
            def _(pe):
                for n, (_, tokens, dst) in enumerate(tiles):
                    pe.wait_ge(low_ready, n + 1)
                    if n >= 2:
                        pe.wait_ge(evicted, n - 1)
                    parts = [(0, 384), (384, 384)] if tokens is ALL else [(NCTX if tokens is X_ONLY else 0, NX)]
                    for b, (t0, nt) in enumerate(parts):
                        for k in range(KD):
                            c = slice(P * k, P * k + P)
                            mm = product3(pe, ps[:, 2 * (n % 2) + b, 0:nt], (wh[:, n % 2, c], wl[:, n % 2, c]),
                                          (hT[0][:, k, t0:t0 + nt], hT[1][:, k, t0:t0 + nt]), k == 0, k == KD - 1)
                    mm.then_inc(pe_done, 1)

            @block.scalar
            def _(act):
                def high(n):
                    act.wait_ge(w_in[n % 2], 16 * (n // 2 + 1))
                    if n >= 2:
                        act.wait_ge(pe_done, n - 1)
                    act.copy(wh[:, n % 2, :], w[:, n % 2, :]).then_inc(high_ready, 1)
                high(0)
                for n, (_, tokens, dst) in enumerate(tiles):
                    if n + 1 < len(tiles):
                        high(n + 1)
                    act.wait_ge(pe_done, n + 1)
                    M, b = dst.shape[0], 2 * (n % 2)
                    if tokens is ALL:
                        act.copy(dst.rearrange("p (b t) -> p b t", b=2), ps[0:M, b:b + 2, 0:384]).then_inc(evicted, 1)
                    else:
                        act.copy(dst, ps[0:M, b, :]).then_inc(evicted, 1)
                    if gates is not None and n in gates:
                        act.wait_ge(evicted, n + 1)
                        act.activation(dst if gates[n] is None else gates[n], dst, ACT.Sigmoid).then_inc(sig_ready, 1)

            @block.vector
            def _(dve):
                if follow is not None:
                    follow(dve, evicted, loaded, steps)
                for i, n in enumerate(sorted(gates or ())):
                    if gates[n] is not None:
                        dve.wait_ge(sig_ready, i + 1)
                        dve.tensor_tensor(tiles[n][2], tiles[n][2], gates[n], ALU.mult).then_inc(gated_done, 1)


def halves(ap, size):
    return ap.rearrange("p (n h l) -> p n h l", h=2, l=size)


def key_gated_head(core, k, qT, kT, gT, v, gate, norm_w, out):
    nc = core.nc
    ps = k.ps
    with ExitStack() as ctx:
        sb = lambda n, s: ctx.enter_context(core.sbuf(n, s, F32))
        cums = sb("kg_cum", [P, 2, T])
        dec = sb("kg_dec", [P, 2, NX])
        mix = sb("kg_mix", [P, 2, NX])
        att = sb("kg_att", [P, 2, NXC, P])
        qe = sb("kg_qe", [P, 2, NX])
        kds = sb("kg_kd", [P, 2, T])
        ktok = sb("kg_ktok", [P, NC, P])
        ebl = sb("kg_ebl", [P, 2, NC])
        S = sb("kg_S", [P, 2, NXC + 1, P])
        scr = sb("kg_scr", [P, 2, NX])
        n_lv = LEVELS + 1
        with core.stage("dve_steps", "act_steps", "diff_ready", "dec_ready", "mix_ready", "att_done", "att_read",
                        "kd_ready", "kt_done", "kt_read", "u_done", "S_ready", "o_done", "sq_ready", "ss_done",
                        "rstd_ready", "cum_ready", "ce_ready", "wdiff_ready") as (
                block, dve_steps, act_steps, diff_ready, dec_ready, mix_ready, att_done, att_read, kd_ready, kt_done,
                kt_read, u_done, S_ready, o_done, sq_ready, ss_done, rstd_ready, cum_ready, ce_ready, wdiff_ready):
            @block.vector
            def _(dve):
                link = chain(dve, dve_steps)
                dve.tensor_tensor_scan(cums[:, 0], k.restart[:, 0, :], gT[0], 0.0, ALU.mult, ALU.add).then_inc(cum_ready, 1)
                dve.tensor_tensor_scan(cums[:, 1, ::-1], k.restart[:, 1, ::-1], gT[1][:, ::-1], 0.0,
                                       ALU.mult, ALU.add).then_inc(cum_ready, 1)
                for d in range(2):
                    dve.wait_ge(cum_ready, d + 1)
                    c3 = cums[:, d].rearrange("p (c t) -> p c t", c=NC)
                    dve.tensor_tensor(kds[:, d].rearrange("p (c t) -> p c t", c=NC),
                                      c3[:, :, LAST[d]:LAST[d] + 1].to_broadcast([P, NC, P]), c3, ALU.subtract).then_inc(wdiff_ready, 1)
                link(dve.memset(att[:], 0.0))
                link(dve.memset(S[:, :, 0, :], 0.0))
                for d in range(2):
                    dve.wait_ge(ce_ready, 3 * d + 3)
                    dve.tensor_tensor(kds[:, d], kds[:, d], kT[d], ALU.mult).then_inc(kd_ready, 1)
                    link(dve.tensor_tensor(qe[:, d, :], qe[:, d, :], qT, ALU.mult))
                for d in range(2):
                    for lv in range(1, n_lv):
                        n = d * n_lv + lv
                        size = 1 << (lv - 1)
                        dv, mv = halves(dec[:, (d * LEVELS + lv) % 2, :], size), halves(mix[:, n % 2, :], size)
                        dve.wait_ge(dec_ready, d * LEVELS + lv)
                        if n >= 2:
                            dve.wait_ge(att_done, n - 1)
                        dve.tensor_tensor(mv[:, :, d, :], dv[:, :, d, :], halves(kT[d][:, NCTX:T], size)[:, :, d, :], ALU.mult)
                        dve.tensor_tensor(mv[:, :, 1 - d, :], dv[:, :, 1 - d, :], halves(qT, size)[:, :, 1 - d, :],
                                          ALU.mult).then_inc(mix_ready, 1)
                        m = n - 1
                        dve.wait_ge(att_done, m + 1)
                        dve.copy_predicated(att[:, d, :, :],
                                            k.level[:, d, lv - 1, :].unsqueeze(1).to_broadcast([P, NXC, P]),
                                            ps[:, m % 2, :].rearrange("p (c t) -> p c t", c=NXC)).then_inc(att_read, 1)
                        dve.wait_ge(att_read, m + 1)
                    m = (d + 1) * n_lv - 1
                    dve.wait_ge(att_done, m + 1)
                    dve.copy_predicated(att[:, d, :, :], k.level[:, d, LEVELS, :].unsqueeze(1).to_broadcast([P, NXC, P]),
                                        ps[:, m % 2, :].rearrange("p (c t) -> p c t", c=NXC)).then_inc(att_read, 1)
                    dve.wait_ge(u_done, d + 1)
                    U = lambda c: ps[:, 4 + c // 4, P * (c % 4):P * (c % 4) + P]
                    slot = 0
                    for i, c in enumerate(ORDER[d][:-1]):
                        nxt = slot if i < C0 else slot + 1
                        ins = dve.scalar_tensor_tensor(out=S[:, d, nxt, :], in0=S[:, d, slot, :], scalar=ebl[:, d, c:c + 1],
                                                       in1=U(c), op0=ALU.mult, op1=ALU.add)
                        link(ins)
                        slot = nxt
                    dve.sem_inc(S_ready, 1)
                dve.wait_ge(rstd_ready, 1)
                link(dve.tensor_tensor(scr[:, 0, :], ps[:, 6, :], scr[:, 1, :], ALU.mult))
                link(dve.scalar_tensor_tensor(out=out, in0=scr[:, 0, :], scalar=norm_w, in1=gate,
                                              op0=ALU.mult, op1=ALU.mult))

            @block.gpsimd
            def _(pool):
                for d in range(2):
                    pool.wait_ge(cum_ready, d + 1)
                    for lv in range(1, n_lv):
                        i = d * LEVELS + lv
                        if i > 2:
                            pool.wait_ge(mix_ready, i - 2)
                        size = 1 << (lv - 1)
                        shape = [P, NX // (2 * size), size]
                        cv, dv = halves(cums[:, d, NCTX:T], size), halves(dec[:, i % 2, :], size)
                        ref = cv[:, :, d, size - 1 if d == 0 else 0].unsqueeze(2).to_broadcast(shape)
                        pool.tensor_tensor(dv[:, :, d, :], ref, cv[:, :, d, :], ALU.subtract)
                        pool.tensor_tensor(dv[:, :, 1 - d, :], cv[:, :, 1 - d, :], ref, ALU.subtract).then_inc(diff_ready, 1)

            @block.scalar
            def _(act):
                alink = chain(act, act_steps)
                for d in range(2):
                    act.wait_ge(cum_ready, d + 1)
                    c3 = cums[:, d].rearrange("p (c t) -> p c t", c=NC)
                    act.activation(ebl[:, d], c3[:, :, LAST[d]], ACT.Exp).then_inc(ce_ready, 1)
                    act.activation(qe[:, d, :], cums[:, d, NCTX:T], ACT.Exp).then_inc(ce_ready, 1)
                    act.wait_ge(wdiff_ready, d + 1)
                    act.activation(kds[:, d], kds[:, d], ACT.Exp).then_inc(ce_ready, 1)
                for d in range(2):
                    if d == 1:
                        act.wait_ge(u_done, 1)
                    for lv in range(1, n_lv):
                        act.wait_ge(diff_ready, d * LEVELS + lv)
                        b = (d * LEVELS + lv) % 2
                        act.activation(dec[:, b, :], dec[:, b, :], ACT.Exp).then_inc(dec_ready, 1)
                        if lv == 1:
                            act.wait_ge(kt_done, 2 * d + 1)
                            act.copy(ktok[:, 0:4, :], ps[:, 2, :].rearrange("p (c t) -> p c t", c=4)).then_inc(kt_read, 1)
                            act.wait_ge(kt_done, 2 * d + 2)
                            act.copy(ktok[:, 4:6, :], ps[:, 3, 0:2 * P].rearrange("p (c t) -> p c t", c=2)).then_inc(kt_read, 1)
                act.wait_ge(o_done, 1)
                act.activation(scr[:, 0, :], ps[:, 6, :], ACT.Square).then_inc(sq_ready, 1)
                act.wait_ge(ss_done, 1)
                alink(act.activation(scr[:, 1, :], ps[:, 7, :], ACT.Ln, bias=k.eps[:, 0:1], scale=1.0 / P))
                act.activation(scr[:, 1, :], scr[:, 1, :], ACT.Exp, scale=-0.5).then_inc(rstd_ready, 1)

            @block.tensor
            def _(pe):
                for d in range(2):
                    pe.wait_ge(kd_ready, d + 1)
                    for c in range(NC):
                        mm = pe.transpose(ps[:, 2 + c // 4, P * (c % 4):P * (c % 4) + P], kds[:, d, P * c:P * c + P], k.ident[:])
                        if c in (3, NC - 1):
                            mm.then_inc(kt_done, 1)
                    for lv in range(n_lv):
                        n = d * n_lv + lv
                        if n >= 2:
                            pe.wait_ge(att_read, n - 1)
                        if lv > 0:
                            pe.wait_ge(mix_ready, d * LEVELS + lv)
                        for c in range(NXC):
                            t0 = P * c
                            if lv == 0:
                                mm = pe.matmul(ps[:, n % 2, t0:t0 + P], kT[d][:, NCTX + t0:NCTX + t0 + P],
                                               qT[:, t0:t0 + P], start=True, stop=True)
                            else:
                                mm = pe.matmul(ps[:, n % 2, t0:t0 + P], mix[:, n % 2, t0:t0 + P],
                                               mix[:, n % 2, t0:t0 + P], start=True, stop=True)
                        mm.then_inc(att_done, 1)
                        if lv == 2:
                            pe.wait_ge(kt_read, 2 * d + 2)
                            if d == 1:
                                pe.wait_ge(S_ready, 1)
                            for c in ORDER[d][:-1]:
                                mm = pe.matmul(ps[:, 4 + c // 4, P * (c % 4):P * (c % 4) + P], ktok[:, c, :], v[:, c, :],
                                               start=True, stop=True)
                            mm.then_inc(u_done, 1)
                pe.wait_ge(att_read, 2 * n_lv)
                pe.wait_ge(S_ready, 2)
                for c in range(NXC):
                    o = ps[:, 6, P * c:P * c + P]
                    for d in range(2):
                        slot = ORDER[d][C0:].index(C0 + c)
                        pe.matmul(o, v[:, C0 + c, :], att[:, d, c, :], start=(d == 0), stop=False)
                        mm = pe.matmul(o, S[:, d, slot, :], qe[:, d, P * c:P * c + P], start=False, stop=(d == 1))
                mm.then_inc(o_done, 1)
                pe.wait_ge(sq_ready, 1)
                pe.matmul(ps[:, 7, :], k.ones[:], scr[:, 0, :], start=True, stop=True).then_inc(ss_done, 1)


def log_sigmoids(core, k, jobs):
    with core.stage("dsteps", "abs_ready", "log_ready", "asteps") as (block, dsteps, abs_ready, log_ready, asteps):
        @block.vector
        def _(dve):
            link = chain(dve, dsteps)
            for n, (src, bias, out, scratch, softplus, times) in enumerate(jobs):
                near, far = (ALU.max, ALU.min) if softplus else (ALU.min, ALU.max)
                if bias.shape[-1] == 1 and len(bias.shape) == 2:
                    link(dve.tensor_scalar(out, src, bias, 0.0, ALU.add, near))
                    link(dve.tensor_scalar(scratch, src, bias, 0.0, ALU.add, far))
                else:
                    link(dve.tensor_tensor(scratch, src, bias, ALU.add))
                    link(dve.tensor_scalar(out, scratch, 0.0, None, near))
                    link(dve.tensor_scalar(scratch, scratch, 0.0, None, far))
                lo, hi = (scratch, out) if softplus else (out, scratch)
                dve.tensor_tensor(scratch, lo, hi, ALU.subtract).then_inc(abs_ready, 1)
                dve.wait_ge(log_ready, n + 1)
                link(dve.tensor_tensor(out, out, scratch, ALU.add if softplus else ALU.subtract))
                if isinstance(times, float):
                    link(dve.tensor_scalar(out, out, times, None, ALU.mult))
                elif times is not None:
                    link(dve.tensor_tensor(times[0], out, times[1], ALU.mult))

        @block.scalar
        def _(act):
            alink = chain(act, asteps)
            for n, (src, bias, out, scratch, softplus, times) in enumerate(jobs):
                act.wait_ge(abs_ready, n + 1)
                alink(act.activation(scratch, scratch, ACT.Exp))
                act.activation(scratch, scratch, ACT.Ln, bias=1.0).then_inc(log_ready, 1)


def gated(core, jobs):
    with core.stage("sig_ready", "done") as (block, sig_ready, done):
        @block.scalar
        def _(act):
            for x, bias, out, scratch, silu in jobs:
                kw = {} if bias is None else {"bias": bias}
                act.activation(scratch if silu else out, x, ACT.Sigmoid, **kw).then_inc(sig_ready, 1)

        @block.vector
        def _(dve):
            for n, (x, bias, out, scratch, silu) in enumerate(jobs):
                dve.wait_ge(sig_ready, n + 1)
                if silu:
                    dve.tensor_tensor(out, x, scratch, ALU.mult).then_inc(done, 1)


def transposes(core, k, jobs):
    ps = k.ps
    with core.stage("pe_done", "evicted") as (block, pe_done, evicted):
        @block.tensor
        def _(pe):
            for n, (srcs, dst) in enumerate(jobs):
                if n >= 8:
                    pe.wait_ge(evicted, n - 7)
                R = srcs[0].shape[0]
                C = srcs[0].shape[1]
                for j, s in enumerate(srcs):
                    ins = pe.transpose(ps[0:C, n % 8, R * j:R * j + R], s, k.ident[0:R, 0:R])
                ins.then_inc(pe_done, 1)

        @block.scalar
        def _(act):
            for n, (srcs, dst) in enumerate(jobs):
                act.wait_ge(pe_done, n + 1)
                R, C, g = srcs[0].shape[0], srcs[0].shape[1], len(srcs)
                act.copy(dst, ps[0:C, n % 8, 0:R * g].rearrange("p (a b) -> p a b", a=g)).then_inc(evicted, 1)


def gla_pair(core, k, hT, pair, alrT, d, out):
    nc = core.nc
    with ExitStack() as ctx:
        sb = lambda n, s: ctx.enter_context(core.sbuf(n, s, F32))
        q = sb("gla_q", [P, NX])
        qpad = sb("gla_qpad", [P, 2, NX])
        kT = sb("gla_k", [P, T])
        v = sb("gla_v", [P, 2, T])
        vt = sb("gla_vt", [P, 2, NC, P])
        gate = sb("gla_gate", [P, 2, NX])
        g = sb("gla_g", [P, 2, T])
        scr = sb("gla_scr", [P, 2, T])
        up = sb("gla_up", [32, 2, P])
        ub = sb("gla_ub", [P, 2])
        project(core, k.ps, hT, d["w_in_gla"][pair], [
            (0, X_ONLY, q[:]), (1, ALL, kT[:]), (2, ALL, v[:, 0, :]), (3, ALL, v[:, 1, :]),
            (4, X_ONLY, gate[:, 0, :]), (5, X_ONLY, gate[:, 1, :])], gates={4: scr[:, 0, 0:NX], 5: scr[:, 1, 0:NX]})
        with core.stage("loaded", "up_clear", "pad_clear") as (block, loaded, up_clear, pad_clear):
            @block.sync
            def _(sp):
                sp.dma_start(ub[:], d["gla_ub"][pair]).then_inc(loaded, 16)
                sp.wait_ge(up_clear, 1)
                sp.dma_start(up[0:16, 0, :], d["gla_up"][pair, 0]).then_inc(loaded, 16)
                sp.dma_start(up[16:32, 1, :], d["gla_up"][pair, 1]).then_inc(loaded, 16)
                sp.wait_ge(loaded, 48)

            @block.vector
            def _(dve):
                dve.memset(up[:], 0.0).then_inc(up_clear, 1)
                dve.memset(qpad[:], 0.0).then_inc(pad_clear, 1)
                dve.wait_ge(pad_clear, 1)
                for e in range(2):
                    r = slice(64 * e, 64 * e + 64)
                    dve.tensor_scalar(qpad[r, e, :], q[r, :], 64.0 ** -0.5, None, ALU.mult)

            @block.tensor
            def _(pe):
                pe.wait_ge(loaded, 48)
                for n in range(2):
                    for b in range(2):
                        pe.matmul(k.ps[:, 2 * n + b, 0:384], up[:, n, :], alrT[0:32, 384 * b:384 * b + 384],
                                  start=True, stop=True)
        log_sigmoids(core, k, [
            (k.ps[:, 2 * n:2 * n + 2, 0:384], ub[:, n:n + 1], g[:, n, :].rearrange("p (b t) -> p b t", b=2),
             scr[:, n, :].rearrange("p (b t) -> p b t", b=2), False, 1.0 / GLA_TAU) for n in range(2)])
        transposes(core, k, [([v[:, e, P * c:P * c + P] for c in cs], vt[:, e, cs[0]:cs[-1] + 1, :])
                             for e in range(2) for cs in (range(0, 4), range(4, 6))])
        for e in range(2):
            key_gated_head(core, k, qpad[:, e, :], (kT[:], kT[:]), (g[:, 0, :], g[:, 1, :]), vt[:, e, :, :],
                           gate[:, e, :], k.gla_onorm[:, 0:1], out(e))


def gdn_head(core, k, hT, head, small, out):
    nc = core.nc
    d = core.dram
    ps = k.ps
    with ExitStack() as ctx:
        sb = lambda n, s: ctx.enter_context(core.sbuf(n, s, F32))
        raw = sb("gdn_raw", [P, 3, T])
        act_ = sb("gdn_act", [P, 3, T])
        scr = sb("gdn_scr", [P, 2, T])
        gate = sb("gdn_gate", [P, NX])
        cw = sb("gdn_cw", [P, 3, 9])
        col = sb("gdn_col", [P, 4, NC])
        ktok = sb("gdn_ktok", [P, NC, P])
        vtok = sb("gdn_vtok", [P, NC, P])
        def conv(dve, evicted, loaded, steps):
            link = chain(dve, steps)
            link(dve.tensor_copy(col[:], small[:, :, :, head].rearrange("p c a -> p a c")))
            dve.wait_ge(loaded, 16)
            for j in range(3):
                dve.wait_ge(evicted, j + 1)
                ci, co = raw[:, j, 0:NCTX], act_[:, j, 0:NCTX]
                link(dve.tensor_scalar(act_[:, j, :], raw[:, j, :], cw[:, j, 4:5], None, ALU.mult))
                n = NCTX
                for dw, o, i in ((-1, slice(1, n), slice(0, n - 1)), (1, slice(0, n - 1), slice(1, n))):
                    link(dve.scalar_tensor_tensor(out=co[:, o], in0=ci[:, i], scalar=cw[:, j, 4 + dw:5 + dw],
                                                  in1=co[:, o], op0=ALU.mult, op1=ALU.add))
                gi = raw[:, j, NCTX:T].rearrange("p (r w) -> p r w", w=GRID_W)
                go = act_[:, j, NCTX:T].rearrange("p (r w) -> p r w", w=GRID_W)
                for dr in (-1, 0, 1):
                    for dw in (-1, 0, 1):
                        if dr == 0 and dw == 0:
                            continue
                        r0, r1 = max(0, -dr), GRID_H - max(0, dr)
                        w0, w1 = max(0, -dw), GRID_W - max(0, dw)
                        tap = 3 * (dr + 1) + dw + 1
                        link(dve.scalar_tensor_tensor(
                            out=go[:, r0:r1, w0:w1], in0=gi[:, r0 + dr:r1 + dr, w0 + dw:w1 + dw],
                            scalar=cw[:, j, tap:tap + 1], in1=go[:, r0:r1, w0:w1], op0=ALU.mult, op1=ALU.add))
        project(core, ps, hT, d["w_in_gdn"][head], [
            (0, ALL, raw[:, 0, :]), (1, ALL, raw[:, 1, :]), (2, ALL, raw[:, 2, :]), (3, X_ONLY, gate[:])],
            [(cw[:], d["gdn_conv"][head])], conv, {3: scr[:, 0, 0:NX]})
        gated(core, [(act_[:, j, :], None, act_[:, j, :], raw[:, j, :], True) for j in range(3)])
        with core.stage("sq_ready", "ss_done", "rstd_ready", "asteps", "dsteps", "v_done") as (
                block, sq_ready, ss_done, rstd_ready, asteps, dsteps, v_done):
            @block.scalar
            def _(act):
                alink = chain(act, asteps)
                act.activation(scr[:], act_[:, 0:2, :], ACT.Square).then_inc(sq_ready, 1)
                act.wait_ge(ss_done, 1)
                sv = scr[:].rearrange("p a (b t) -> p (a b) t", b=2)
                alink(act.activation(sv, ps[:, 0:4, 0:384], ACT.Ln, bias=k.eps[:, 0:1]))
                act.activation(scr[:], scr[:], ACT.Exp, scale=-0.5).then_inc(rstd_ready, 1)

            @block.tensor
            def _(pe):
                pe.wait_ge(sq_ready, 1)
                for n in range(4):
                    mm = pe.matmul(ps[:, n, 0:384], k.ones[:], scr[:, n // 2, 384 * (n % 2):384 * (n % 2) + 384],
                                   start=True, stop=True)
                mm.then_inc(ss_done, 1)

            @block.vector
            def _(dve):
                dve.wait_ge(rstd_ready, 1)
                dve.scalar_tensor_tensor(out=act_[:, 0, :], in0=act_[:, 0, :], scalar=float(P) ** -0.5,
                                         in1=scr[:, 0, :], op0=ALU.mult, op1=ALU.mult)
                dve.tensor_tensor(act_[:, 1, :], act_[:, 1, :], scr[:, 1, :], ALU.mult)
        transposes(core, k, [([act_[:, a, P * c:P * c + P] for c in cs], dst[:, cs[0]:cs[-1] + 1, :])
                             for a, dst in ((1, ktok), (2, vtok)) for cs in (range(0, 4), range(4, 6))])
        qT, kT = act_[:, 0, NCTX:T], act_[:, 1, :]

        gc = sb("gdn_gc", [P, 2, NC])
        exs = sb("gdn_ex", [P, 2, 3, NC])
        dec = sb("gdn_dec", [P, NC, P])
        lows = sb("gdn_low", [P, 2 * NC, P])
        bts = sb("gdn_bt", [P, 2 * NC, P])
        Ts = sb("gdn_T", [P, 2 * NC, P])
        Us = sb("gdn_U", [P, 2 * NC, P])
        Pm = sb("gdn_P", [P, 2 * NC, P])
        att = sb("gdn_att", [P, 2, NXC, P])
        qe = sb("gdn_qe", [P, 2, NX])
        kgs = sb("gdn_kg", [P, 2, NC, P])
        vbs = sb("gdn_vb", [P, 2, NC, P])
        S = sb("gdn_S", [P, 2, NC + 1, P])
        R = sb("gdn_R", [P, 2, P])
        vn = sb("gdn_vn", [P, 2, 2, P])
        c3 = lambda a: a.rearrange("p (b c) t -> p b c t", b=2)
        bank2 = lambda b: ps[:, b:b + 2, 0:384].rearrange("p b (c t) -> p b c t", c=3)
        chunk = lambda b, c: ps[:, b + c // 3, P * (c % 3):P * (c % 3) + P]
        for dr in range(2):
            incl = k.incl[:, dr, :]
            ex, kg, vb = exs[:, dr], kgs[:, dr], vbs[:, dr]
            low, bt, Tm, Um = (a[:, NC * dr:NC * dr + NC, :] for a in (lows, bts, Ts, Us))
            with core.stage("sums_done", "gc_ready", "gram_done", "dsteps", "dec_ready", "exp_ready", "low_ready",
                            "turn_done", "asteps", "evict") as (
                    block, sums_done, gc_ready, gram_done, dsteps, dec_ready, exp_ready, low_ready, turn_done, asteps, evict):
                @block.tensor
                def _(pe):
                    beta, g = col[:, dr, :], col[:, 2 + dr, :]
                    pe.matmul(ps[:, 6, 0:NC], incl, g, start=True, stop=True)
                    pe.matmul(ps[:, 6, NC:2 * NC], k.ones[:], g, start=True, stop=True).then_inc(sums_done, 1)
                    for c in range(NC):
                        pe.matmul(chunk(0, c), g[:, c:c + 1].to_broadcast([P, P]), incl, start=True, stop=True)
                        mm = pe.matmul(chunk(2, c), beta[:, c:c + 1].to_broadcast([P, P]), k.ident[:], start=True, stop=True)
                    mm.then_inc(sums_done, 1)
                    for c in range(NC):
                        kc = kT[:, P * c:P * c + P]
                        mm = pe.matmul(chunk(4, c), kc, kc, start=True, stop=True)
                    mm.then_inc(gram_done, 1)
                    pe.wait_ge(low_ready, 1)
                    for c in range(NC):
                        mm = pe.transpose(chunk(0, c), Um[:, c, :], k.ident[:])
                    mm.then_inc(turn_done, 1)
                    pe.wait_ge(gc_ready, 1)
                    for c in range(NXC):
                        mm = pe.matmul(ps[:, 7, P * c:P * c + P], kT[:, NCTX + P * c:NCTX + P * c + P],
                                       qT[:, P * c:P * c + P], start=True, stop=True)
                    mm.then_inc(turn_done, 1)

                @block.vector
                def _(dve):
                    link = chain(dve, dsteps)
                    dve.wait_ge(sums_done, 1)
                    link(dve.tensor_copy(gc[:], ps[:, 6, 0:2 * NC].rearrange("p (a c) -> p a c", a=2)))
                    dve.tensor_tensor(ex[:, 1, :], gc[:, 1, :], gc[:, 0, :], ALU.subtract).then_inc(gc_ready, 1)
                    dve.wait_ge(sums_done, 2)
                    for c in range(NC):
                        ins = dve.tensor_scalar(dec[:, c, :], chunk(0, c), gc[:, 0, c:c + 1], 0.0, ALU.subtract, ALU.min)
                    ins.then_inc(dec_ready, 1)
                    dve.wait_ge(exp_ready, 3)
                    link(dve.tensor_tensor(ex[:, 0, :], ex[:, 0, :], col[:, dr, :], ALU.mult))
                    link(dve.tensor_tensor(kg, ktok[:], ex[:, 1, :].unsqueeze(2).to_broadcast([P, NC, P]), ALU.mult))
                    link(dve.tensor_tensor(vb, vtok[:], col[:, dr, :].unsqueeze(2).to_broadcast([P, NC, P]), ALU.mult))
                    dve.wait_ge(exp_ready, 4)
                    link(dve.tensor_tensor(qe[:, dr, :], qe[:, dr, :], qT, ALU.mult))
                    dve.wait_ge(exp_ready, 5)
                    link(dve.tensor_tensor(c3(low), c3(dec[:]), bank2(2), ALU.mult))
                    dve.wait_ge(gram_done, 1)
                    link(dve.tensor_tensor(c3(low), c3(low), bank2(4), ALU.mult))
                    link(dve.tensor_tensor(bt, low, k.levelf[:, dr, 1, :].unsqueeze(1).to_broadcast([P, NC, P]), ALU.mult))
                    dve.tensor_tensor(Um, k.ident[:].unsqueeze(1).to_broadcast([P, NC, P]), bt,
                                      ALU.subtract).then_inc(low_ready, 1)
                    dve.wait_ge(turn_done, 1)
                    link(dve.tensor_copy(c3(Tm), bank2(0)))
                    dve.wait_ge(turn_done, 2)
                    link(dve.tensor_tensor(att[:, dr, :, :], dec[:, C0:NC, :],
                                           ps[:, 7, :].rearrange("p (c t) -> p c t", c=NXC), ALU.mult))
                    link(dve.tensor_tensor(att[:, dr, :, :], att[:, dr, :, :],
                                           incl.unsqueeze(1).to_broadcast([P, NXC, P]), ALU.mult))

                @block.scalar
                def _(act):
                    act.wait_ge(gc_ready, 1)
                    act.activation(ex[:, 0, :], gc[:, 0, :], ACT.Exp).then_inc(exp_ready, 1)
                    act.activation(ex[:, 1, :], ex[:, 1, :], ACT.Exp).then_inc(exp_ready, 1)
                    act.activation(ex[:, 2, :], gc[:, 1, :], ACT.Exp).then_inc(exp_ready, 1)
                    act.wait_ge(dec_ready, 1)
                    for c in range(NXC):
                        ins = act.activation(qe[:, dr, P * c:P * c + P], chunk(0, C0 + c), ACT.Exp)
                    ins.then_inc(exp_ready, 1)
                    act.activation(dec[:], dec[:], ACT.Exp).then_inc(exp_ready, 1)
        lots, last = range(3), LEVELS - 1
        four = lambda a, q: a[:, 4 * q:4 * q + 4, :]
        bank = lambda b: ps[:, b, :].rearrange("p (c t) -> p c t", c=4)
        with core.stage("b_ready", "p_done", "p_read", "q_done", "t_ready") as (block, b_ready, p_done, p_read, q_done, t_ready):
            @block.gpsimd
            def _(pool):
                for i in range(1, LEVELS):
                    if i > 1:
                        pool.wait_ge(p_done, 3 * (i - 1))
                    for dr in range(2):
                        pool.tensor_tensor(bts[:, NC * dr:NC * dr + NC, :], lows[:, NC * dr:NC * dr + NC, :],
                                           k.levelf[:, dr, i + 1, :].unsqueeze(1).to_broadcast([P, NC, P]),
                                           ALU.mult).then_inc(b_ready, 1)

            @block.vector
            def _(dve):
                for i in range(1, LEVELS):
                    for q in lots:
                        dve.wait_ge(q_done, 3 * (i - 1) + q + 1)
                        if i < last:
                            dve.tensor_tensor(four(Ts, q), four(Ts, q), bank(3 + q), ALU.subtract)
                        dve.tensor_tensor(four(Us, q), four(Us, q), bank(q), ALU.subtract).then_inc(t_ready, 1)
                        if i < last:
                            dve.wait_ge(t_ready, 3 * (i - 1) + q + 1)

            @block.scalar
            def _(act):
                for i in range(1, LEVELS):
                    for q in lots:
                        act.wait_ge(p_done, 3 * (i - 1) + q + 1)
                        act.copy(four(Pm, q), bank(q)).then_inc(p_read, 1)

            @block.tensor
            def _(pe):
                for i in range(1, LEVELS):
                    pe.wait_ge(b_ready, 2 * i)
                    for q in lots:
                        if i > 1:
                            pe.wait_ge(t_ready, 3 * (i - 2) + q + 1)
                        for j in range(4):
                            n = 4 * q + j
                            mm = pe.matmul(ps[:, q, P * j:P * j + P], bts[:, n, :], Ts[:, n, :], start=True, stop=True)
                        mm.then_inc(p_done, 1)
                    for q in lots:
                        pe.wait_ge(p_read, 3 * (i - 1) + q + 1)
                        for j in range(4):
                            n, o = 4 * q + j, slice(P * j, P * j + P)
                            if i < last:
                                pe.matmul(ps[:, 3 + q, o], Us[:, n, :], Pm[:, n, :], start=True, stop=True)
                            mm = pe.matmul(ps[:, q, o], Pm[:, n, :], Us[:, n, :], start=True, stop=True)
                        mm.then_inc(q_done, 1)
        with core.stage("S_ready", "x_done", "r_ready", "w_done", "v_ready", "u_done") as (
                block, S_ready, x_done, r_ready, w_done, v_ready, u_done):
            turns = [(2 * i + dr, i, dr, ORDER[dr][i]) for i in range(NC) for dr in range(2)]
            pairs = [turns[2 * i:2 * i + 2] for i in range(NC)]

            @block.vector
            def _(dve):
                for dr in range(2):
                    dve.memset(S[:, dr, 0, :], 0.0).then_inc(S_ready, 1)
                for pair in pairs:
                    for n, i, dr, c in pair:
                        dve.wait_ge(x_done, n + 1)
                        dve.scalar_tensor_tensor(out=R[:, dr], in0=ps[:, dr, 0:P], scalar=exs[:, dr, 0, c:c + 1], in1=vbs[:, dr, c, :],
                                                 op0=ALU.mult, op1=ALU.subtract).then_inc(r_ready, 1)
                    for n, i, dr, c in pair:
                        dve.wait_ge(w_done, n + 1)
                        dve.tensor_scalar(vn[:, dr, i % 2, :], ps[:, 2 + dr, 0:P], -1.0, None, ALU.mult).then_inc(v_ready, 1)
                    for n, i, dr, c in pair:
                        dve.wait_ge(u_done, n + 1)
                        dve.scalar_tensor_tensor(out=S[:, dr, i + 1, :], in0=S[:, dr, i, :], scalar=exs[:, dr, 2, c:c + 1],
                                                 in1=ps[:, 4 + dr, 0:P], op0=ALU.mult, op1=ALU.add).then_inc(S_ready, 1)

            @block.tensor
            def _(pe):
                for pair in pairs:
                    for n, i, dr, c in pair:
                        pe.wait_ge(S_ready, n + 1)
                        pe.matmul(ps[:, dr, 0:P], kT[:, P * c:P * c + P], S[:, dr, i, :], start=True, stop=True).then_inc(x_done, 1)
                    for n, i, dr, c in pair:
                        pe.wait_ge(r_ready, n + 1)
                        pe.matmul(ps[:, 2 + dr, 0:P], Us[:, NC * dr + c, :], R[:, dr], start=True, stop=True).then_inc(w_done, 1)
                    for n, i, dr, c in pair:
                        pe.wait_ge(v_ready, n + 1)
                        pe.matmul(ps[:, 4 + dr, 0:P], kgs[:, dr, c, :], vn[:, dr, i % 2, :], start=True, stop=True).then_inc(u_done, 1)
                    for n, i, dr, c in pair:
                        if c >= C0:
                            x = slice(P * (c - C0), P * (c - C0) + P)
                            pe.matmul(ps[:, 6 + dr, x], S[:, dr, i, :], qe[:, dr, x], start=True, stop=False)
                            pe.matmul(ps[:, 6 + dr, x], vn[:, dr, i % 2, :], att[:, dr, c - C0, :], start=False, stop=True)
        with core.stage("dsteps", "o_ready", "sq_ready", "ss_done", "rstd_ready", "asteps", "kept") as (
                block, dsteps, o_ready, sq_ready, ss_done, rstd_ready, asteps, kept):
            @block.vector
            def _(dve):
                link = chain(dve, dsteps)
                dve.wait_ge(kept, 1)
                dve.tensor_tensor(raw[:, 0, 0:NX], raw[:, 2, 0:NX], ps[:, 7, :], ALU.add).then_inc(o_ready, 1)
                dve.wait_ge(rstd_ready, 1)
                link(dve.tensor_tensor(raw[:, 0, 0:NX], raw[:, 0, 0:NX], raw[:, 1, 0:NX], ALU.mult))
                link(dve.scalar_tensor_tensor(out=out, in0=raw[:, 0, 0:NX], scalar=k.gdn_onorm[:, 0:1], in1=gate[:],
                                              op0=ALU.mult, op1=ALU.mult))

            @block.scalar
            def _(act):
                alink = chain(act, asteps)
                act.copy(raw[:, 2, 0:NX], ps[:, 6, :]).then_inc(kept, 1)
                act.wait_ge(o_ready, 1)
                act.activation(raw[:, 1, 0:NX], raw[:, 0, 0:NX], ACT.Square).then_inc(sq_ready, 1)
                act.wait_ge(ss_done, 1)
                alink(act.activation(raw[:, 1, 0:NX], ps[:, 0, :], ACT.Ln, bias=k.eps[:, 0:1], scale=1.0 / P))
                act.activation(raw[:, 1, 0:NX], raw[:, 1, 0:NX], ACT.Exp, scale=-0.5).then_inc(rstd_ready, 1)

            @block.tensor
            def _(pe):
                pe.wait_ge(sq_ready, 1)
                pe.matmul(ps[:, 0, :], k.ones[:], raw[:, 1, 0:NX], start=True, stop=True).then_inc(ss_done, 1)


def merge(core, k, hT, w_dram, nA, nB, aT, bT, gate_bias, mT):
    nc = core.nc
    ps = k.ps
    width = nA + nB + 2 * KD
    with ExitStack() as ctx:
        w = ctx.enter_context(core.sbuf("mg_w", [P, 2, width - 2 * KD, P], F32))
        wg = ctx.enter_context(core.sbuf("mg_wg", [P, 2 * KD, P], F32))
        wh = ctx.enter_context(core.sbuf("mg_wh", [P, 2 * KD, P], F32R))
        wl = ctx.enter_context(core.sbuf("mg_wl", [P, 2 * KD, P], F32R))
        sg = ctx.enter_context(core.sbuf("mg_sg", [P, 2, 2, NX], F32))
        with core.stage("w_in*2", "g_in", "high_ready", "low_ready", "gates_done", "pe_done", "sg_ready", "dsteps", "out_done") as (
                block, w_in, g_in, high_ready, low_ready, gates_done, pe_done, sg_ready, dsteps, out_done):
            @block.sync
            def _(sp):
                for n in range(KD):
                    if n >= 1:
                        sp.wait_ge(low_ready, n)
                    sp.dma_start(wg[:], w_dram[n][:, nA + nB:width, :]).then_inc(g_in, 16)
                    if n >= 2:
                        sp.wait_ge(pe_done, n - 1)
                    sp.dma_start(w[:, n % 2, :, :], w_dram[n][:, 0:nA + nB, :]).then_inc(w_in[n % 2], 16)

            @block.gpsimd
            def _(pool):
                for n in range(KD):
                    pool.wait_ge(high_ready, n + 1)
                    pool.tensor_tensor(wl[:], wg[:], wh[:].bitcast(F32), ALU.subtract).then_inc(low_ready, 1)

            @block.tensor
            def _(pe):
                for n in range(KD):
                    if n >= 2:
                        pe.wait_ge(out_done, n - 1)
                    b = 4 * (n % 2)
                    pe.wait_ge(low_ready, n + 1)
                    for bank in range(2):
                        for j in range(KD):
                            o = KD * bank + j
                            mm = product3(pe, ps[:, b + bank, :], (wh[:, o, :], wl[:, o, :]),
                                          (hT[0][:, j, NCTX:T], hT[1][:, j, NCTX:T]), j == 0, j == KD - 1)
                    mm.then_inc(gates_done, 1)
                    pe.wait_ge(w_in[n % 2], 16 * (n // 2 + 1))
                    for bank, off, kn, src in ((2, 0, nA, aT), (3, nA, nB, bT)):
                        for j in range(kn):
                            mm = pe.matmul(ps[:, b + bank, :], w[:, n % 2, off + j, :], src[:, j, :], start=(j == 0), stop=(j == kn - 1))
                    mm.then_inc(pe_done, 1)

            @block.scalar
            def _(act):
                def high(n):
                    act.wait_ge(g_in, 16 * (n + 1))
                    if n >= 1:
                        act.wait_ge(gates_done, n)
                    act.copy(wh[:], wg[:]).then_inc(high_ready, 1)
                high(0)
                for n in range(KD):
                    if n + 1 < KD:
                        high(n + 1)
                    act.wait_ge(gates_done, n + 1)
                    if n >= 2:
                        act.wait_ge(out_done, n - 1)
                    b = 4 * (n % 2)
                    for a in range(2):
                        kw = {} if gate_bias is None else {"bias": gate_bias[:, KD * a + n:KD * a + n + 1]}
                        act.activation(sg[:, n % 2, a, :], ps[:, b + a, :], ACT.Sigmoid, **kw).then_inc(sg_ready, 1)

            @block.vector
            def _(dve):
                link = chain(dve, dsteps)
                for n in range(KD):
                    dve.wait_ge(sg_ready, 2 * n + 2)
                    dve.wait_ge(pe_done, n + 1)
                    b = 4 * (n % 2)
                    for a in range(2):
                        link(dve.tensor_tensor(sg[:, n % 2, a, :], sg[:, n % 2, a, :], ps[:, b + 2 + a, :], ALU.mult))
                    dve.tensor_tensor(mT[:, n, :], sg[:, n % 2, 0, :], sg[:, n % 2, 1, :], ALU.add).then_inc(out_done, 1)


def output_product(core, k, mT, w_dram, gate_row, alpha, xs):
    nc = core.nc
    ps = k.ps
    with ExitStack() as ctx:
        w = ctx.enter_context(core.sbuf("op_w", [P, KD, D], F32))
        y = ctx.enter_context(core.sbuf("op_y", [P, 2, 512], F32))
        with core.stage("w_in", "pe_done", "out_done", "dsteps") as (block, w_in, pe_done, out_done, dsteps):
            @block.sync
            def _(sp):
                for j in range(KD):
                    sp.dma_start(w[:, j, :], w_dram[P * j:P * j + P, :]).then_inc(w_in, 16)
                sp.wait_ge(w_in, 16 * KD)

            @block.tensor
            def _(pe):
                pe.wait_ge(w_in, 16 * KD)
                for n in range(8):
                    t, h = n // 2, n % 2
                    for j in range(KD):
                        mm = pe.matmul(ps[:, n, :], mT[:, j, P * t:P * t + P], w[:, j, 512 * h:512 * h + 512],
                                       start=(j == 0), stop=(j == KD - 1))
                    mm.then_inc(pe_done, 1)

            @block.vector
            def _(dve):
                link = chain(dve, dsteps)
                for n in range(8):
                    t, h = n // 2, n % 2
                    dve.wait_ge(pe_done, n + 1)
                    link(dve.tensor_tensor(y[:, n % 2, :], ps[:, n, :], gate_row[:, h, :], ALU.mult))
                    x = xs[t][:, 512 * h:512 * h + 512]
                    link(dve.scalar_tensor_tensor(out=x, in0=x, scalar=alpha, in1=y[:, n % 2, :], op0=ALU.mult, op1=ALU.add))


def norm_rows(core, k, tiles, centre, g, b):
    nc = core.nc
    with ExitStack() as ctx:
        sq = ctx.enter_context(core.sbuf("nr_sq", [P, D], F32))
        st = ctx.enter_context(core.sbuf("nr_st", [P, len(tiles), 4], F32))
        with core.stage("dsteps", "asteps", "mean_ready", "rstd_ready") as (block, dsteps, asteps, mean_ready, rstd_ready):
            @block.vector
            def _(dve):
                link = chain(dve, dsteps)
                for i, x in enumerate(tiles):
                    s = st[:, i, :]
                    if centre:
                        link(dve.tensor_reduce(s[:, 0:1], x, AX.X, ALU.add))
                        link(dve.tensor_scalar(s[:, 1:2], s[:, 0:1], -1.0 / D, None, ALU.mult))
                        link(dve.tensor_scalar(x, x, s[:, 1:2], None, ALU.add))
                    dve.sem_inc(mean_ready, 1)
                for i, x in enumerate(tiles):
                    s = st[:, i, :]
                    dve.wait_ge(rstd_ready, i + 1)
                    link(dve.scalar_tensor_tensor(out=x, in0=x, scalar=s[:, 3:4], in1=g, op0=ALU.mult, op1=ALU.mult))
                    if b is not None:
                        link(dve.tensor_tensor(x, x, b, ALU.add))

            @block.scalar
            def _(act):
                alink = chain(act, asteps)
                for i, x in enumerate(tiles):
                    s = st[:, i, :]
                    act.wait_ge(mean_ready, i + 1)
                    alink(act.activation(sq[:], x, ACT.Square, accum_out=s[:, 2:3]))
                    alink(act.activation(s[:, 3:4], s[:, 2:3], ACT.Ln, bias=k.eps[:, 0:1], scale=1.0 / D))
                    act.activation(s[:, 3:4], s[:, 3:4], ACT.Exp, scale=-0.5).then_inc(rstd_ready, 1)


class Buffers:
    pass


def program(nc, dram, out, taps=None, upto=99):
    d = dram
    with ExitStack() as ctx:
        core = Core(nc, ctx, dram)
        sbt = lambda n, s, dt=F32: ctx.enter_context(core.sbuf(n, s, dt))
        k = Buffers()
        k.ps = ctx.enter_context(nc.psum_tensor("ps", [P, 8, 512], F32))
        k.ident, k.eps = sbt("ident", [P, P]), sbt("eps", [P, 1])
        xs = sbt("xs", [P, NXC, D])
        cols = sbt("cols2", [P, 4 * KD, 2])
        rows = sbt("rows2", [P, 4, 512])

        def tap(name, ap):
            if taps is not None and name in taps:
                with core.stage("kept") as (block, kept):
                    @block.sync
                    def _(sp):
                        sp.dma_start(taps[name], ap).then_inc(kept, 16)
                        sp.wait_ge(kept, 16)

        with ExitStack() as mix:
            sbm = lambda n, s, dt=F32: mix.enter_context(core.sbuf(n, s, dt))
            k.ones, k.incl = sbm("ones", [P, P]), sbm("incl", [P, 2, P])
            hT = sbm("hT_high", [P, KD, T], F32R), sbm("hT_low", [P, KD, T], F32R)
            load_all(core, [(k.ident[:], d["ident"]), (k.ones[:], d["ones"]), (k.incl[:], d["incl"])]
                     + [(xs[:, t, :], d["x"][P * t:P * t + P, :]) for t in range(NXC)])
            with core.stage("eps_ready") as (block, eps_ready):
                @block.vector
                def _(dve):
                    dve.memset(k.eps[:], EPS).then_inc(eps_ready, 1)
            first_block(core, k, hT, xs, tap)
            tap("x1", xs[:])
            if upto > 1:
                mixer_block(core, k, hT, xs, cols, rows, tap)
        if upto > 2:
            expert_block(core, k, xs, cols, rows, tap)
        with core.stage("stored") as (block, stored):
            @block.sync
            def _(sp):
                for t in range(NXC):
                    sp.dma_start(out[P * t:P * t + P, :], xs[:, t, :]).then_inc(stored, 16)
                sp.wait_ge(stored, 16 * NXC)


@contextmanager
def gated_constants(core, k):
    with core.sbuf("level", [P, 2, LEVELS + 1, P], U32) as k.level, core.sbuf("restart", [P, 2, T]) as k.restart:
        load_all(core, [(k.level[:], core.dram["level"]), (k.restart[:], core.dram["restart"])])
        yield


def first_block(core, k, hT, xs, tap):
    nc, d = core.nc, core.dram
    with ExitStack() as ctx:
        sbt = lambda n, s, dt=F32: ctx.enter_context(core.sbuf(n, s, dt))
        cond = sbt("cond", [P, KD, 2])
        cols = sbt("cols", [P, 2 * KD, 2])
        rows = sbt("rows", [P, 2, 512])
        b_cols, b_rows = sbt("b_cols", [P, 2 * KD]), sbt("b_rows", [P, 2, 512])
        norm_g = sbt("norm_g", [P, KD])
        scale = sbt("scale", [P, KD, 2])
        k.gla_onorm, k.gdn_onorm = sbt("gla_onorm", [P, 1]), sbt("gdn_onorm", [P, 1])
        b_gate = sbt("b_gate", [P, 2 * KD])
        glog_rows = sbt("glog_rows", [P, 2, 8])
        load_all(core, [(cond[:], d["cond"]), (b_cols[:], d["b_mod_cols"]),
                        (b_rows[:], d["b_mod_rows"].partition_broadcast(P)),
                        (norm_g[:], d["norm_g"]), (k.gla_onorm[:], d["gla_onorm"]), (k.gdn_onorm[:], d["gdn_onorm"]),
                        (b_gate[:], d["b_gate"]), (glog_rows[:, 0, :], d["gdn_a_log"].partition_broadcast(P)),
                        (glog_rows[:, 1, :], d["gdn_dt_bias"].partition_broadcast(P))])
        modulation(core, sbt, k.ps, cond, d["w_mod_cols"], 2 * KD, cols, b_cols, d["w_mod_rows"], 2, rows, b_rows)
        with core.stage("steps") as (block, steps):
            @block.vector
            def _(dve):
                link = chain(dve, steps)
                link(dve.tensor_scalar(scale[:], cols[:, KD:2 * KD, :], 1.0, None, ALU.add))
                link(dve.tensor_tensor(scale[:], scale[:], norm_g[:].unsqueeze(2).to_broadcast([P, KD, 2]), ALU.mult))
        tap("cols1", cols[:])
        with core.sbuf("ctx_rows", [P, C0, D], F32) as ctx_rows, core.sbuf("h_whole", [P, KD, T]) as whole:
            load_all(core, [(ctx_rows[:, t, :], d["ctx"][P * t:P * t + P, :]) for t in range(C0)])
            norm_transpose(core, k.ps, k.ident, k.eps,
                           [(ctx_rows[:, t, :], P * t, 1) for t in range(C0)]
                           + [(xs[:, t, :], NCTX + P * t, 0) for t in range(NXC)], False, scale, cols[:, 0:KD, :], whole)
            tap("hT1", whole[:])
            split(core, whole, *hT)
        smallT = sbt("smallT", [48, T])
        small = sbt("small", [P, NC, 48])
        gates = sbt("gates", [P, NC, 4, 4])
        tmp = sbt("gates_tmp", [P, NC, 8])
        project(core, k.ps, hT, d["w_in_small"], [(0, ALL, smallT[:])])
        transposes(core, k, [([smallT[:, P * c:P * c + P] for c in cs], small[:, cs[0]:cs[-1] + 1, :])
                             for cs in (range(0, 4), range(4, 6))])
        with core.stage("exp_ready") as (block, exp_ready):
            @block.scalar
            def _(act):
                act.activation(gates[:, :, 0:2, :], small[:, :, 32:40].rearrange("p c (a h) -> p c a h", a=2), ACT.Sigmoid)
                act.activation(glog_rows[:, 0, :], glog_rows[:, 0, :], ACT.Exp).then_inc(exp_ready, 1)

            @block.vector
            def _(dve):
                dve.wait_ge(exp_ready, 1)
                dve.tensor_scalar(glog_rows[:, 0, :], glog_rows[:, 0, :], -1.0, None, ALU.mult)
        wide = lambda a: a.unsqueeze(1).to_broadcast([P, NC, 8])
        lg = gates[:, :, 2:4, :].rearrange("p c a h -> p c (a h)")
        log_sigmoids(core, k, [(small[:, :, 40:48], wide(glog_rows[:, 1, :]), lg, tmp[:], True, (lg, wide(glog_rows[:, 0, :])))])
        yaT, ybT = sbt("yaT", [P, 4, NX]), sbt("ybT", [P, 4, NX])
        with gated_constants(core, k), nc.Fori(0, GLA_HEADS // 2) as pair:
            gla_pair(core, k, hT, pair, smallT, d, lambda e: yaT[:, pair * 2 + e, :])
        tap("yaT", yaT[:])
        with core.sbuf("levelf", [P, 2, LEVELS + 1, P]) as k.levelf:
            load_all(core, [(k.levelf[:], d["levelf"])])
            with nc.Fori(0, GDN_HEADS) as head:
                gdn_head(core, k, hT, head, gates, ybT[:, head, :])
        tap("ybT", ybT[:])
        mT = sbt("mT", [P, KD, NX])
        merge(core, k, hT, d["w_merge"], 4, 4, yaT, ybT, b_gate[:], mT)
        tap("mT1", mT[:])
        output_product(core, k, mT, d["w_o"], rows, 1.0, [xs[:, t, :] for t in range(NXC)])
        with core.sbuf("final_g", [P, D], F32) as final_g:
            load_all(core, [(final_g[:], d["final_g"].partition_broadcast(P))])
            norm_rows(core, k, [xs[:, t, :] for t in range(NXC)], False, final_g[:], None)


TG = 64
JG = 4
N_TG, N_JG = NX // TG, PEER_KEYS // JG


def top16(dve, link, values, copy, best, index):
    def each(make):
        for n in range(len(values) - 1):
            make(n)
        link(make(len(values) - 1))
    each(lambda n: dve.max(best[n][:, 0:8], values[n]))
    each(lambda n: dve.max_index(index[n][:, 0:8], best[n][:, 0:8], values[n]))
    each(lambda n: dve.match_replace(copy[n], best[n][:, 0:8], values[n], -3.0e38))
    each(lambda n: dve.max(best[n][:, 8:16], copy[n]))
    each(lambda n: dve.max_index(index[n][:, 8:16], best[n][:, 8:16], copy[n]))


def route_head(core, k, hT, head, iota16, chosen):
    nc, d, ps = core.nc, core.dram, k.ps
    with ExitStack() as ctx:
        sb = lambda n, s, dt=F32: ctx.enter_context(core.sbuf(n, s, dt))
        q = sb("pr_q", [P, 2, NX])
        keys = sb("pr_keys", [P, 2, P])
        sc = sb("pr_sc", [P, 2, NXC, P])
        copy = sb("pr_copy", [P, NXC, 2 * P])
        best = sb("pr_best", [P, 2, NXC, TOPK])
        idx = sb("pr_idx", [P, 2, NXC, TOPK], U32)
        idf = sb("pr_idf", [P, 2, NXC, TOPK])
        cand = sb("pr_cand", [P, NXC, TOPK, TOPK])
        top = sb("pr_top", [P, NXC, TOPK])
        pos = sb("pr_pos", [P, NXC, TOPK], U32)
        part = sb("pr_part", [P, 2, NXC, TOPK], U32)
        partf = sb("pr_partf", [P, 2, NXC, TOPK])
        hot = sb("pr_hot", [P, NXC, TOPK, TOPK])
        val = sb("pr_val", [P, 3, NXC, TOPK])
        s1 = sb("pr_s1", [P, NXC])
        project(core, ps, hT, d["w_q"][head], [(0, X_AT_0, q[:, 0, :]), (1, X_AT_0, q[:, 1, :])])
        with core.stage("loaded", "score_done", "dsteps", "shift_ready", "exp_ready") as (
                block, loaded, score_done, dsteps, shift_ready, exp_ready):
            @block.sync
            def _(sp):
                sp.dma_start(keys[:], d["subkeys"][head]).then_inc(loaded, 16)
                sp.wait_ge(loaded, 16)

            @block.tensor
            def _(pe):
                pe.wait_ge(loaded, 16)
                for i in range(2):
                    for t in range(NXC):
                        mm = pe.matmul(ps[:, i, P * t:P * t + P], q[:, i, P * t:P * t + P], keys[:, i, :], start=True, stop=True)
                    mm.then_inc(score_done, 1)

            @block.vector
            def _(dve):
                link = chain(dve, dsteps)
                big = [P, NXC, TOPK, TOPK]
                for i in range(2):
                    dve.wait_ge(score_done, i + 1)
                    link(dve.tensor_copy(sc[:, i], ps[:, i, :].rearrange("p (t n) -> p t n", t=NXC)))
                    top16(dve, link, *zip(*[(sc[:, i, t, :], copy[:, t, 0:P], best[:, i, t, :], idx[:, i, t, :])
                                            for t in range(NXC)]))
                link(dve.tensor_copy(idf[:], idx[:]))
                link(dve.tensor_tensor(cand[:], best[:, 0].unsqueeze(3).to_broadcast(big),
                                       best[:, 1].unsqueeze(2).to_broadcast(big), ALU.add))
                top16(dve, link, *zip(*[(cand[:, t].rearrange("p a b -> p (a b)"), copy[:, t, :], top[:, t, :], pos[:, t, :])
                                        for t in range(NXC)]))
                dve.tensor_tensor(val[:, 2], top[:], top[:, :, 0:1].to_broadcast([P, NXC, TOPK]), ALU.subtract).then_inc(shift_ready, 1)
                link(dve.tensor_scalar(part[:, 0], pos[:], 4, None, ALU.logical_shift_right))
                link(dve.tensor_scalar(part[:, 1], pos[:], 15, None, ALU.bitwise_and))
                link(dve.tensor_copy(partf[:], part[:]))
                for i in range(2):
                    link(dve.tensor_tensor(hot[:], partf[:, i].unsqueeze(3).to_broadcast(big),
                                           iota16.unsqueeze(1).unsqueeze(1).to_broadcast(big), ALU.is_equal))
                    link(dve.tensor_tensor(hot[:], hot[:], idf[:, i].unsqueeze(2).to_broadcast(big), ALU.mult))
                    link(dve.tensor_reduce(val[:, i], hot[:], AX.X, ALU.add))
                dve.wait_ge(exp_ready, 1)
                link(dve.tensor_reduce(s1[:], val[:, 2], AX.X, ALU.add))
                link(dve.reciprocal(s1[:], s1[:]))
                link(dve.tensor_tensor(val[:, 2], val[:, 2], s1[:].unsqueeze(2).to_broadcast([P, NXC, TOPK]), ALU.mult))
                link(dve.tensor_copy(chosen[:, :, :, bass.ds(head * TOPK, TOPK)], val[:].rearrange("p a t m -> p t a m")))

            @block.scalar
            def _(act):
                act.wait_ge(shift_ready, 1)
                act.activation(val[:, 2], val[:, 2], ACT.Exp).then_inc(exp_ready, 1)


def spread_gates(core, k, chosenT, iota, g_dram):
    nc, ps = core.nc, k.ps
    OH = 8
    LOTS = 4
    quads = TG // 4
    with ExitStack() as ctx:
        sb = lambda n, s: ctx.enter_context(core.sbuf(n, s))
        cur = sb("sg_cur", [P, 3, LOTS * TG])
        one = sb("sg_one", [P, OH, P])
        two = sb("sg_two", [P, OH, P])
        gbuf = sb("sg_gbuf", [P, 2, PEER_KEYS, TG])
        with nc.Fori(0, N_TG // LOTS) as part:
            with core.stage("cur_ready", "hot_ready", "g_done", "g_read", "stored*2") as (
                    block, cur_ready, hot_ready, g_done, g_read, stored):
                @block.vector
                def _(dve):
                    dve.tensor_copy(cur[:], chosenT[:, :, bass.ds(part * (LOTS * TG), LOTS * TG)]).then_inc(cur_ready, 1)
                    dve.wait_ge(cur_ready, 1)
                    for n in range(LOTS * quads):
                        if n >= OH // 4:
                            dve.wait_ge(g_done, n - OH // 4 + 1)
                        t0 = 4 * n % OH
                        dve.tensor_tensor(one[:, t0:t0 + 4, :], iota.unsqueeze(1).to_broadcast([P, 4, P]),
                                          cur[:, 0, 4 * n:4 * n + 4].unsqueeze(2).to_broadcast([P, 4, P]), ALU.is_equal)
                        for a in range(4):
                            t = 4 * n + a
                            ins = dve.tensor_scalar(two[:, t0 + a, :], iota, cur[:, 1, t:t + 1], cur[:, 2, t:t + 1],
                                                    ALU.is_equal, ALU.mult)
                        ins.then_inc(hot_ready, 1)

                @block.tensor
                def _(pe):
                    for n in range(LOTS * quads):
                        pe.wait_ge(hot_ready, n + 1)
                        if n >= 8:
                            pe.wait_ge(g_read, n - 7)
                        for a in range(4):
                            t = (4 * n + a) % OH
                            mm = pe.matmul(ps[:, n % 8, P * a:P * a + P], one[:, t, :], two[:, t, :], start=True, stop=True)
                        mm.then_inc(g_done, 1)

                @block.scalar
                def _(act):
                    for n in range(LOTS * quads):
                        act.wait_ge(g_done, n + 1)
                        lot, at = n // quads, 4 * (n % quads)
                        if lot >= 2 and at == 0:
                            act.wait_ge(stored[lot % 2], 16 * (lot // 2))
                        act.copy(gbuf[:, lot % 2, :, at:at + 4].rearrange("p j t -> p t j"),
                                 ps[:, n % 8, :].rearrange("p (t j) -> p t j", t=4)).then_inc(g_read, 1)

                @block.sync
                def _(sp):
                    for lot in range(LOTS):
                        sp.wait_ge(g_read, quads * (lot + 1))
                        sp.dma_start(g_dram[:, :, bass.ds(part * LOTS + lot, 1)].rearrange("g p o e -> p (g o) e"),
                                     gbuf[:, lot % 2].rearrange("p (g j) t -> p g (j t)", j=JG)).then_inc(stored[lot % 2], 16)
                    for b in range(2):
                        sp.wait_ge(stored[b], 16 * (LOTS // 2))


def expert_layer(core, k, x, g_dram, acc):
    nc, d, ps = core.nc, core.dram, k.ps
    VB = 6
    n_out = 2 * NXC
    with ExitStack() as ctx:
        sb = lambda n, s, dt=F32: ctx.enter_context(core.sbuf(n, s, dt))
        u, v = sb("ex_u", [P, 2, KD * P]), sb("ex_v", [P, 2, D])
        uh, ul = sb("ex_uh", [P, JG, KD * P], F32R), sb("ex_ul", [P, JG, KD * P], F32R)
        vh, vl = sb("ex_vh", [P, JG, D], F32R), sb("ex_vl", [P, JG, D], F32R)
        g = sb("ex_g", [P, N_TG, JG, TG])
        ab, af = sb("ex_ab", [P, 2, NX]), sb("ex_af", [P, 2, NX])
        ah, al = sb("ex_ah", [P, JG, NX], F32R), sb("ex_al", [P, JG, NX], F32R)
        with core.stage("u_in*2", "v_in*2", "g_in", "uh_ready", "ul_ready", "vh_ready", "vl_ready", "h_done", "h_read",
                        "af_ready", "ah_ready", "al_ready", "v_done", "v_read", "clear") as (
                block, u_in, v_in, g_in, uh_ready, ul_ready, vh_ready, vl_ready, h_done, h_read,
                af_ready, ah_ready, al_ready, v_done, v_read, clear):
            def passes(engine, group):
                group(0, True, False)
                with engine.Fori(1, N_JG - 1) as jg:
                    group(jg, False, False)
                group(N_JG - 1, False, True)

            @block.sync
            def _(sp):
                def load_u(jg, j, later=0):
                    sp.dma_start(u[:, j % 2], d["peer_u"][later:][jg, j]).then_inc(u_in[j % 2], 16)

                def load_g(jg):
                    sp.dma_start(g[:].rearrange("p t j e -> p (t j e)"),
                                 g_dram[jg].rearrange("p t e -> p (t e)")).then_inc(g_in, 16)

                def group(jg, first, last):
                    for j in range(JG):
                        if j + 2 < JG or not last:
                            sp.wait_ge(ul_ready, jg * JG + (j + 1))
                            if j + 2 < JG:
                                load_u(jg, j + 2)
                            else:
                                load_u(jg, j + 2 - JG, 1)
                        if not (first and j < 2):
                            sp.wait_ge(vl_ready, jg * JG + (j - 1))
                        if j == 0 and not first:
                            sp.wait_ge(af_ready, jg * JG)
                            load_g(jg)
                        sp.dma_start(v[:, j % 2], d["peer_v"][jg, j]).then_inc(v_in[j % 2], 16)
                load_u(0, 0)
                load_u(0, 1)
                load_g(0)
                passes(sp, group)

            @block.tensor
            def _(pe):
                def group(jg, first, last):
                    for j in range(JG):
                        pe.wait_ge(ul_ready, jg * JG + (j + 1))
                        if not (first and j < 2):
                            pe.wait_ge(h_read, jg * JG + (j - 1))
                        for kk in range(KD):
                            c = slice(P * kk, P * kk + P)
                            mm = product3(pe, ps[:, j % 2, :], (uh[:, j, c], ul[:, j, c]),
                                          (x[0][:, kk, :], x[1][:, kk, :]), kk == 0, kk == KD - 1)
                        mm.then_inc(h_done, 1)
                    def second(n, j):
                        t, h = slice(P * (n // 2), P * (n // 2) + P), slice(512 * (n % 2), 512 * (n % 2) + 512)
                        return product3(pe, ps[:, 2 + n % VB, :], (ah[:, j, t], al[:, j, t]), (vh[:, j, h], vl[:, j, h]),
                                        j == 0, j == JG - 1)

                    ahead = 3
                    for n in range(n_out):
                        if not (first and n < VB):
                            pe.wait_ge(v_read, jg * n_out + (n - VB + 1))
                        for j in range(JG - 1 if n < ahead else JG):
                            if n == 0:
                                pe.wait_ge(vl_ready, jg * JG + (j + 1))
                                pe.wait_ge(al_ready, jg * JG + (j + 1))
                            mm = second(n, j)
                        if n >= ahead:
                            mm.then_inc(v_done, 1)
                        if n == ahead - 1:
                            pe.wait_ge(vl_ready, jg * JG + JG)
                            pe.wait_ge(al_ready, jg * JG + JG)
                            for m in range(ahead):
                                second(m, JG - 1).then_inc(v_done, 1)
                passes(pe, group)

            @block.scalar
            def _(act):
                def high_u(jg, j, fresh):
                    act.wait_ge(u_in[j % 2], jg * (8 * JG) + 16 * (j // 2 + 1))
                    if not fresh:
                        act.wait_ge(h_done, jg * JG + (j + 1 - JG))
                    act.copy(uh[:, j], u[:, j % 2]).then_inc(uh_ready, 1)

                def group(jg, first, last):
                    for j in range(JG):
                        if j + 2 < JG:
                            high_u(jg, j + 2, first)
                        elif not last:
                            high_u(jg + 1, j + 2 - JG, False)
                        act.wait_ge(h_done, jg * JG + (j + 1))
                        if not (first and j < 2):
                            act.wait_ge(af_ready, jg * JG + (j - 1))
                        act.activation(ab[:, j % 2, :], ps[:, j % 2, :], ACT.Gelu).then_inc(h_read, 1)
                        act.wait_ge(v_in[j % 2], jg * (8 * JG) + 16 * (j // 2 + 1))
                        if not first:
                            act.wait_ge(v_done, jg * n_out)
                        act.copy(vh[:, j], v[:, j % 2]).then_inc(vh_ready, 1)
                        act.wait_ge(af_ready, jg * JG + (j + 1))
                        act.copy(ah[:, j], af[:, j % 2]).then_inc(ah_ready, 1)
                high_u(0, 0, True)
                high_u(0, 1, True)
                passes(act, group)

            @block.gpsimd
            def _(pool):
                def group(jg, first, last):
                    for j in range(JG):
                        pool.wait_ge(vh_ready, jg * JG + (j + 1))
                        pool.tensor_tensor(vl[:, j], v[:, j % 2], vh[:, j].bitcast(F32), ALU.subtract).then_inc(vl_ready, 1)
                passes(pool, group)

            @block.vector
            def _(dve):
                dve.memset(acc[:], 0.0).then_inc(clear, 1)
                dve.wait_ge(clear, 1)

                def low_u(jg, j):
                    dve.wait_ge(uh_ready, jg * JG + (j + 1))
                    dve.tensor_tensor(ul[:, j], u[:, j % 2], uh[:, j].bitcast(F32), ALU.subtract).then_inc(ul_ready, 1)

                def group(jg, first, last):
                    dve.wait_ge(g_in, jg * 16 + 16)
                    for j in range(JG):
                        if j + 2 < JG:
                            low_u(jg, j + 2)
                        elif not last:
                            low_u(jg + 1, j + 2 - JG)
                        dve.wait_ge(h_read, jg * JG + (j + 1))
                        dve.tensor_tensor(af[:, j % 2, :].rearrange("p (t e) -> p t e", e=TG),
                                          ab[:, j % 2, :].rearrange("p (t e) -> p t e", e=TG), g[:, :, j, :],
                                          ALU.mult).then_inc(af_ready, 1)
                        dve.wait_ge(ah_ready, jg * JG + (j + 1))
                        dve.tensor_tensor(al[:, j], af[:, j % 2], ah[:, j].bitcast(F32), ALU.subtract).then_inc(al_ready, 1)
                    for n in range(n_out):
                        dve.wait_ge(v_done, jg * n_out + (n + 1))
                        if not first:
                            dve.wait_ge(v_read, jg * n_out + (n + 1 - n_out))
                        dve.tensor_tensor(acc[:, n // 2, n % 2, :], acc[:, n // 2, n % 2, :], ps[:, 2 + n % VB, :],
                                          ALU.add).then_inc(v_read, 1)
                low_u(0, 0)
                low_u(0, 1)
                passes(dve, group)


def experts(core, k, xs, cols, rows, tap):
    nc, d = core.nc, core.dram
    g_dram = nc.dram_tensor("gates_by_expert", (N_JG, P, N_TG, JG * TG), F32, kind="Internal").ap()
    with ExitStack() as outer:
        xh, xl = (outer.enter_context(core.sbuf(n, [P, KD, NX], F32R)) for n in ("ex_xh", "ex_xl"))
        with ExitStack() as ctx:
            sb = lambda n, s: ctx.enter_context(core.sbuf(n, s))
            uT = sb("ex_xT", [P, KD, NX])
            norm_transpose(core, k.ps, k.ident, k.eps, [(xs[:, t, :], P * t, 0) for t in range(NXC)], True,
                           cols[:, 3 * KD:4 * KD, :], cols[:, 2 * KD:3 * KD, :], uT)
            tap("hT3", uT[:])
            split(core, uT, xh, xl)
            iota = sb("iota", [P, P])
            chosen, chosenT = sb("chosen", [P, NXC, 3, P]), sb("chosenT", [P, 3, NX])
            load_all(core, [(iota[:], d["iota"].partition_broadcast(P))])
            with nc.Fori(0, PEER_HEADS) as head:
                route_head(core, k, (xh, xl), head, iota[:, 0:TOPK], chosen)
            transposes(core, k, [([chosen[:, t, a, :] for t in range(NXC)], chosenT[:, a, :].rearrange("p (t e) -> p t e", t=NXC))
                                 for a in range(3)])
            spread_gates(core, k, chosenT, iota[:], g_dram)
        acc = outer.enter_context(core.sbuf("ex_acc", [P, NXC, 2, 512]))
        expert_layer(core, k, (xh, xl), g_dram, acc)
        tap("ffn", acc[:])
        with core.stage("steps") as (block, steps):
            @block.vector
            def _(dve):
                link = chain(dve, steps)
                for t in range(NXC):
                    link(dve.tensor_tensor(acc[:, t], acc[:, t], rows[:, 2:4, :], ALU.mult))
                    x = xs[:, t, :].rearrange("p (h c) -> p h c", h=2)
                    link(dve.scalar_tensor_tensor(out=x, in0=x, scalar=ALPHA, in1=acc[:, t], op0=ALU.mult, op1=ALU.add))


def head_block(core, k, hT, head, lower, norm_w, out):
    nc, d = core.nc, core.dram
    with ExitStack() as ctx:
        sb = lambda n, s: ctx.enter_context(core.sbuf(n, s))
        f = sb("hg_f", [P, 2, T])
        kT = sb("hg_k", [P, 2, T])
        v = sb("hg_v", [P, T])
        vt = sb("hg_vt", [P, NC, P])
        q, gate = sb("hg_q", [P, NX]), sb("hg_gate", [P, NX])
        scr = sb("hg_scr", [P, 2, NX])
        lb = sb("hg_lb", [P, 2, 2])
        project(core, k.ps, hT, d["w_in_hg"][head], [
            (0, ALL, f[:, 0, :]), (1, ALL, f[:, 1, :]), (3, X_ONLY, q[:]), (4, X_ONLY, gate[:]), (2, ALL, v[:])],
            gates={0: None, 1: None, 2: scr[:, 0, :], 3: scr[:, 1, :]})
        with core.stage("dsteps", "f_ready", "done") as (block, dsteps, f_ready, done):
            @block.vector
            def _(dve):
                link = chain(dve, dsteps)
                link(dve.tensor_copy(lb[:, 0, :], lower[:, :, head]))
                link(dve.tensor_scalar(lb[:, 1, :], lb[:, 0, :], -1.0, 1.0, ALU.mult, ALU.add))
                for n in range(2):
                    link(dve.tensor_scalar(f[:, n, :], f[:, n, :], lb[:, 1, n:n + 1], lb[:, 0, n:n + 1], ALU.mult, ALU.add))
                    link(dve.tensor_scalar(kT[:, n, :], f[:, n, :], -1.0, 1.0, ALU.mult, ALU.add))
                    dve.tensor_scalar(f[:, n, :], f[:, n, :], 1e-19, None, ALU.max).then_inc(f_ready, 1)

            @block.scalar
            def _(act):
                for n in range(2):
                    act.wait_ge(f_ready, n + 1)
                    act.activation(f[:, n, :], f[:, n, :], ACT.Ln).then_inc(done, 1)
        transposes(core, k, [([v[:, P * c:P * c + P] for c in cs], vt[:, cs[0]:cs[-1] + 1, :])
                             for cs in (range(0, 4), range(4, 6))])
        key_gated_head(core, k, q[:], (kT[:, 0, :], kT[:, 1, :]), (f[:, 0, :], f[:, 1, :]), vt, gate[:], norm_w, out)


def ssd_group(core, k, hT, g, dt, loga, out):
    nc, d, ps = core.nc, core.dram, k.ps
    with ExitStack() as ctx:
        sb = lambda n, s: ctx.enter_context(core.sbuf(n, s))
        raw = sb("ma_raw", [P, 4, T])
        cv = sb("ma_cv", [P, 4, T])
        z = sb("ma_z", [P, 2, NX])
        y = sb("ma_y", [P, 2, NX])
        zs = y
        cw, cb = sb("ma_cw", [P, 4, MA_TAPS]), sb("ma_cb", [P, 4])
        par = sb("ma_par", [P, 2, 2])
        col = sb("ma_col", [P, 2, NC, 2, MA_HPG])
        xtok = sb("ma_xtok", [P, NC, 2 * P])
        btok = sb("ma_btok", [P, NC, P])
        def conv(dve, evicted, loaded, steps):
            link = chain(dve, steps)
            link(dve.tensor_copy(col[:, 0], dt[:, :, :, bass.ds(g * MA_HPG, MA_HPG)]))
            link(dve.tensor_copy(col[:, 1], loga[:, :, :, bass.ds(g * MA_HPG, MA_HPG)]))
            dve.wait_ge(loaded, 48)
            mid = MA_TAPS // 2
            for j in range(4):
                dve.wait_ge(evicted, j + 1)
                for lo, n, step in (((0, NCTX, 1),) if j < 3 else ()) + ((NCTX, NX, GRID_W),):
                    src, dst = raw[:, j, lo:lo + n], cv[:, j, lo:lo + n]
                    link(dve.tensor_scalar(dst, src, cw[:, j, mid:mid + 1], cb[:, j:j + 1], ALU.mult, ALU.add))
                    for s in (-2, -1, 1, 2):
                        o0, o1 = max(0, -s * step), n - max(0, s * step)
                        link(dve.scalar_tensor_tensor(out=dst[:, o0:o1], in0=src[:, o0 + s * step:o1 + s * step],
                                                      scalar=cw[:, j, mid + s:mid + s + 1], in1=dst[:, o0:o1],
                                                      op0=ALU.mult, op1=ALU.add))
        project(core, ps, hT, d["w_in_ma"][g], [
            (0, ALL, raw[:, 0, :]), (1, ALL, raw[:, 1, :]), (2, ALL, raw[:, 2, :]), (3, X_ONLY, raw[:, 3, NCTX:T]),
            (4, X_ONLY, z[:, 0, :]), (5, X_ONLY, z[:, 1, :])],
            [(cw[:], d["ma_conv_w"][g]), (cb[:], d["ma_conv_b"][g]), (par[:], d["ma_par"][g])], conv,
            {4: zs[:, 0, :], 5: zs[:, 1, :]})
        by_col = lambda a: a.rearrange("p (r w) -> p w r", w=GRID_W)
        cols = lambda a: a.rearrange("p (w r) -> p w r", r=GRID_H)
        gated(core, [(cv[:, j, 0:NCTX], None, raw[:, j, 0:NCTX], raw[:, j, 0:NCTX], True) for j in range(3)]
              + [(by_col(cv[:, j, NCTX:T]), None, cols(raw[:, j, NCTX:T]), cols(raw[:, j, NCTX:T]), True) for j in range(4)])
        transposes(core, k, [([raw[:, a, P * c:P * c + P] for c in cs], dst[:, cs[0]:cs[-1] + 1, s])
                             for a, dst, s in ((0, xtok, slice(0, P)), (1, xtok, slice(P, 2 * P)), (2, btok, slice(0, P)))
                             for cs in (range(0, 4), range(4, 6))])
        BT, CT = raw[:, 2, :], raw[:, 3, NCTX:T]
        lcs = sb("ma_lc", [P, 2, 2, NC, MA_HPG])
        exs = sb("ma_ex", [P, 2, 2, NC, MA_HPG])
        xdt, xw = (cv[:, 2 * a:2 * a + 2, :].rearrange("p a t -> p (a t)").rearrange("p (c e) -> p c e", c=NC) for a in range(2))
        cbm = sb("ma_cbm", [P, 2, NXC, P])
        L = sb("ma_L", [P, 2, MA_HPG, P])
        ce = sb("ma_ce", [P, 2, MA_HPG, P])
        H = sb("ma_H", [P, 2, NXC + 1, 2 * P])
        tmp = sb("ma_tmp", [P, 2 * P])
        rs = sb("ma_rs", [P, NX])
        heads = lambda a: a.rearrange("p c (h e) -> p c h e", e=MA_P)
        over = lambda a: a.unsqueeze(3).to_broadcast([P, NC, MA_HPG, MA_P])
        with core.stage("cb_done", "sums_done", "lc_ready", "ex_ready", "xw_ready", "u_done", "dsteps", "H_ready",
                        "rows_done", "l_ready", "dec_ready", "ce_ready", "m_ready", "y_done", "cb_read", "lexp_ready", "u_read", "ce_scaled") as (
                block, cb_done, sums_done, lc_ready, ex_ready, xw_ready, u_done, dsteps, H_ready,
                rows_done, l_ready, dec_ready, ce_ready, m_ready, y_done, cb_read, lexp_ready, u_read, ce_scaled):
            @block.tensor
            def _(pe):
                for c in range(NXC):
                    mm = pe.matmul(ps[:, 0, P * c:P * c + P], BT[:, NCTX + P * c:NCTX + P * c + P], CT[:, P * c:P * c + P],
                                   start=True, stop=True)
                mm.then_inc(cb_done, 1)
                for dr in range(2):
                    g_ = col[:, 1, :, dr, :]
                    o = ps[:, 1, 48 * dr:48 * dr + 48].rearrange("p (a c h) -> p a c h", a=2, c=NC)
                    pe.matmul(o[:, 0], k.incl[:, dr, :], g_, start=True, stop=True)
                    mm = pe.matmul(o[:, 1], k.ones[:], g_, start=True, stop=True)
                mm.then_inc(sums_done, 1)
                for dr in range(2):
                    pe.wait_ge(xw_ready, dr + 1)
                    for i, c in enumerate(ORDER[dr][:-1]):
                        n = 5 * dr + i
                        if n >= 2:
                            pe.wait_ge(u_read, n - 1)
                        pe.matmul(ps[:, 2 + n % 2, 0:2 * P], btok[:, c, :], xw[:, c, :], start=True, stop=True).then_inc(u_done, 1)
                    def rows_of(c):
                        n = NXC * dr + c
                        if n >= 2:
                            pe.wait_ge(ce_ready, n - 1)
                            pe.wait_ge(l_ready, n - 1)
                        for j in range(MA_HPG):
                            mm = pe.matmul(ps[:, 4 + n % 2, P * j:P * j + P],
                                           col[:, 1, C0 + c, dr, j:j + 1].to_broadcast([P, P]), k.incl[:, dr, :],
                                           start=True, stop=True)
                        mm.then_inc(rows_done, 1)

                    rows_of(0)
                    for c in range(NXC):
                        n = NXC * dr + c
                        if c + 1 < NXC:
                            rows_of(c + 1)
                        pe.wait_ge(m_ready, n + 1)
                        pe.wait_ge(ce_scaled, n + 1)
                        slot = ORDER[dr][C0:].index(C0 + c)
                        for j in range(MA_HPG):
                            o = ps[MA_P * (j % 2):MA_P * (j % 2) + MA_P, 6 + j // 2, P * c:P * c + P]
                            hs = slice(MA_P * j, MA_P * j + MA_P)
                            pe.matmul(o, xdt[:, C0 + c, hs], L[:, n % 2, j, :], start=True, stop=False)
                            mm = pe.matmul(o, H[:, dr, slot, hs], ce[:, n % 2, j, :], start=False, stop=True)
                        mm.then_inc(y_done, 1)

            @block.gpsimd
            def _(pool):
                for n in range(2 * NXC):
                    c = n % NXC
                    pool.wait_ge(ce_ready, n + 1)
                    pool.tensor_tensor(ce[:, n % 2], ce[:, n % 2],
                                       CT[:, P * c:P * c + P].unsqueeze(1).to_broadcast([P, MA_HPG, P]),
                                       ALU.mult).then_inc(ce_scaled, 1)

            @block.vector
            def _(dve):
                link = chain(dve, dsteps)
                dve.wait_ge(sums_done, 1)
                link(dve.tensor_copy(lcs[:], ps[:, 1, 0:96].rearrange("p (d a c h) -> p d a c h", d=2, a=2, c=NC)))
                dve.tensor_tensor(exs[:, :, 0], lcs[:, :, 1], lcs[:, :, 0], ALU.subtract).then_inc(lc_ready, 1)
                dve.wait_ge(cb_done, 1)
                for dr in range(2):
                    link(dve.tensor_tensor(cbm[:, dr], ps[:, 0, :].rearrange("p (c t) -> p c t", c=NXC),
                                           k.incl[:, dr, :].unsqueeze(1).to_broadcast([P, NXC, P]), ALU.mult))
                link(dve.memset(H[:, :, 0, :], 0.0))
                for dr in range(2):
                    lc, ex = lcs[:, dr], exs[:, dr]
                    if dr == 1:
                        dve.wait_ge(y_done, NXC)
                        link(dve.tensor_copy(y[:], ps[:, 6:8, :]))
                    link(dve.tensor_tensor(heads(xdt), heads(xtok[:]), over(col[:, 0, :, dr, :]), ALU.mult))
                    dve.wait_ge(ex_ready, 1)
                    dve.tensor_tensor(heads(xw), heads(xdt), over(ex[:, 0]), ALU.mult).then_inc(xw_ready, 1)
                    slot = 0
                    for i, c in enumerate(ORDER[dr][:-1]):
                        n = 5 * dr + i
                        nxt = slot if i < C0 else slot + 1
                        link(dve.tensor_tensor(tmp[:].rearrange("p (h e) -> p h e", e=MA_P),
                                               H[:, dr, slot, :].rearrange("p (h e) -> p h e", e=MA_P),
                                               ex[:, 1, c, :].unsqueeze(2).to_broadcast([P, MA_HPG, MA_P]), ALU.mult))
                        dve.wait_ge(u_done, n + 1)
                        dve.tensor_tensor(H[:, dr, nxt, :], tmp[:], ps[:, 2 + n % 2, 0:2 * P], ALU.add).then_inc(u_read, 1)
                        dve.wait_ge(u_read, n + 1)
                        slot = nxt
                    def exponents(c):
                        n = NXC * dr + c
                        dve.wait_ge(rows_done, n + 1)
                        if n >= 2:
                            dve.wait_ge(y_done, n - 1)
                        for j in range(MA_HPG):
                            ins = dve.tensor_scalar(L[:, n % 2, j, :], ps[:, 4 + n % 2, P * j:P * j + P],
                                                    lc[:, 0, C0 + c, j:j + 1], 0.0, ALU.subtract, ALU.min)
                        ins.then_inc(l_ready, 1)

                    exponents(0)
                    for c in range(NXC):
                        n = NXC * dr + c
                        if c + 1 < NXC:
                            exponents(c + 1)
                        dve.wait_ge(lexp_ready, n + 1)
                        dve.tensor_tensor(L[:, n % 2], L[:, n % 2],
                                          cbm[:, dr, c, :].unsqueeze(1).to_broadcast([P, MA_HPG, P]), ALU.mult).then_inc(m_ready, 1)

            @block.scalar
            def _(act):
                act.wait_ge(lc_ready, 1)
                act.activation(exs[:, :, 1], lcs[:, :, 1], ACT.Exp)
                act.activation(exs[:, :, 0], exs[:, :, 0], ACT.Exp).then_inc(ex_ready, 1)
                for dr in range(2):
                    for c in range(NXC):
                        n = NXC * dr + c
                        act.wait_ge(l_ready, n + 1)
                        if n >= 2:
                            act.wait_ge(y_done, n - 1)
                        act.activation(ce[:, n % 2], ps[:, 4 + n % 2, :].rearrange("p (h t) -> p h t", h=MA_HPG),
                                       ACT.Exp).then_inc(ce_ready, 1)
                        act.activation(L[:, n % 2], L[:, n % 2], ACT.Exp).then_inc(lexp_ready, 1)
        with core.stage("dsteps", "y_ready", "sq_ready", "ss_done", "rstd_ready", "asteps") as (
                block, dsteps, y_ready, sq_ready, ss_done, rstd_ready, asteps):
            @block.vector
            def _(dve):
                link = chain(dve, dsteps)
                link(dve.tensor_tensor(y[:], y[:], ps[:, 6:8, :], ALU.add))
                for e in range(2):
                    link(dve.scalar_tensor_tensor(out=y[:, e, :], in0=raw[:, e, NCTX:T], scalar=par[:, e, 0:1], in1=y[:, e, :],
                                                  op0=ALU.mult, op1=ALU.add))
                    rm = lambda a: a.rearrange("p (r w) -> p r w", w=GRID_W)
                    ins = dve.tensor_tensor(rm(z[:, e, :]), y[:, e, :].rearrange("p (w r) -> p r w", r=GRID_H), rm(z[:, e, :]),
                                            ALU.mult)
                ins.then_inc(y_ready, 1)
                dve.wait_ge(rstd_ready, 1)
                for e in range(2):
                    dve.scalar_tensor_tensor(out=out[:, e, :], in0=z[:, e, :], scalar=par[:, e, 1:2], in1=rs[:],
                                             op0=ALU.mult, op1=ALU.mult)

            @block.scalar
            def _(act):
                alink = chain(act, asteps)
                act.wait_ge(y_ready, 1)
                act.activation(cv[:, 0:2, 0:NX], z[:], ACT.Square).then_inc(sq_ready, 1)
                act.wait_ge(ss_done, 1)
                alink(act.activation(rs[:], ps[:, 0, :], ACT.Ln, bias=k.eps[:, 0:1], scale=1.0 / (2 * P)))
                act.activation(rs[:], rs[:], ACT.Exp, scale=-0.5).then_inc(rstd_ready, 1)

            @block.tensor
            def _(pe):
                pe.wait_ge(sq_ready, 1)
                for e in range(2):
                    mm = pe.matmul(ps[:, 0, :], k.ones[:], cv[:, e, 0:NX], start=(e == 0), stop=(e == 1))
                mm.then_inc(ss_done, 1)


def mixer_block(core, k, hT, xs, cols, rows, tap):
    nc, d = core.nc, core.dram
    with ExitStack() as ctx:
        sbt = lambda n, s, dt=F32: ctx.enter_context(core.sbuf(n, s, dt))
        xt = [xs[:, t, :] for t in range(NXC)]
        with ExitStack() as ctx2:
            sb2 = lambda n, s: ctx2.enter_context(core.sbuf(n, s))
            cond = sb2("cond2", [P, KD, 2])
            b_cols, b_rows = sb2("b_cols2", [P, 4 * KD]), sb2("b_rows2", [P, 4, 512])
            ctx_rows = sb2("ctx_rows2", [P, C0, D])
            load_all(core, [(cond[:], d["cond_2"]), (b_cols[:], d["b_ada_cols"]), (b_rows[:], d["b_ada_rows"].partition_broadcast(P))]
                     + [(ctx_rows[:, t, :], d["ctx_2"][P * t:P * t + P, :]) for t in range(C0)])
            modulation(core, sbt, k.ps, cond, d["w_ada_cols"], 4 * KD, cols, b_cols, d["w_ada_rows"], 4, rows, b_rows)
            with core.stage("steps") as (block, steps):
                @block.vector
                def _(dve):
                    for a in (1, 3):
                        s = cols[:, KD * a:KD * a + KD, :]
                        dve.tensor_scalar(s, s, 1.0, None, ALU.add).then_inc(steps, 1)
            whole = sb2("h_whole2", [P, KD, T])
            norm_transpose(core, k.ps, k.ident, k.eps,
                           [(ctx_rows[:, t, :], P * t, 1) for t in range(C0)]
                           + [(xs[:, t, :], NCTX + P * t, 0) for t in range(NXC)], True,
                           cols[:, KD:2 * KD, :], cols[:, 0:KD, :], whole)
            tap("hT2", whole[:])
            split(core, whole, *hT)
        with ExitStack() as ctx2:
            sb2 = lambda n, s: ctx2.enter_context(core.sbuf(n, s))
            oT = sb2("oT", [P, HG_HEADS, NX])
            yzT = sb2("yzT", [P, 2 * MA_GROUPS, NX])
            with ExitStack() as ctx3:
                sb3 = lambda n, s: ctx3.enter_context(core.sbuf(n, s))
                lower = sb3("lower", [P, 2, HG_HEADS])
                lg = sb3("lower_logits", [P, 2, 2, HG_HEADS])
                top = sb3("lower_top", [P, 2, HG_HEADS])
                norm_w = sb3("hg_norm_w", [P, 1])
                load_all(core, [(lg[:], d["hg_lb"]), (norm_w[:], d["hg_norm_w"])])
                with core.stage("dsteps", "diff_ready", "exp_ready") as (block, dsteps, diff_ready, exp_ready):
                    @block.vector
                    def _(dve):
                        link = chain(dve, dsteps)
                        link(dve.tensor_tensor(top[:], lg[:, :, 0, :], lg[:, :, 1, :], ALU.max))
                        dve.tensor_tensor(lg[:], lg[:], top[:].unsqueeze(2).to_broadcast([P, 2, 2, HG_HEADS]),
                                          ALU.subtract).then_inc(diff_ready, 1)
                        dve.wait_ge(exp_ready, 1)
                        link(dve.tensor_tensor(top[:], lg[:, :, 0, :], lg[:, :, 1, :], ALU.add))
                        link(dve.reciprocal(top[:], top[:]))
                        link(dve.tensor_tensor(lower[:], lg[:, :, 0, :], top[:], ALU.mult))

                    @block.scalar
                    def _(act):
                        act.wait_ge(diff_ready, 1)
                        act.activation(lg[:], lg[:], ACT.Exp).then_inc(exp_ready, 1)
                with gated_constants(core, k), nc.Fori(0, HG_HEADS) as head:
                    head_block(core, k, hT, head, lower, norm_w[:, 0:1], oT[:, head, :])
            tap("oT", oT[:])
            with ExitStack() as ctx3:
                sb3 = lambda n, s: ctx3.enter_context(core.sbuf(n, s))
                dt, loga = sb3("ma_dt", [P, NC, 2, 32]), sb3("ma_loga", [P, NC, 2, 32])
                par = sb3("ma_rows", [P, 2, 2 * 32])
                with ExitStack() as ctx4:
                    sb4 = lambda n, s: ctx4.enter_context(core.sbuf(n, s))
                    dT, dT2 = sb4("dT", [64, T]), sb4("dT2", [64, T])
                    tmp = sb4("dt_tmp", [P, NC, 64])
                    load_all(core, [(par[:, 0, :], d["ma_dt_bias"].partition_broadcast(P)),
                                    (par[:, 1, :], d["ma_a_log"].partition_broadcast(P))])
                    project(core, k.ps, hT, d["w_in_dt"], [(0, ALL, dT[:])])
                    with core.stage("turned", "exp_ready") as (block, turned, exp_ready):
                        @block.vector
                        def _(dve):
                            dve.tensor_copy(dT2[:, 0:NCTX], dT[:, 0:NCTX]).then_inc(turned, 1)
                            dve.tensor_copy(dT2[:, NCTX:T].rearrange("p (w r) -> p w r", r=GRID_H),
                                            dT[:, NCTX:T].rearrange("p (r w) -> p w r", w=GRID_W)).then_inc(turned, 1)
                            dve.wait_ge(exp_ready, 1)
                            dve.tensor_scalar(par[:, 1, :], par[:, 1, :], -1.0, None, ALU.mult)

                        @block.scalar
                        def _(act):
                            act.activation(par[:, 1, :], par[:, 1, :], ACT.Exp).then_inc(exp_ready, 1)
                    flat = lambda a: a[:].rearrange("p c a h -> p c (a h)")
                    transposes(core, k, [([dT2[:, P * c:P * c + P] for c in cs], flat(dt)[:, cs[0]:cs[-1] + 1, :])
                                         for cs in (range(0, 4), range(4, 6))])
                    wide = lambda a: a.unsqueeze(1).to_broadcast([P, NC, 64])
                    log_sigmoids(core, k, [(flat(dt), wide(par[:, 0, :]), flat(dt), tmp[:], True,
                                            (flat(loga), wide(par[:, 1, :])))])
                with nc.Fori(0, MA_GROUPS) as g:
                    ssd_group(core, k, hT, g, dt, loga, yzT[:, bass.ds(2 * g, 2), :])
            tap("yzT", yzT[:])
            mT = sb2("mT2", [P, KD, NX])
            merge(core, k, hT, d["w_merge_2"], 8, 16, oT, yzT, None, mT)
            output_product(core, k, mT, d["w_out_2"], rows[:, 0:2, :], ALPHA, xt)
        with ExitStack() as ctx2:
            gb = ctx2.enter_context(core.sbuf("ln_gb", [P, 2, D]))
            load_all(core, [(gb[:, 0, :], d["ln1_g"].partition_broadcast(P)), (gb[:, 1, :], d["ln1_b"].partition_broadcast(P))])
            norm_rows(core, k, xt, True, gb[:, 0, :], gb[:, 1, :])
        tap("xln1", xs[:])


def expert_block(core, k, xs, cols, rows, tap):
    d = core.dram
    experts(core, k, xs, cols, rows, tap)
    with core.sbuf("ln2_gb", [P, 2, D]) as gb:
        load_all(core, [(gb[:, 0, :], d["ln2_g"].partition_broadcast(P)), (gb[:, 1, :], d["ln2_b"].partition_broadcast(P))])
        norm_rows(core, k, [xs[:, t, :] for t in range(NXC)], True, gb[:, 0, :], gb[:, 1, :])


def second_laid_out(a, d, col, rows_of, tiles, quads, wide_rows):
    import numpy as np
    d["cond_2"], d["ctx_2"] = np.stack([col(a["c_2"]), col(a["c_ctx_2"])], -1), a["ctx_2"]
    c_starts = [s + P * j for s in (0, D, 3 * D, 4 * D) for j in range(KD)]
    r_starts = [2 * D, 2 * D + 512, 5 * D, 5 * D + 512]
    d["w_ada_cols"], d["w_ada_rows"] = quads(a["w_ada_2"], c_starts), wide_rows(a["w_ada_2"], r_starts)
    d["b_ada_cols"] = np.stack([a["b_ada_2"][s:s + P] for s in c_starts], 1)
    d["b_ada_rows"] = np.stack([a["b_ada_2"][s:s + 512] for s in r_starts])
    d["hg_lb"] = a["hg_lb_logits_2"].reshape(2, 2, HG_HEADS, P).transpose(3, 0, 1, 2)
    d["hg_norm_w"] = col(a["hg_norm_w_2"])
    at = dict(zip(("f_f", "f_b", "iv", "xh", "b", "dt", "q", "og", "cm", "z", "ga", "gb"),
                  np.cumsum([0, D, D, D, 2 * D, D, 64, D, D, D, 2 * D, D]).tolist()))
    w = a["w_in_2"]
    d["w_in_hg"] = np.stack([tiles(w, [at[n] + P * h for n in ("f_f", "f_b", "iv", "q", "og")]) for h in range(HG_HEADS)])
    d["w_in_ma"] = np.stack([tiles(w, (at["xh"] + 2 * P * g, at["xh"] + 2 * P * g + P, at["b"] + P * g, at["cm"] + P * g,
                                       at["z"] + 2 * P * g, at["z"] + 2 * P * g + P)) for g in range(MA_GROUPS)])
    dtw = rows_of(w)[:, :, at["dt"]:at["dt"] + 64]
    d["w_in_dt"] = np.pad(dtw, ((0, 0), (0, 0), (0, 64))).transpose(1, 0, 2)[None]
    d["ma_dt_bias"], d["ma_a_log"] = a["ma_dt_bias_2"].reshape(-1), a["ma_a_log_2"].reshape(-1)
    chans = lambda g: [2 * P * g, 2 * P * g + P, 2 * D + P * g, 3 * D + P * g]
    d["ma_conv_w"] = np.stack([np.stack([a["ma_conv_w_2"][s:s + P] for s in chans(g)], 1) for g in range(MA_GROUPS)])
    d["ma_conv_b"] = np.stack([np.stack([a["ma_conv_b_2"][s:s + P] for s in chans(g)], 1) for g in range(MA_GROUPS)])
    md = np.repeat(a["ma_d_2"], MA_P)
    d["ma_par"] = np.stack([md.reshape(MA_GROUPS, 2, P), a["ma_norm_w_2"].reshape(MA_GROUPS, 2, P)], -1).transpose(0, 2, 1, 3)
    d["w_merge_2"] = np.concatenate([tiles(a["w_branch_a_2"], range(0, D, P)), tiles(a["w_branch_b_2"], range(0, D, P)),
                                     tiles(w, range(at["ga"], at["ga"] + D, P)), tiles(w, range(at["gb"], at["gb"] + D, P))], 2)
    d["w_out_2"], d["ln1_g"], d["ln1_b"], d["ln2_g"], d["ln2_b"] = (
        a["w_out_2"], a["ln1_g_2"], a["ln1_b_2"], a["ln2_g_2"], a["ln2_b_2"])
    d["w_q"] = np.stack([tiles(a["peer_wq_2"], (2 * P * h, 2 * P * h + P)) for h in range(PEER_HEADS)])
    d["subkeys"] = a["peer_subkeys_2"].transpose(0, 3, 1, 2)
    d["iota"] = np.arange(P, dtype=np.float32)
    d["peer_u"] = a["peer_u_2"].reshape(P, N_JG, JG, KD, P).transpose(1, 2, 4, 3, 0)
    d["peer_v"] = a["peer_v_2"].reshape(P, N_JG, JG, D).transpose(1, 2, 0, 3)


def laid_out(i):
    import numpy as np
    a = {n: np.asarray(v) for n, v in i.items()}
    for n in list(a):
        if n in ("w_mod", "b_mod", "norm_g", "w_in", "gla_up", "gla_ub", "gla_onorm", "gdn_conv", "gdn_a_log", "gdn_dt_bias",
                 "gdn_onorm", "w_gla_out", "w_gdn_out", "b_gate", "w_o", "w_ada_2", "b_ada_2", "w_in_2", "hg_norm_w_2",
                 "ma_conv_w_2", "ma_conv_b_2", "ma_dt_bias_2", "ma_a_log_2", "ma_d_2", "ma_norm_w_2", "w_branch_a_2",
                 "w_branch_b_2", "w_out_2", "ln1_g_2", "ln1_b_2", "peer_wq_2", "peer_subkeys_2", "peer_u_2", "peer_v_2",
                 "ln2_g_2", "ln2_b_2", "x", "ctx", "ctx_2", "c", "c_2"):
            a[n] = a[n][0]
    tri = np.tril(np.ones((P, P), np.float32))
    t = np.arange(P)
    level = np.zeros((2, LEVELS + 1, P, P), np.float32)
    level[:, 0] = np.eye(P)
    for i_ in range(1, LEVELS + 1):
        size = 1 << (i_ - 1)
        same = (t[:, None] // (2 * size)) == (t[None, :] // (2 * size))
        first, second = (t // size) % 2 == 0, (t // size) % 2 == 1
        level[0, i_] = same & first[:, None] & second[None, :]
        level[1, i_] = same & second[:, None] & first[None, :]
    restart = np.ones((2, T), np.float32)
    restart[0, 0::P] = 0
    restart[1, P - 1::P] = 0
    d = {
        "ident": np.eye(P, dtype=np.float32), "ones": np.ones((P, P), np.float32),
        "incl": np.stack([tri.T, tri], 1),
        "levelf": level.transpose(2, 0, 1, 3), "level": level.transpose(2, 0, 1, 3).astype(np.uint32),
        "restart": np.broadcast_to(restart, (P, 2, T)),
    }
    col = lambda v: v.reshape(-1, P).T
    rows_of = lambda w: w.reshape(-1, P, w.shape[-1])

    def tiles(w, starts):
        r = rows_of(w)
        return np.stack([r[:, :, s:s + P].transpose(1, 0, 2) for s in starts])

    def quads(w, starts):
        return tiles(w, starts).reshape(len(starts) // 4, 4, P, KD, P).transpose(0, 2, 1, 3, 4).reshape(len(starts) // 4, P, -1)

    def wide_rows(w, starts):
        r = rows_of(w)
        return np.stack([r[:, :, s:s + 512].transpose(1, 0, 2).reshape(P, -1) for s in starts])

    d["x"], d["ctx"], d["cond"] = a["x"], a["ctx"], np.stack([col(a["c"]), col(a["c_ctx"])], -1)
    d["w_mod_cols"] = quads(a["w_mod"], range(0, 2 * D, P))
    d["w_mod_rows"] = wide_rows(a["w_mod"], (2 * D, 2 * D + 512))
    d["b_mod_cols"], d["b_mod_rows"] = col(a["b_mod"][:2 * D]), a["b_mod"][2 * D:].reshape(2, 512)
    d["norm_g"], d["gla_onorm"], d["gdn_onorm"], d["b_gate"] = (
        col(a["norm_g"]), col(a["gla_onorm"]), col(a["gdn_onorm"]), col(a["b_gate"]))
    d["gdn_a_log"], d["gdn_dt_bias"], d["final_g"] = a["gdn_a_log"].reshape(-1), a["gdn_dt_bias"].reshape(-1), a["final_g"]
    at = dict(zip(("aq", "ak", "av", "ag", "alr", "bq", "bk", "bv", "bg", "bbeta", "bdec", "mg"),
                  np.cumsum([0, 256, 256, 512, 512, 32, 512, 512, 512, 512, 8, 8]).tolist()))
    w = a["w_in"]
    d["w_in_gla"] = np.stack([tiles(w, (at["aq"] + P * p, at["ak"] + P * p, at["av"] + 2 * P * p, at["av"] + 2 * P * p + P,
                                        at["ag"] + 2 * P * p, at["ag"] + 2 * P * p + P)) for p in range(2)])
    d["w_in_gdn"] = np.stack([tiles(w, (at["bq"] + P * h, at["bk"] + P * h, at["bv"] + P * h, at["bg"] + P * h))
                              for h in range(GDN_HEADS)])
    r = rows_of(w)
    small = np.concatenate([r[:, :, at["alr"]:at["alr"] + 32], r[:, :, at["bbeta"]:at["bbeta"] + 16]], -1)
    d["w_in_small"] = np.pad(small, ((0, 0), (0, 0), (0, P - 48))).transpose(1, 0, 2)[None]
    d["gla_up"] = a["gla_up"].reshape(2, GLA_RANK, 2, P).transpose(2, 0, 1, 3)
    d["gla_ub"] = a["gla_ub"].reshape(2, 2, P).transpose(1, 2, 0)
    d["gdn_conv"] = a["gdn_conv"].reshape(9, 3, GDN_HEADS, P).transpose(2, 3, 1, 0)
    ta, tb = tiles(a["w_gla_out"], range(0, D, P)), tiles(a["w_gdn_out"], range(0, D, P))
    d["w_merge"] = np.concatenate([ta, tb, tiles(w, range(at["mg"], at["mg"] + D, P)),
                                   tiles(w, range(at["mg"] + D, at["mg"] + 2 * D, P))], 2)
    d["w_o"] = a["w_o"]
    second_laid_out(a, d, col, rows_of, tiles, quads, wide_rows)
    return {n: np.ascontiguousarray(v) for n, v in d.items()}


def kernel(**inputs):
    import numpy as _np
    import concourse.bacc as _bacc
    from concourse import mybir as _mybir
    from concourse.bass_utils import run_bass_kernel_spmd as _run

    arrays = laid_out(inputs)
    nc = _bacc.Bacc("TRN2", target_bir_lowering=False, num_devices=1)
    dram = {n: nc.dram_tensor(f"in_{n}", v.shape, _mybir.dt.from_np(v.dtype), kind="ExternalInput").ap()
            for n, v in arrays.items()}
    out = nc.dram_tensor("out", (NX, D), F32, kind="ExternalOutput").ap()
    program(nc, dram, out)
    r = _run(nc, [{f"in_{n}": v for n, v in arrays.items()}], core_ids=[0])
    return _np.asarray(r.results[0]["out"]).reshape(1, NX, D)
```
